# Optimizing a Trainium2 kernel written in Bass

```python
import jax, jax.numpy as jnp
from jax import lax
import numpy as np

D_MODEL = 1024
BATCH = 1
SEQ = 2048
DEPTH = 1

ATTN_HEADS = 16
ATTN_KV_HEADS = 4
ATTN_HEAD_DIM = 64
ATTN_WIDTH = ATTN_HEADS * ATTN_HEAD_DIM
KV_WIDTH = ATTN_KV_HEADS * ATTN_HEAD_DIM
WINDOW = 128
ATTN_BLOCK = 128
ROPE_THETA = 10000.0
REC_HEADS = 8
REC_KEY_DIM = 128
REC_VAL_DIM = 128
REC_KEY_WIDTH = REC_HEADS * REC_KEY_DIM
REC_WIDTH = REC_HEADS * REC_VAL_DIM
REC_CHUNK = 64
EPS = 1e-6
D_MIX = ATTN_WIDTH + REC_WIDTH

IN_SPLITS = (ATTN_WIDTH, KV_WIDTH, KV_WIDTH, ATTN_WIDTH,
             REC_KEY_WIDTH, REC_KEY_WIDTH, REC_WIDTH, REC_WIDTH)
IN_WIDTH = sum(IN_SPLITS)

kernel_name = "hymba_swa_sink_hgrn2_adaln"

def rms_norm(x, w):
    xf = x.astype(jnp.float32)
    y = xf * lax.rsqrt(jnp.mean(xf * xf, axis=-1, keepdims=True) + EPS)
    return (y * w.astype(jnp.float32)).astype(x.dtype)

def rope(x, positions):
    hd = x.shape[-1]
    inv_freq = ROPE_THETA ** (-jnp.arange(0, hd, 2, dtype=jnp.float32) / hd)
    ang = positions.astype(jnp.float32)[..., None] * inv_freq
    cos = jnp.cos(ang)[:, :, None, :]
    sin = jnp.sin(ang)[:, :, None, :]
    xf = x.astype(jnp.float32)
    x1, x2 = jnp.split(xf, 2, axis=-1)
    out = jnp.concatenate([x1 * cos - x2 * sin, x2 * cos + x1 * sin], axis=-1)
    return out.astype(x.dtype)

def sliding_window_attention(q, k, v, sinks):
    B, S, Hq, hd = q.shape
    Hkv = k.shape[2]
    G = Hq // Hkv
    nb = S // ATTN_BLOCK
    qb = q.reshape(B, nb, ATTN_BLOCK, Hkv, G, hd)
    kb = k.reshape(B, nb, ATTN_BLOCK, Hkv, hd)
    vb = v.reshape(B, nb, ATTN_BLOCK, Hkv, hd)

    def with_prev(t):
        prev = jnp.pad(t[:, :-1], ((0, 0), (1, 0), (0, 0), (0, 0), (0, 0)))
        return jnp.concatenate([prev, t], axis=2)

    kk, vv = with_prev(kb), with_prev(vb)
    s = jnp.einsum('bnqhgd,bnkhd->bnhgqk', qb, kk,
                   preferred_element_type=jnp.float32) * (hd ** -0.5)
    qi = jnp.arange(ATTN_BLOCK)[:, None]
    kj = jnp.arange(2 * ATTN_BLOCK)[None, :]
    dist = ATTN_BLOCK + qi - kj
    band = (dist >= 0) & (dist < WINDOW)
    blk = jnp.arange(nb)[:, None, None]
    mask = band[None] & ((blk > 0) | (kj >= ATTN_BLOCK)[None])
    s = jnp.where(mask[None, :, None, None], s, -jnp.inf)
    sink = sinks.astype(jnp.float32).reshape(Hkv, G)[None, None, :, :, None, None]
    m = jnp.maximum(jnp.max(s, axis=-1, keepdims=True), sink)
    p = jnp.exp(s - m)
    denom = jnp.sum(p, axis=-1, keepdims=True) + jnp.exp(sink - m)
    o = jnp.einsum('bnhgqk,bnkhd->bnqhgd', (p / denom).astype(v.dtype), vv)
    return o.reshape(B, S, Hq * hd)

def hgrn2_chunkwise(q, f, i):
    B, S, H, dk = q.shape
    dv = i.shape[-1]
    C = REC_CHUNK
    nc = S // C
    k = (1.0 - f).reshape(B, nc, C, H, dk)
    logf = jnp.log(f).reshape(B, nc, C, H, dk)
    q = q.reshape(B, nc, C, H, dk)
    v = i.reshape(B, nc, C, H, dv)
    b = jnp.cumsum(logf, axis=2)
    b_last = b[:, :, -1]
    q_dec = q * jnp.exp(b)
    k_inv = k * jnp.exp(-b)
    k_out = k * jnp.exp(b_last[:, :, None] - b)
    causal = jnp.tril(jnp.ones((C, C), dtype=bool))
    a = jnp.einsum('bnthk,bnshk->bnhts', q_dec, k_inv)
    a = jnp.where(causal, a, 0.0)
    o_intra = jnp.einsum('bnhts,bnshv->bnthv', a, v)
    u = jnp.einsum('bnshk,bnshv->bnhkv', k_out, v)
    decay = jnp.exp(b_last)

    def step(state, xs):
        d, u_c = xs
        return d[..., None] * state + u_c, state

    s0 = jnp.zeros((B, H, dk, dv), jnp.float32)
    _, s_before = lax.scan(step, s0, (jnp.moveaxis(decay, 1, 0), jnp.moveaxis(u, 1, 0)))
    s_before = jnp.moveaxis(s_before, 0, 1)
    o_inter = jnp.einsum('bnthk,bnhkv->bnthv', q_dec, s_before)
    return (o_intra + o_inter).reshape(B, S, H, dv)

def hybrid_layer(x, c_act, positions, lb, norm_w, w_ada, b_ada, w_in,
                 q_norm_w, k_norm_w, sinks, rec_norm_w, w_out):
    B, S, _ = x.shape
    mod = c_act @ w_ada + b_ada
    shift, scale, gate = jnp.split(mod, 3, axis=-1)
    h = rms_norm(x, norm_w) * (1.0 + scale[:, None]) + shift[:, None]
    proj = h @ w_in
    offsets = [int(o) for o in np.cumsum(IN_SPLITS)[:-1]]
    aq, ak, av, ag, rq, rf, ri, rg = jnp.split(proj, offsets, axis=-1)

    aq = rope(rms_norm(aq.reshape(B, S, ATTN_HEADS, ATTN_HEAD_DIM), q_norm_w), positions)
    ak = rope(rms_norm(ak.reshape(B, S, ATTN_KV_HEADS, ATTN_HEAD_DIM), k_norm_w), positions)
    av = av.reshape(B, S, ATTN_KV_HEADS, ATTN_HEAD_DIM)
    attn = sliding_window_attention(aq, ak, av, sinks) * jax.nn.silu(ag)

    f = lb + (1.0 - lb) * jax.nn.sigmoid(rf.astype(jnp.float32))
    rec = hgrn2_chunkwise(rq.astype(jnp.float32).reshape(B, S, REC_HEADS, REC_KEY_DIM),
                          f.reshape(B, S, REC_HEADS, REC_KEY_DIM),
                          ri.astype(jnp.float32).reshape(B, S, REC_HEADS, REC_VAL_DIM))
    rec = rms_norm(rec, rec_norm_w).reshape(B, S, REC_WIDTH).astype(x.dtype)
    rec = rec * jax.nn.silu(rg)

    mixed = jnp.concatenate([attn, rec], axis=-1) @ w_out
    return x + gate[:, None] * mixed

def setup_inputs(seed: int = 0) -> dict:
    key = jax.random.key(seed)
    ks = jax.random.split(key, 16)
    f32 = jnp.float32
    x = jax.random.normal(ks[0], (BATCH, SEQ, D_MODEL), f32)
    c = jax.random.normal(ks[1], (BATCH, D_MODEL), f32)
    positions = jnp.broadcast_to(jnp.arange(SEQ, dtype=jnp.int32), (BATCH, SEQ))
    norm_w = 1.0 + 0.02 * jax.random.normal(ks[2], (DEPTH, D_MODEL), f32)
    w_ada = jax.random.normal(ks[3], (DEPTH, D_MODEL, 3 * D_MODEL), f32) * D_MODEL ** -0.5
    b_ada = 0.02 * jax.random.normal(ks[4], (DEPTH, 3 * D_MODEL), f32)
    w_in = jax.random.normal(ks[5], (DEPTH, D_MODEL, IN_WIDTH), f32) * D_MODEL ** -0.5
    q_norm_w = 1.0 + 0.02 * jax.random.normal(ks[6], (DEPTH, ATTN_HEAD_DIM), f32)
    k_norm_w = 1.0 + 0.02 * jax.random.normal(ks[7], (DEPTH, ATTN_HEAD_DIM), f32)
    sinks = 0.5 * jax.random.normal(ks[8], (DEPTH, ATTN_HEADS), f32)
    rec_norm_w = 1.0 + 0.02 * jax.random.normal(ks[9], (DEPTH, REC_VAL_DIM), f32)
    lower_bounds = 0.1 * jax.random.normal(ks[10], (DEPTH + 1, REC_KEY_WIDTH), f32)
    w_out = jax.random.normal(ks[11], (DEPTH, D_MIX, D_MODEL), f32) * D_MIX ** -0.5
    return {"x": x, "c": c, "positions": positions, "norm_w": norm_w,
            "w_ada": w_ada, "b_ada": b_ada, "w_in": w_in, "q_norm_w": q_norm_w,
            "k_norm_w": k_norm_w, "sinks": sinks, "rec_norm_w": rec_norm_w,
            "lower_bounds": lower_bounds, "w_out": w_out}

def reference(x, c, positions, norm_w, w_ada, b_ada, w_in, q_norm_w, k_norm_w,
              sinks, rec_norm_w, lower_bounds, w_out):
    c_act = jax.nn.silu(c)
    lb_all = jnp.cumsum(jax.nn.softmax(lower_bounds.astype(jnp.float32), axis=0), axis=0)
    h = x
    for l in range(DEPTH):
        h = hybrid_layer(h, c_act, positions, lb_all[l], norm_w[l], w_ada[l], b_ada[l],
                         w_in[l], q_norm_w[l], k_norm_w[l], sinks[l], rec_norm_w[l],
                         w_out[l])
    return h


_drawn_inputs = setup_inputs


def setup_inputs(seed=0):
    import zlib

    import numpy as np

    out = dict(_drawn_inputs(seed))
    spreads = {}
    factors = {'norm_w': 3.718, 'q_norm_w': 8.0, 'k_norm_w': 8.0, 'sinks': 200.0, 'rec_norm_w': 21.308}
    for name, (base, spread) in spreads.items():
        noise = np.random.default_rng([zlib.crc32(name.encode()), seed]).standard_normal(out[name].shape)
        drawn = base * np.exp(spread * noise) if base else spread * noise
        out[name] = __import__('jax').numpy.asarray(drawn.astype(out[name].dtype))
    for name, factor in factors.items():
        out[name] = (out[name] * factor).astype(out[name].dtype)
    return out
```

```python
from contextlib import ExitStack

import numpy as np

import concourse.bass as bass
from concourse import mybir

F32 = mybir.dt.float32
F32R = mybir.dt.float32r
I32 = mybir.dt.int32
ALU = mybir.AluOpType
ACT = mybir.ActivationFunctionType
AX_X = mybir.AxisListType.X

P = 128
D = 1024
KT = D // P
SEQ = 2048
SEGS = 2
SEG = SEQ // SEGS
NBLK = SEG // P
HEADS, GROUPS, HD = 16, 4, 64
GH = HEADS // GROUPS
QW = GH * HD
ATT = HEADS * HD
RHEADS, RK = 8, 128
QUAD = 512
QUADS = SEG // QUAD
QB = QUAD // P
CH = 64
NCH = QUAD // CH
OUT_BLKS = SEQ // P
UNITS = GROUPS + RHEADS
MIX = ATT + RHEADS * RK
FT = MIX // P
HALF = 512
WO_PARTS = 4
WO_F = FT // WO_PARTS
EPS = 1e-6
NEG = -1.0e30
COL_Q, COL_K, COL_V, COL_G = 0, ATT, ATT + GROUPS * HD, ATT + 2 * GROUPS * HD
COL_RQ = 2 * ATT + 2 * GROUPS * HD
COL_RF, COL_RI, COL_RG = COL_RQ + RHEADS * RK, COL_RQ + 2 * RHEADS * RK, COL_RQ + 3 * RHEADS * RK
REG = KT * (QW + HD)
TWO_PI = 2.0 * np.pi
PI_A = 6.28125
PI_B = float(np.float32(np.round((TWO_PI - PI_A) * 2.0 ** 21) / 2.0 ** 21))
PI_C = float(TWO_PI - PI_A - PI_B)
PI_MAX = 3.1415925
ROUND = 1.5 * 2.0 ** 23


def hybrid_layer(nc, x, cT, pos, norm_w, w_ada, b_cols, b_gate, w_in, qk_w, sinks, rec_w, lbT, w_out,
                 ident_d, masks_d, causal_d, freq_d, out, mixed):
    with ExitStack() as ctx:
        def sem(name):
            return ctx.enter_context(nc.semaphore(name))

        bank = [ctx.enter_context(nc.psum_tensor(f"bank{i}", [P, 512], F32)) for i in range(8)]

        def sbuf(where, name, shape, dt=F32):
            return where.enter_context(nc.sbuf_tensor(name, shape, dt))

        ident = sbuf(ctx, "ident", [P, P])
        gate_bc = sbuf(ctx, "gate_bc", [P, D])

        main = ExitStack()
        h_hi = sbuf(main, "h_hi", [P, KT, SEG], F32R)
        h_lo = sbuf(main, "h_lo", [P, KT, SEG], F32R)
        w_hi = [sbuf(main, f"w_hi{r}", [P, REG], F32R) for r in range(2)]
        w_lo = [sbuf(main, f"w_lo{r}", [P, REG], F32R) for r in range(2)]
        raw = [sbuf(main, f"raw{r}", [P, REG]) for r in range(2)]
        rot = sbuf(main, "rot", [P, NBLK, 2, 2, HD])
        masks = sbuf(main, "masks", [P, SEGS, 2 * P])
        mask_first = sbuf(main, "mask_first", [P, 2 * P])
        k_carry = sbuf(main, "k_carry", [P, GROUPS, P])
        v_carry = sbuf(main, "v_carry", [P, GROUPS, P])
        mod_a = sbuf(main, "mod_a", [P, KT])
        mod_b = sbuf(main, "mod_b", [P, KT])
        head_par = sbuf(main, "head_par", [P, RHEADS, 4])
        sink_bc = sbuf(main, "sink_bc", [P, HEADS])
        qk_wt = sbuf(main, "qk_wt", [P, 2, HD])
        rec_wt = sbuf(main, "rec_wt", [P, RK])
        minus_half = sbuf(main, "minus_half", [P, 8])
        half_pi = sbuf(main, "half_pi", [P, 1])
        freq = sbuf(main, "freq", [P, HD // 2])
        pos_f = sbuf(main, "pos_f", [P, SEQ // P])
        chunk_keep = sbuf(main, "chunk_keep", [P, QUAD])
        causal = sbuf(main, "causal", [P, P], I32)
        state = sbuf(main, "state", [P, RHEADS, RK])

        pre = ExitStack()
        wa = [sbuf(pre, f"wa{i}", [P, KT, HALF]) for i in range(2)]
        c_in = sbuf(pre, "c_in", [P, KT])
        c_th = sbuf(pre, "c_th", [P, KT])
        c_act = sbuf(pre, "c_act", [P, KT])
        c_bc = sbuf(pre, "c_bc", [P, KT, P])
        ones = sbuf(pre, "ones", [P, P])
        diag_junk = sbuf(pre, "diag_junk", [P, 4, P])
        mod_cols = sbuf(pre, "mod_cols", [P, 2 * KT])
        b_col = sbuf(pre, "b_col", [P, 2 * KT])
        b_gate_s = sbuf(pre, "b_gate_s", [P, D])
        norm_s = sbuf(pre, "norm_s", [P, KT])
        pos_i = sbuf(pre, "pos_i", [P, SEQ // P], I32)
        lb_in = sbuf(pre, "lb_in", [P, 2, RHEADS])
        lb_t = sbuf(pre, "lb_t", [P, 4, RHEADS])
        pre.close()

        nrm = ExitStack()
        xb = [sbuf(nrm, f"xb{i}", [P, D]) for i in range(2)]
        xn = [sbuf(nrm, f"xn{i}", [P, D]) for i in range(2)]
        x_sq = sbuf(nrm, "x_sq", [P, D])
        h_f = [sbuf(nrm, f"h_f{i}", [P, KT, P]) for i in range(2)]
        x_ss = sbuf(nrm, "x_ss", [P, 2])
        x_var = sbuf(nrm, "x_var", [P, 2])
        x_rinv = sbuf(nrm, "x_rinv", [P, 2])
        ang = sbuf(nrm, "ang", [P, NBLK, HD // 2])
        turns = sbuf(nrm, "turns", [P, NBLK, HD // 2])
        cosv = sbuf(nrm, "cosv", [P, NBLK, HD // 2])
        sinv = sbuf(nrm, "sinv", [P, NBLK, HD // 2])
        nrm.close()

        att = ExitStack()
        sq = sbuf(att, "sq", [P, GH + 1, HD])
        q_ss = sbuf(att, "q_ss", [P, GH + 1])
        q_var = sbuf(att, "q_var", [P, GH + 1])
        q_rinv = sbuf(att, "q_rinv", [P, GH + 1])
        qn = [sbuf(att, f"qn{i}", [P, GH + 1, HD]) for i in range(2)]
        rc = sbuf(att, "rc", [P, GH + 1, HD])
        rs = sbuf(att, "rs", [P, GH + 1, HD])
        q_rot = [sbuf(att, f"q_rot{i}", [P, GH, HD]) for i in range(2)]
        k_rot = [sbuf(att, f"k_rot{i}", [P, 2, HD]) for i in range(2)]
        qT = [sbuf(att, f"qT{i}", [P, 2, P]) for i in range(2)]
        kT = sbuf(att, "kT", [P, NBLK + 1, P])
        vv = sbuf(att, "vv", [P, NBLK + 1, 2, HD])
        sm = [sbuf(att, f"sm{i}", [P, GH, 2 * P]) for i in range(2)]
        row_max = sbuf(att, "row_max", [P, GH])
        m_row = sbuf(att, "m_row", [P, GH])
        neg_m = [sbuf(att, f"neg_m{i}", [P, GH]) for i in range(2)]
        sink_d = [sbuf(att, f"sink_d{i}", [P, GH]) for i in range(2)]
        den = [sbuf(att, f"den{i}", [P, GH]) for i in range(2)]
        sink_e = [sbuf(att, f"sink_e{i}", [P, GH]) for i in range(2)]
        den2 = sbuf(att, "den2", [P, GH])
        den3 = sbuf(att, "den3", [P, GH])
        r_den = [sbuf(att, f"r_den{i}", [P, GH]) for i in range(2)]
        pT = [sbuf(att, f"pT{i}", [P, GH, 2, P]) for i in range(2)]
        g_th = [sbuf(att, f"g_th{i}", [P, GH, HD]) for i in range(2)]
        g_s = [sbuf(att, f"g_s{i}", [P, GH, HD]) for i in range(2)]
        g_r = [sbuf(att, f"g_r{i}", [P, GH, HD]) for i in range(2)]
        o_mix = [sbuf(att, f"o_mix{i}", [P, GH, HD]) for i in range(2)]
        att.close()

        rec = ExitStack()
        par = sbuf(rec, "par", [P, 4])
        f_th = sbuf(rec, "f_th", [P, QUAD])
        f_r = sbuf(rec, "f_r", [P, QUAD])
        k_f = sbuf(rec, "k_f", [P, QUAD])
        log_f = sbuf(rec, "log_f", [P, QUAD])
        b_cum = sbuf(rec, "b_cum", [P, QUAD])
        e_b = [sbuf(rec, f"e_b{i}", [P, QUAD]) for i in range(2)]
        e_nb = sbuf(rec, "e_nb", [P, QUAD])
        b_rest = sbuf(rec, "b_rest", [P, QUAD])
        q_dec = [sbuf(rec, f"q_dec{i}", [P, QUAD]) for i in range(2)]
        k_inv = [sbuf(rec, f"k_inv{i}", [P, QUAD]) for i in range(2)]
        k_out = [sbuf(rec, f"k_out{i}", [P, QUAD]) for i in range(2)]
        k_nat = sbuf(rec, "k_nat", [P, QUAD])
        r_v = sbuf(rec, "r_v", [P, QB, RK])
        rg_th = sbuf(rec, "rg_th", [P, QB, RK])
        rg_s = sbuf(rec, "rg_s", [P, QB, RK])
        rg_w = sbuf(rec, "rg_w", [P, QB, RK])
        a_T = sbuf(rec, "a_T", [P, QB, P])
        s_in = [sbuf(rec, f"s_in{i}", [P, NCH, RK]) for i in range(2)]
        o_sq = sbuf(rec, "o_sq", [P, QB, RK])
        o_ss = sbuf(rec, "o_ss", [P, QB])
        o_var = sbuf(rec, "o_var", [P, QB])
        o_rinv = sbuf(rec, "o_rinv", [P, QB])
        r_mix = [sbuf(rec, f"r_mix{i}", [P, QB, RK]) for i in range(2)]
        rec.close()
        main.close()

        raw_rows = ExitStack()
        wo_raw = sbuf(raw_rows, "wo_raw", [P, FT, D])
        raw_rows.close()
        fin = ExitStack()
        wo_lo = sbuf(fin, "wo_lo", [P, FT, D], F32R)
        wo_hi = sbuf(fin, "wo_hi", [P, FT, D], F32R)
        m_raw = [sbuf(fin, f"m_raw{i}", [P, FT, P]) for i in range(2)]
        m_hi = [sbuf(fin, f"m_hi{i}", [P, FT, P], F32R) for i in range(2)]
        m_lo = [sbuf(fin, f"m_lo{i}", [P, FT, P], F32R) for i in range(2)]
        m_y = sbuf(fin, "m_y", [P, D])
        xo = [sbuf(fin, f"xo{i}", [P, D]) for i in range(2)]
        fin.close()

        phase_end = sem("phase_end")
        const_in = sem("const_in")
        const_ok = sem("const_ok")
        wa_in = [sem(f"wa_in{i}") for i in range(2)]
        wa_used = sem("wa_used")
        c_tanh = sem("c_tanh")
        c_ready = sem("c_ready")
        mod_used = sem("mod_used")
        pre_v = sem("pre_v")
        pre_e = sem("pre_e")
        x_in = [sem(f"x_in{i}") for i in range(2)]
        x_sqd = sem("x_sqd")
        x_rs = sem("x_rs")
        x_nrm = sem("x_nrm")
        x_T = sem("x_T")
        h_mod = sem("h_mod")
        h_split = sem("h_split")
        trig_v = sem("trig_v")
        trig_a = sem("trig_a")
        raw_in = [sem(f"raw_in{r}") for r in range(2)]
        hi_ok = [sem(f"hi_ok{r}") for r in range(2)]
        lo_ok = [sem(f"lo_ok{r}") for r in range(2)]
        qk_ok, vg_ok = sem("qk_ok"), sem("vg_ok")
        sq_ok, ss_ok, rinv_ok, qn_ok = sem("sq_ok"), sem("ss_ok"), sem("rinv_ok"), sem("qn_ok")
        rot_parts, rot_ok = sem("rot_parts"), sem("rot_ok")
        t_ok, tcopy_ok = sem("t_ok"), sem("tcopy_ok")
        s_ok, masked_ok, max_ok, exp_ok = sem("s_ok"), sem("masked_ok"), sem("max_ok"), sem("exp_ok")
        rden_ok = sem("rden_ok")
        vg_read, gs_ok, gr_ok = sem("vg_read"), sem("gs_ok"), sem("gr_ok")
        pt_ok, pta_ok, ptv_ok = sem("pt_ok"), sem("pta_ok"), sem("ptv_ok")
        pv_ok, omix_ok = sem("pv_ok"), sem("omix_ok")
        att_out = [sem(f"att_out{i}") for i in range(2)]
        carry_ok = sem("carry_ok")
        rf_ok, rq_ok, nat_ok = sem("rf_ok"), sem("rq_ok"), sem("nat_ok")
        par_ok, fth_ok, fr_ok, kf_ok = sem("par_ok"), sem("fth_ok"), sem("fr_ok"), sem("kf_ok")
        logf_ok, bcum_ok, eb_ok, enb_ok = sem("logf_ok"), sem("bcum_ok"), sem("eb_ok"), sem("enb_ok")
        rest_ok, erest_ok = sem("rest_ok"), sem("erest_ok")
        qdec_ok, kinv_ok, kout_ok = sem("qdec_ok"), sem("kinv_ok"), sem("kout_ok")
        nat_read, rgs_ok, rgw_ok = sem("nat_read"), sem("rgs_ok"), sem("rgw_ok")
        ak_ok, at_ok, knat_ok = sem("ak_ok"), sem("at_ok"), sem("knat_ok")
        state_in = sem("state_in")
        u_ok, st_ok, o_ok = sem("u_ok"), sem("st_ok"), sem("o_ok")
        oss_ok, orinv_ok, rmix_ok = sem("oss_ok"), sem("orinv_ok"), sem("rmix_ok")
        rec_out = [sem(f"rec_out{i}") for i in range(2)]
        wo_in = [sem(f"wo_in{i}") for i in range(WO_PARTS)]
        wohi_ok, wolo_ok = sem("wohi_ok"), sem("wolo_ok")
        m_in = [sem(f"m_in{i}") for i in range(2)]
        xo_in = [sem(f"xo_in{i}") for i in range(2)]
        mt_ok, mhi_ok, mlo_ok = sem("mt_ok"), sem("mhi_ok"), sem("mlo_ok")
        y_ok, ygate_ok, yout_ok = sem("y_ok"), sem("ygate_ok"), sem("yout_ok")
        y_out = [sem(f"y_out{i}") for i in range(2)]

        x_b = x.rearrange("(b p) d -> b p d", p=P)
        out_b = out.rearrange("(b p) d -> b p d", p=P)
        mixed_b = mixed.rearrange("(b p) f -> b p f", p=P)
        wi = w_in.rearrange("(k p) n -> p k n", p=P)
        wad = w_ada.rearrange("(k p) n -> p k n", p=P)
        wo_d = w_out.rearrange("(f p) n -> p f n", p=P)

        def waits_alone(eng, *waits):
            values = [v if isinstance(v, int) else eng.to_reg(v) for _, v in waits]
            eng.wait_ge(const_in, 16)
            for (semaphore, _), v in zip(waits, values):
                eng.wait_ge(semaphore, v)

        def phase_over(eng, k):
            eng.drain().then_inc(phase_end, 1)
            waits_alone(eng, (phase_end, 5 * k))

        def seg_phase(s, j):
            return s * 3 + (1 + j)

        def region(t, width):
            return t[:, 0:KT * width].rearrange("p (k n) -> p k n", k=KT)

        block = ctx.enter_context(nc.Block())

        @block.sync
        def _(sp):
            def load(r, pieces):
                at = 0
                width = sum(n for _, n in pieces)
                dst = region(raw[r], width)
                for col, n in pieces:
                    sp.dma_start(dst[:, :, at:at + n], wi[:, :, bass.ds(col, n)]).then_inc(raw_in[r], 16)
                    at += n

            def load_att(g):
                load(0, [(g * QW + COL_Q, QW), (g * HD + COL_K, HD)])

            def load_att_b(g):
                load(1, [(g * HD + COL_V, HD), (g * QW + COL_G, QW)])

            def load_rec(h):
                load(0, [(h * RK + COL_RF, RK), (h * RK + COL_RQ, RK)])

            def load_rec_b(h):
                load(1, [(h * RK + COL_RI, RK), (h * RK + COL_RG, RK)])

            for j in range(QUADS):
                sp.sem_inc(rec_out[j], 16)
            for dst, src in ((ident[:], ident_d), (masks[:], masks_d), (causal[:], causal_d), (freq[:], freq_d),
                             (c_in[:], cT), (pos_i[:], pos), (norm_s[:], norm_w), (b_col[:], b_cols),
                             (b_gate_s[:], b_gate), (qk_wt[:], qk_w), (sink_bc[:], sinks), (rec_wt[:], rec_w),
                             (lb_in[:], lbT)):
                sp.dma_start(dst, src).then_inc(const_in, 16)
            for t in range(6):
                if t >= 2:
                    sp.wait_ge(wa_used, t - 1)
                sp.dma_start(wa[t % 2][:], wad[:, :, t * HALF:(t + 1) * HALF]).then_inc(wa_in[t % 2], 16)
            phase_over(sp, 1)

            def segment(s, last):
                load_att(0)
                load_att_b(0)
                with sp.Fori(0, NBLK // 2) as bp:
                    for b in range(2):
                        sp.wait_ge(x_nrm, s * NBLK + bp * 2 + (b + 1))
                        sp.dma_start(xb[b][:], x_b[bass.ds(s * NBLK + bp * 2 + b, 1)].rearrange("o p d -> (o p) d")
                                     ).then_inc(x_in[b], 16)
                phase_over(sp, seg_phase(s, 1))

                def att_spill(g, i):
                    n = s * (GROUPS * NBLK) + g * NBLK
                    sp.wait_ge(omix_ok, n + (i + 1))
                    sp.dma_start(mixed_b[bass.ds(s * NBLK + i, 1), :, bass.ds(g * QW, QW)]
                                 .rearrange("o p f -> (o p) f"),
                                 o_mix[i % 2][:].rearrange("p h d -> p (h d)")).then_inc(att_out[i % 2], 16)

                def prefetch(w, load_a, load_b, arg):
                    for r, fn in ((0, load_a), (1, load_b)):
                        sp.wait_ge(lo_ok[r], w + 1)
                        fn(arg)

                with sp.Fori(0, GROUPS - 1) as g:
                    prefetch(s * UNITS + g, load_att, load_att_b, g + 1)
                    for i in range(NBLK):
                        att_spill(g, i)
                prefetch(s * UNITS + (GROUPS - 1), load_rec, load_rec_b, 0)
                for i in range(NBLK):
                    att_spill(GROUPS - 1, i)
                waits_alone(sp, *((att_out[i], (s + 1) * (16 * GROUPS * NBLK // 2)) for i in range(2)))
                phase_over(sp, seg_phase(s, 2))

                def rec_spill(h, j):
                    sp.wait_ge(rmix_ok, (s * (RHEADS * QUADS) + h * QUADS) * QB + (j + 1) * QB)
                    sp.dma_start(mixed_b[bass.ds(s * NBLK + j * QB, QB), :, bass.ds(h * RK + ATT, RK)]
                                 .rearrange("b p f -> p b f"), r_mix[j][:]).then_inc(rec_out[j], 16)

                with sp.Fori(0, RHEADS - 1) as h:
                    prefetch(s * UNITS + h + GROUPS, load_rec, load_rec_b, h + 1)
                    for j in range(QUADS):
                        rec_spill(h, j)
                if last:
                    sp.wait_ge(nat_ok, SEGS * RHEADS * QUADS)
                    load_mixed(0, 0)
                    for t in range(WO_PARTS):
                        fs = slice(t * WO_F, (t + 1) * WO_F)
                        sp.dma_start(wo_raw[:, fs, :], wo_d[:, fs, :]).then_inc(wo_in[t], 16)
                for j in range(QUADS):
                    rec_spill(RHEADS - 1, j)
                waits_alone(sp, *((rec_out[j], (s + 1) * (16 * RHEADS) + 16) for j in range(QUADS)))
                phase_over(sp, seg_phase(s, 3))

            def load_mixed(m, b):
                sp.dma_start(m_raw[b][:].rearrange("p f t -> p (f t)"),
                             mixed_b[bass.ds(m, 1)].rearrange("o p f -> (o p) f")).then_inc(m_in[b], 16)

            def load_residual(m, b):
                sp.dma_start(xo[b][:], x_b[bass.ds(m, 1)].rearrange("o p d -> (o p) d")).then_inc(xo_in[b], 16)

            with sp.Fori(0, SEGS - 1) as s:
                segment(s, False)
            segment(SEGS - 1, True)

            load_mixed(1, 1)
            for b in range(2):
                load_residual(b, b)
            sp.wait_ge(mt_ok, 4)
            load_mixed(2, 0)

            def rows_out(n, b, ahead):
                if ahead >= 3:
                    sp.wait_ge(mt_ok, n * 4 + 4 * (b + 2))
                    load_mixed(n + (b + 3), 1 - b)
                sp.wait_ge(yout_ok, n * 2 + 2 * (b + 1))
                sp.dma_start(out_b[bass.ds(n + b, 1)].rearrange("o p d -> (o p) d"), xo[b][:]).then_inc(y_out[b], 16)
                if ahead >= 2:
                    sp.wait_ge(y_out[b], n * 8 + 16)
                    load_residual(n + (b + 2), b)

            with sp.Fori(0, OUT_BLKS // 2 - 2) as bp:
                for b in range(2):
                    rows_out(bp * 2, b, 3)
            for m in range(OUT_BLKS - 4, OUT_BLKS):
                rows_out(m - m % 2, m % 2, OUT_BLKS - 1 - m)
            for b in range(2):
                sp.wait_ge(y_out[b], 16 * (SEQ // P // 2))

        @block.tensor
        def _(pe):
            pe.wait_ge(c_ready, 1)
            for t in range(6):
                pe.wait_ge(wa_in[t % 2], 16 * (t // 2 + 1))
                if t >= 2:
                    pe.wait_ge(mod_used, t - 1)
                for k in range(KT):
                    mm = pe.matmul(bank[t % 2][:, :], c_bc[:, k, :], wa[t % 2][:, k, :],
                                   start=(k == 0), stop=(k == KT - 1))
                mm.then_inc(wa_used, 1)
            phase_over(pe, 1)

            def split_products(dst, pairs, first, last):
                mm = None
                for m, (a, b) in enumerate(pairs):
                    mm = pe.matmul(dst, a, b, start=(first and m == 0), stop=(last and m == 2))
                return mm

            def project_rows(dst, r, i, c0, c1, width, k):
                wh, wl = region(w_hi[r], width)[:, k, c0:c1], region(w_lo[r], width)[:, k, c0:c1]
                ah, al = h_hi[:, k, i * P:(i + 1) * P], h_lo[:, k, i * P:(i + 1) * P]
                return split_products(dst, ((ah, wh), (ah, wl), (al, wh)), k == 0, k == KT - 1)

            def project_cols(dst, c0, j, k):
                wh, wl = region(w_hi[0], 2 * RK)[:, k, c0:c0 + RK], region(w_lo[0], 2 * RK)[:, k, c0:c0 + RK]
                ah, al = h_hi[:, k, j * QUAD:(j + 1) * QUAD], h_lo[:, k, j * QUAD:(j + 1) * QUAD]
                return split_products(dst, ((wh, ah), (wl, ah), (wh, al)), k == 0, k == KT - 1)

            def weights_ready(r, w):
                pe.wait_ge(hi_ok[r], w + 1)
                pe.wait_ge(lo_ok[r], w + 1)

            def att_iter(s, g, i, head, tail1, tail2, first):
                n = s * (GROUPS * NBLK) + g * NBLK
                w = s * UNITS + g
                steady = not first
                if head:
                    if i == 0:
                        weights_ready(0, w)
                    if steady or i >= 1:
                        pe.wait_ge(sq_ok, n + i)
                        pe.wait_ge(qn_ok, n + i)
                    for k in range(KT):
                        mm = project_rows(bank[0][:, 0:QW + HD], 0, i, 0, QW + HD, QW + HD, k)
                    mm.then_inc(qk_ok, 1)
                if tail1:
                    j = (i - 1) % NBLK
                    pe.wait_ge(tcopy_ok, n * 2 + 2 * i)
                    if steady or i >= 2:
                        pe.wait_ge(masked_ok, n * GH + GH * (i - 1))
                    for h in range(GH):
                        lo = HD * (h % 2)
                        mm = pe.matmul(bank[2 + h % 2][:, (h // 2) * 2 * P:(h // 2 + 1) * 2 * P],
                                       qT[j % 2][lo:lo + HD, h // 2, :],
                                       kT[lo:lo + HD, j:j + 2, :], start=True, stop=True)
                    mm.then_inc(s_ok, 1)
                if head:
                    if i == 0:
                        weights_ready(1, w)
                    if steady or i >= 1:
                        pe.wait_ge(vg_read, n * 2 + 2 * i)
                        pe.wait_ge(gs_ok, n + i)
                    for k in range(KT):
                        mm = project_rows(bank[1][:, 0:QW + HD], 1, i, 0, QW + HD, QW + HD, k)
                    mm.then_inc(vg_ok, 1)
                if tail2:
                    j = (i - 2) % NBLK
                    pe.wait_ge(pta_ok, n + (i - 1))
                    pe.wait_ge(ptv_ok, n + (i - 1))
                    if steady or i >= 3:
                        pe.wait_ge(omix_ok, n + (i - 2))
                    for h in range(GH):
                        for half in range(2):
                            mm = pe.matmul(bank[7][:, h * P:(h + 1) * P], pT[j % 2][:, h, half, :],
                                           vv[:, j + half, :, :].rearrange("p a d -> p (a d)"),
                                           start=(half == 0), stop=(half == 1))
                    mm.then_inc(pv_ok, 1)
                if tail1:
                    j = (i - 1) % NBLK
                    pe.wait_ge(exp_ok, n * (GH + 1) + (GH + 1) * i)
                    if steady or i >= 2:
                        pe.wait_ge(pta_ok, n + (i - 1))
                        pe.wait_ge(ptv_ok, n + (i - 1))
                    for h in range(GH):
                        for half in range(2):
                            at = ((h % 2) * 2 + half) * P
                            mm = pe.transpose(bank[5 + h // 2][:, at:at + P],
                                              sm[j % 2][:, h, half * P:(half + 1) * P], ident[:])
                    mm.then_inc(pt_ok, 1)
                if head:
                    pe.wait_ge(rot_ok, n * 2 + 2 * (i + 1))
                    if steady or i >= 1:
                        pe.wait_ge(tcopy_ok, n * 2 + 2 * i)
                    for h in range(2):
                        pe.transpose(bank[4][:, h * P:(h + 1) * P],
                                     q_rot[i % 2][:, 2 * h:2 * h + 2, :].rearrange("p a d -> p (a d)"), ident[:])
                    pe.transpose(bank[4][:, 2 * P:3 * P], k_rot[i % 2][:].rearrange("p a d -> p (a d)"),
                                 ident[:]).then_inc(t_ok, 1)

            def rec_iter(s, h, j, head, tail, first):
                n = s * (RHEADS * QUADS) + h * QUADS
                w = s * UNITS + h + GROUPS
                steady = not first
                jt = (j - 1) % QUADS
                if head:
                    if j == 0:
                        weights_ready(0, w)
                    if steady or j >= 1:
                        pe.wait_ge(fth_ok, n + j)
                    for k in range(KT):
                        mm = project_cols(bank[0][:, :], 0, j, k)
                    mm.then_inc(rf_ok, 1)
                if tail:
                    pe.wait_ge(qdec_ok, n + j)
                    pe.wait_ge(kinv_ok, n + j)
                    pe.wait_ge(kout_ok, n + j)
                    if steady or j >= 2:
                        pe.wait_ge(at_ok, n * QB + QB * (j - 1))
                        pe.wait_ge(st_ok, n * NCH + NCH * (j - 1))
                    for b in range(QB):
                        pe.matmul(bank[4][:, b * P:(b + 1) * P], k_inv[jt][:, b * P:(b + 1) * P],
                                  q_dec[jt][:, b * P:(b + 1) * P], start=True, stop=True)
                    for b in range(QB):
                        mm = pe.transpose(bank[5][:, b * P:(b + 1) * P], k_out[jt][:, b * P:(b + 1) * P], ident[:])
                    mm.then_inc(ak_ok, 1)
                if head:
                    if steady or j >= 1:
                        pe.wait_ge(qdec_ok, n + j)
                    for k in range(KT):
                        mm = project_cols(bank[1][:, :], RK, j, k)
                    mm.then_inc(rq_ok, 1)
                if tail:
                    pe.wait_ge(knat_ok, n + j)
                    pe.wait_ge(nat_read, n * 4 + 4 * j)
                    for c in range(NCH):
                        lo, b = CH * (c % 2), c // 2
                        mm = pe.matmul(bank[6 - c % 2][:, b * P:(b + 1) * P], k_nat[lo:lo + CH, b * P:(b + 1) * P],
                                       r_v[lo:lo + CH, b, :], start=True, stop=True)
                    mm.then_inc(u_ok, 1)
                for half in range(2):
                    if head:
                        if half == 0:
                            if j == 0:
                                weights_ready(1, w)
                            if steady or j >= 1:
                                pe.wait_ge(nat_read, n * 4 + 4 * j)
                                pe.wait_ge(rgs_ok, n * 2 + 2 * j)
                        for b in range(2):
                            for k in range(KT):
                                mm = project_rows(bank[2 + half][:, b * 2 * RK:(b + 1) * 2 * RK], 1,
                                                  j * QB + half * 2 + b, 0, 2 * RK, 2 * RK, k)
                        if half == 1:
                            mm.then_inc(nat_ok, 1)
                    if tail and half == 0:
                        pe.wait_ge(at_ok, n * QB + QB * j)
                        pe.wait_ge(st_ok, n * NCH + NCH * j)
                        if steady or j >= 2:
                            pe.wait_ge(rmix_ok, n * QB + QB * (j - 1))
                        for b in range(QB):
                            dst = bank[7][:, b * P:(b + 1) * P]
                            pe.matmul(dst, a_T[:, b, :], r_v[:, b, :], start=True, stop=False,
                                      skip_group_check=True)
                            for c in range(2):
                                t0 = b * P + c * CH
                                mm = pe.matmul(bank[7][c * CH:(c + 1) * CH, b * P:(b + 1) * P],
                                               q_dec[jt][:, t0:t0 + CH], s_in[jt][:, 2 * b + c, :],
                                               start=False, stop=True, skip_group_check=True)
                        mm.then_inc(o_ok, 1)

            with pe.Fori(0, SEGS) as s:
                with pe.Fori(0, NBLK // 2) as bp:
                    for b in range(2):
                        n = s * NBLK + bp * 2 + b
                        pe.wait_ge(x_nrm, n + 3)
                        pe.wait_ge(h_mod, n * 2 + 2)
                        for k in range(KT):
                            mm = pe.transpose(bank[2 * b + k // 4][:, (k % 4) * P:(k % 4 + 1) * P],
                                              xn[b][:, k * P:(k + 1) * P], ident[:])
                        mm.then_inc(x_T, 1)
                phase_over(pe, seg_phase(s, 1))
                for i in range(NBLK):
                    att_iter(s, 0, i, True, i >= 1, i >= 2, True)
                with pe.Fori(1, GROUPS) as g:
                    for i in range(NBLK):
                        att_iter(s, g, i, True, True, True, False)
                att_iter(s, GROUPS - 1, NBLK, False, True, True, False)
                att_iter(s, GROUPS - 1, NBLK + 1, False, False, True, False)
                phase_over(pe, seg_phase(s, 2))
                for j in range(QUADS):
                    rec_iter(s, 0, j, True, j >= 1, True)
                with pe.Fori(1, RHEADS) as h:
                    for j in range(QUADS):
                        rec_iter(s, h, j, True, True, False)
                rec_iter(s, RHEADS - 1, QUADS, False, True, False)
                phase_over(pe, seg_phase(s, 3))

            def transposes(n, b, q):
                if q == 0:
                    pe.wait_ge(m_in[b], n * 8 + 16)
                if not isinstance(n, int) or n + b > 0 or q >= 2:
                    pe.wait_ge(mlo_ok, n * 4 + (4 * b + q - 1))
                for f in range(4):
                    mm = pe.transpose(bank[q % 2][:, f * P:(f + 1) * P], m_raw[b][:, q * 4 + f, :], ident[:])
                mm.then_inc(mt_ok, 1)

            def out_rows(n, b, first, last):
                pe.wait_ge(mlo_ok, n * 4 + 4 * (b + 1))
                if not first:
                    pe.wait_ge(ygate_ok, n * 2 + 2 * (b - 1))
                for f in range(FT):
                    if first and b == 0:
                        pe.wait_ge(wolo_ok, f + 1)
                    mh, ml = m_hi[b][:, f, :], m_lo[b][:, f, :]
                    for c in range(2):
                        wh, wl = wo_hi[:, f, c * HALF:(c + 1) * HALF], wo_lo[:, f, c * HALF:(c + 1) * HALF]
                        mm = split_products(bank[4 + 2 * b + c][:, :], ((mh, wh), (mh, wl), (ml, wh)), f == 0, f == FT - 1)
                    if not last and f % 4 == 2:
                        transposes(n + 2 * b, 1 - b, f // 4)
                mm.then_inc(y_ok, 1)

            for q in range(4):
                transposes(0, 0, q)
            out_rows(0, 0, True, False)
            out_rows(0, 1, True, False)
            with pe.Fori(1, OUT_BLKS // 2 - 1) as bp:
                out_rows(bp * 2, 0, False, False)
                out_rows(bp * 2, 1, False, False)
            out_rows(OUT_BLKS - 2, 0, False, False)
            out_rows(OUT_BLKS - 2, 1, False, True)

        @block.scalar
        def _(act):
            act.wait_ge(const_in, 16 * 13)
            act.activation(c_th[:], c_in[:], ACT.Tanh, scale=0.5).then_inc(c_tanh, 1)
            act.wait_ge(pre_v, 2)
            act.activation(lb_t[:, 2:4, :], lb_t[:, 0:2, :], ACT.Exp).then_inc(pre_e, 1)
            act.sem_inc(x_sqd, 1)
            act.sem_inc(h_mod, 4)
            phase_over(act, 1)

            def split_hi(r, w, size):
                act.wait_ge(raw_in[r], w * 32 + 32)
                act.activation(w_hi[r][:, 0:size], raw[r][:, 0:size], ACT.Copy).then_inc(hi_ok[r], 1)

            def att_iter(s, g, i, head, tail1, tail2, first):
                n = s * (GROUPS * NBLK) + g * NBLK
                w = s * UNITS + g
                if head and i == 0:
                    if not first:
                        act.wait_ge(qk_ok, n)
                    split_hi(0, w, REG)
                    if first:
                        split_hi(1, w, REG)
                if head:
                    act.wait_ge(qk_ok, n + (i + 1))
                    if not first or i >= 1:
                        act.wait_ge(ss_ok, n + i)
                    act.activation(sq[:].rearrange("p h d -> p (h d)"), bank[0][:, 0:QW + HD],
                                   ACT.Square).then_inc(sq_ok, 1)
                if head and i == 0 and not first:
                    act.wait_ge(vg_ok, n)
                    split_hi(1, w, REG)
                if tail1:
                    j = (i - 1) % NBLK
                    act.wait_ge(max_ok, n * 3 + 3 * i)
                    if not first or i >= 3:
                        act.wait_ge(rden_ok, n * 3 + 3 * (i - 2))
                    for h in range(GH):
                        act.activation(sm[j % 2][:, h, :], sm[j % 2][:, h, :], ACT.Exp,
                                       bias=neg_m[j % 2][:, h:h + 1],
                                       accum_out=den[j % 2][:, h:h + 1]).then_inc(exp_ok, 1)
                    act.activation(sink_e[j % 2][:], sink_d[j % 2][:], ACT.Exp).then_inc(exp_ok, 1)
                if head:
                    act.wait_ge(vg_ok, n + (i + 1))
                    if not first or i >= 2:
                        act.wait_ge(gs_ok, n + (i - 1))
                    if i == 0 and not first:
                        act.wait_ge(carry_ok, s * GROUPS + g)
                    act.activation(vv[:, i + 1, :, :], bank[1][:, 0:HD].unsqueeze(1).to_broadcast([P, 2, HD]),
                                   ACT.Copy).then_inc(vg_read, 1)
                    act.activation(g_th[i % 2][:].rearrange("p h d -> p (h d)"), bank[1][:, HD:HD + QW],
                                   ACT.Tanh, scale=0.5).then_inc(vg_read, 1)
                if tail1:
                    j = (i - 1) % NBLK
                    act.wait_ge(pt_ok, n + i)
                    if not first or i >= 3:
                        act.wait_ge(pv_ok, n + (i - 2))
                    act.activation(pT[j % 2][:, 0:2, :, :].rearrange("p h a q -> p (h a q)"), bank[5][:, :],
                                   ACT.Copy).then_inc(pta_ok, 1)

            def rec_iter(s, h, j, head, tail, first):
                n = s * (RHEADS * QUADS) + h * QUADS
                w = s * UNITS + h + GROUPS
                jt = (j - 1) % QUADS
                if head and j == 0:
                    if not first:
                        act.wait_ge(rq_ok, n)
                    split_hi(0, w, KT * 2 * RK)
                    if first:
                        split_hi(1, w, KT * 2 * RK)
                if tail:
                    act.wait_ge(nat_ok, n + j)
                    if not first or j >= 2:
                        act.wait_ge(o_ok, n + (j - 1))
                        act.wait_ge(rgs_ok, n * 2 + 2 * (j - 1))
                    for half in range(2):
                        nat = bank[2 + half][:, :].rearrange("p (b n) -> p b n", b=2)
                        act.activation(r_v[:, 2 * half:2 * half + 2, :], nat[:, :, 0:RK],
                                       ACT.Copy).then_inc(nat_read, 1)
                        act.activation(rg_th[:, 2 * half:2 * half + 2, :], nat[:, :, RK:2 * RK],
                                       ACT.Tanh, scale=0.5).then_inc(nat_read, 1)
                if head:
                    act.wait_ge(rf_ok, n + (j + 1))
                    if not first or j >= 1:
                        act.wait_ge(kf_ok, n + j)
                    act.activation(f_th[:], bank[0][:, :], ACT.Tanh, scale=0.5).then_inc(fth_ok, 1)
                if tail:
                    act.wait_ge(ak_ok, n + j)
                    act.activation(k_nat[:], bank[5][:, :], ACT.Copy).then_inc(knat_ok, 1)
                if head and j == 0 and not first:
                    act.wait_ge(nat_ok, n)
                    split_hi(1, w, KT * 2 * RK)
                if head:
                    act.wait_ge(fr_ok, n + (j + 1))
                    if not first or j >= 1:
                        act.wait_ge(bcum_ok, n + j)
                    act.activation(log_f[:], f_r[:], ACT.Ln, bias=par[:, 0:1]).then_inc(logf_ok, 1)
                    act.wait_ge(bcum_ok, n + (j + 1))
                    if not first or j >= 2:
                        act.wait_ge(st_ok, n * NCH + NCH * (j - 1))
                    act.activation(e_b[j % 2][:], b_cum[:], ACT.Exp).then_inc(eb_ok, 1)
                    if not first or j >= 1:
                        act.wait_ge(kinv_ok, n + j)
                    act.activation(e_nb[:], b_cum[:], ACT.Exp, scale=-1.0).then_inc(enb_ok, 1)
                    act.wait_ge(rest_ok, n + (j + 1))
                    act.activation(b_rest[:], b_rest[:], ACT.Exp).then_inc(erest_ok, 1)
                if tail:
                    act.wait_ge(o_ok, n + j)
                    if not first or j >= 2:
                        act.wait_ge(orinv_ok, n * 2 + 2 * (j - 1))
                    for b in range(QB):
                        act.activation(o_sq[:, b, :], bank[7][:, b * P:(b + 1) * P], ACT.Square,
                                       accum_out=o_ss[:, b:b + 1]).then_inc(oss_ok, 1)

            with act.Fori(0, SEGS) as s:
                act.wait_ge(trig_v, s * 11 + 7)
                act.activation(sinv[:].rearrange("p b f -> p (b f)"), ang[:].rearrange("p b f -> p (b f)"),
                               ACT.Sin).then_inc(trig_a, 1)
                act.activation(turns[:].rearrange("p b f -> p (b f)"), ang[:].rearrange("p b f -> p (b f)"),
                               ACT.Abs).then_inc(trig_a, 1)
                act.wait_ge(trig_a, s * 3 + 2)
                act.activation(cosv[:].rearrange("p b f -> p (b f)"), turns[:].rearrange("p b f -> p (b f)"),
                               ACT.Sin, bias=half_pi[:, 0:1], scale=-1.0).then_inc(trig_a, 1)
                with act.Fori(0, NBLK // 2) as bp:
                    for b in range(2):
                        n = s * NBLK + bp * 2 + b
                        act.wait_ge(x_in[b], (s * (NBLK // 2) + bp) * 16 + 16)
                        act.wait_ge(x_sqd, n + 1)
                        act.activation(x_sq[:], xb[b][:], ACT.Square,
                                       accum_out=x_ss[:, b:b + 1]).then_inc(x_sqd, 1)
                        act.wait_ge(x_T, n + 1)
                        act.wait_ge(h_split, n * 2 + 2)
                        for half in range(2):
                            for q in range(4):
                                k = half * 4 + q
                                a = act.activation(h_f[b][:, k, :], bank[2 * b + half][:, q * P:(q + 1) * P],
                                                   ACT.Identity, bias=mod_b[:, k:k + 1], scale=mod_a[:, k:k + 1])
                            a.then_inc(h_mod, 1)
                phase_over(act, seg_phase(s, 1))
                for i in range(NBLK):
                    att_iter(s, 0, i, True, i >= 1, i >= 2, True)
                with act.Fori(1, GROUPS) as g:
                    for i in range(NBLK):
                        att_iter(s, g, i, True, True, True, False)
                att_iter(s, GROUPS - 1, NBLK, False, True, True, False)
                phase_over(act, seg_phase(s, 2))
                for j in range(QUADS):
                    rec_iter(s, 0, j, True, j >= 1, True)
                with act.Fori(1, RHEADS) as h:
                    for j in range(QUADS):
                        rec_iter(s, h, j, True, True, False)
                rec_iter(s, RHEADS - 1, QUADS, False, True, False)
                phase_over(act, seg_phase(s, 3))

            def m_rounded(n, b, first):
                for q in range(4):
                    act.wait_ge(mt_ok, n * 4 + (4 * b + q + 1))
                    if not first:
                        act.wait_ge(y_ok, n + (b - 1))
                    act.activation(m_hi[b][:, 4 * q:4 * q + 4, :].rearrange("p f t -> p (f t)"), bank[q % 2][:, :],
                                   ACT.Copy).then_inc(mhi_ok, 1)

            for f in range(FT):
                if f == 1:
                    m_rounded(0, 0, True)
                if f % WO_F == 0:
                    act.wait_ge(wo_in[f // WO_F], 16)
                act.activation(wo_hi[:, f, :], wo_raw[:, f, :], ACT.Copy).then_inc(wohi_ok, 1)

            m_rounded(0, 1, True)
            with act.Fori(1, OUT_BLKS // 2) as bp:
                for b in range(2):
                    m_rounded(bp * 2, b, False)

        @block.vector
        def _(dve):
            ready = 0
            for t, v in ((ones, 1.0), (half_pi, float(np.pi / 2)), (state, 0.0), (k_carry, 0.0), (v_carry, 0.0),
                         (chunk_keep, 1.0)):
                dve.memset(t[:], v).then_inc(const_ok, 1)
                ready += 1
            dve.wait_ge(const_ok, ready)
            dve.memset(chunk_keep[:].rearrange("p (c t) -> p c t", t=CH)[:, :, 0:1], 0.0).then_inc(const_ok, 1)
            dve.wait_ge(const_in, 16 * 13)
            dve.tensor_tensor(lb_t[:, 2, :], lb_in[:, 0, :], lb_in[:, 1, :], ALU.max).then_inc(pre_v, 1)
            dve.wait_ge(pre_v, 1)
            dve.tensor_tensor(lb_t[:, 0:2, :], lb_in[:], lb_t[:, 2:3, :].to_broadcast([P, 2, RHEADS]),
                              ALU.subtract).then_inc(pre_v, 1)
            dve.wait_ge(c_tanh, 1)
            dve.scalar_tensor_tensor(c_act[:], c_th[:], 1.0, c_in[:], ALU.add, ALU.mult).then_inc(pre_v, 1)
            dve.wait_ge(pre_v, 3)
            for k in range(KT):
                a = dve.tensor_scalar(c_bc[:, k, :], ones[:], c_act[:, k:k + 1], 0.5, ALU.mult, ALU.mult)
            a.then_inc(c_ready, 1)
            dve.tensor_copy(pos_f[:], pos_i[:]).then_inc(pre_v, 1)
            dve.wait_ge(pre_e, 1)
            dve.tensor_tensor(lb_t[:, 0, :], lb_t[:, 2, :], lb_t[:, 3, :], ALU.add).then_inc(pre_v, 1)
            dve.wait_ge(pre_v, 5)
            dve.reciprocal(lb_t[:, 1, :], lb_t[:, 0, :]).then_inc(pre_v, 1)
            dve.wait_ge(pre_v, 6)
            dve.tensor_tensor(head_par[:, :, 0], lb_t[:, 2, :], lb_t[:, 1, :], ALU.mult).then_inc(pre_v, 1)
            dve.wait_ge(pre_v, 7)
            dve.tensor_scalar(head_par[:, :, 1], head_par[:, :, 0], -0.5, 0.5, ALU.mult, ALU.add).then_inc(pre_v, 1)
            dve.tensor_scalar(head_par[:, :, 2], head_par[:, :, 0], 0.5, -0.5, ALU.mult, ALU.add).then_inc(pre_v, 1)
            dve.memset(head_par[:, :, 3], 0.0).then_inc(pre_v, 1)
            dve.tensor_scalar(qk_wt[:, 0, :], qk_wt[:, 0, :], float(HD) ** -0.5, None, ALU.mult).then_inc(pre_v, 1)
            dve.tensor_scalar(rec_wt[:], rec_wt[:], 0.5, None, ALU.mult).then_inc(pre_v, 1)
            for t in range(6):
                dve.wait_ge(wa_used, t + 1)
                if t < 4:
                    if t >= 1:
                        dve.wait_ge(mod_used, t)
                    for q in range(4):
                        a = dve.tensor_tensor_reduce(diag_junk[:, q, :], bank[t % 2][:, q * P:(q + 1) * P], ident[:],
                                                     1.0, 0.0, ALU.mult, ALU.add, mod_cols[:, 4 * t + q:4 * t + q + 1])
                else:
                    g0 = (t - 4) * HALF
                    a = dve.tensor_tensor(gate_bc[:, g0:g0 + HALF], bank[t % 2][:, :], b_gate_s[:, g0:g0 + HALF], ALU.add)
                a.then_inc(mod_used, 1)
            dve.wait_ge(mod_used, 6)
            dve.tensor_tensor(mod_b[:], mod_cols[:, 0:KT], b_col[:, 0:KT], ALU.add).then_inc(pre_v, 1)
            dve.tensor_tensor(mod_a[:], mod_cols[:, KT:2 * KT], b_col[:, KT:2 * KT], ALU.add).then_inc(pre_v, 1)
            dve.wait_ge(pre_v, 14)
            dve.scalar_tensor_tensor(mod_a[:], mod_a[:], 1.0, norm_s[:], ALU.add, ALU.mult).then_inc(pre_v, 1)
            dve.sem_inc(x_nrm, 2)
            dve.sem_inc(h_split, 4)
            phase_over(dve, 1)

            def split_lo(r, w, size):
                dve.wait_ge(hi_ok[r], w + 1)
                dve.tensor_tensor(w_lo[r][:, 0:size], raw[r][:, 0:size], w_hi[r][:, 0:size].bitcast(F32),
                                  ALU.subtract).then_inc(lo_ok[r], 1)

            def att_iter(s, g, i, head, tail1, tail2, first, gt):
                n = s * (GROUPS * NBLK) + g * NBLK
                w = s * UNITS + g
                if head and i == 0:
                    split_lo(0, w, REG)
                    if first:
                        split_lo(1, w, REG)
                    dve.tensor_copy(kT[:, 0, :], k_carry[:, bass.ds(g, 1), :].rearrange("p o t -> p (o t)"))
                    dve.tensor_copy(vv[:, 0, :, :].rearrange("p a d -> p (a d)"),
                                    v_carry[:, bass.ds(g, 1), :].rearrange("p o t -> p (o t)"))
                if head:
                    dve.wait_ge(sq_ok, n + (i + 1))
                    dve.reduce_sum(q_ss[:], sq[:], AX_X).then_inc(ss_ok, 1)
                if tail1:
                    j = (i - 1) % NBLK
                    waits = [(s_ok, n + i)]
                    if not first or i >= 2:
                        waits.append((max_ok, n * 3 + 3 * (i - 1)))
                    if not first or i >= 3:
                        waits.append((pt_ok, n + (i - 2)))
                    waits_alone(dve, *waits)
                    mask = mask_first[:] if j == 0 else masks[:, SEGS - 1, :]
                    for h in range(GH):
                        dve.tensor_tensor_reduce(sm[j % 2][:, h, :],
                                                 bank[2 + h % 2][:, (h // 2) * 2 * P:(h // 2 + 1) * 2 * P],
                                                 mask, 1.0, NEG, ALU.add, ALU.max,
                                                 row_max[:, h:h + 1]).then_inc(masked_ok, 1)
                    dve.wait_ge(masked_ok, n * GH + GH * i)
                    sink = sink_bc[:, bass.ds(gt * GH, GH)]
                    dve.tensor_tensor(m_row[:], row_max[:], sink, ALU.max).then_inc(max_ok, 1)
                    dve.wait_ge(max_ok, n * 3 + (3 * i - 2))
                    dve.tensor_scalar(neg_m[j % 2][:], m_row[:], -1.0, None, ALU.mult).then_inc(max_ok, 1)
                    dve.tensor_tensor(sink_d[j % 2][:], sink, m_row[:], ALU.subtract).then_inc(max_ok, 1)
                if head:
                    dve.wait_ge(rinv_ok, n * 2 + 2 * (i + 1))
                    dve.tensor_tensor(qn[i % 2][:], bank[0][:, 0:QW + HD].rearrange("p (h d) -> p h d", d=HD),
                                      q_rinv[:].unsqueeze(2).to_broadcast([P, GH + 1, HD]),
                                      ALU.mult).then_inc(qn_ok, 1)
                if head and i == 0 and not first:
                    split_lo(1, w, REG)
                if tail1:
                    j = (i - 1) % NBLK
                    dve.wait_ge(exp_ok, n * (GH + 1) + (GH + 1) * i)
                    dve.tensor_tensor(den2[:], den[j % 2][:], sink_e[j % 2][:], ALU.add).then_inc(rden_ok, 1)
                    dve.wait_ge(rden_ok, n * 3 + (3 * i - 2))
                    dve.tensor_scalar(den3[:], den2[:], 2.0, None, ALU.mult).then_inc(rden_ok, 1)
                    dve.wait_ge(rden_ok, n * 3 + (3 * i - 1))
                    if not first or i >= 3:
                        dve.wait_ge(gr_ok, n + (i - 2))
                    dve.reciprocal(r_den[j % 2][:], den3[:]).then_inc(rden_ok, 1)
                if head:
                    dve.wait_ge(vg_read, n * 2 + 2 * (i + 1))
                    if not first or i >= 2:
                        dve.wait_ge(gr_ok, n + (i - 1))
                    dve.scalar_tensor_tensor(g_s[i % 2][:].rearrange("p h d -> p (h d)"),
                                             g_th[i % 2][:].rearrange("p h d -> p (h d)"), 1.0,
                                             bank[1][:, HD:HD + QW], ALU.add, ALU.mult).then_inc(gs_ok, 1)
                if tail2:
                    j = (i - 2) % NBLK
                    dve.wait_ge(pv_ok, n + (i - 1))
                    dve.wait_ge(gr_ok, n + (i - 1))
                    if not first or i >= 4:
                        dve.wait_ge(att_out[j % 2], n * 8 + 16 * ((i - 2) // 2))
                    dve.tensor_tensor(o_mix[j % 2][:], bank[7][:, :].rearrange("p (h d) -> p h d", d=P)[:, :, 0:HD],
                                      g_r[j % 2][:], ALU.mult).then_inc(omix_ok, 1)
                if tail1:
                    j = (i - 1) % NBLK
                    dve.wait_ge(pt_ok, n + i)
                    if not first or i >= 3:
                        dve.wait_ge(pv_ok, n + (i - 2))
                    dve.tensor_copy(pT[j % 2][:, 2:4, :, :].rearrange("p h a q -> p (h a q)"),
                                    bank[6][:, :]).then_inc(ptv_ok, 1)
                if head:
                    dve.wait_ge(t_ok, n + (i + 1))
                    if not first or i >= 2:
                        dve.wait_ge(s_ok, n + (i - 1))
                    dve.tensor_copy(qT[i % 2][:].rearrange("p a t -> p (a t)"), bank[4][:, 0:2 * P]).then_inc(tcopy_ok, 1)
                    dve.tensor_copy(kT[:, i + 1, :], bank[4][:, 2 * P:3 * P]).then_inc(tcopy_ok, 1)
                if head and i == NBLK - 1:
                    waits_alone(dve, (tcopy_ok, n * 2 + 2 * (i + 1)))
                    dve.tensor_copy(k_carry[:, bass.ds(g, 1), :].rearrange("p o t -> p (o t)"), kT[:, NBLK, :])
                    dve.tensor_copy(v_carry[:, bass.ds(g, 1), :].rearrange("p o t -> p (o t)"),
                                    vv[:, NBLK, :, :].rearrange("p a d -> p (a d)")).then_inc(carry_ok, 1)

            def rec_iter(s, h, j, head, tail, first, ht):
                n = s * (RHEADS * QUADS) + h * QUADS
                w = s * UNITS + h + GROUPS
                jt = (j - 1) % QUADS
                if head and j == 0:
                    split_lo(0, w, KT * 2 * RK)
                    if first:
                        split_lo(1, w, KT * 2 * RK)
                    else:
                        waits_alone(dve, (logf_ok, n))
                    dve.tensor_copy(par[:], head_par[:, bass.ds(h, 1), :].rearrange("p o c -> p (o c)")
                                    ).then_inc(par_ok, 1)
                if tail:
                    dve.wait_ge(nat_read, n * 4 + 4 * j)
                    if not first or j >= 2:
                        dve.wait_ge(rgw_ok, n + (j - 1))
                    for half in range(2):
                        nat = bank[2 + half][:, :].rearrange("p (b n) -> p b n", b=2)
                        dve.scalar_tensor_tensor(rg_s[:, 2 * half:2 * half + 2, :], rg_th[:, 2 * half:2 * half + 2, :],
                                                 1.0, nat[:, :, RK:2 * RK], ALU.add, ALU.mult).then_inc(rgs_ok, 1)
                if head:
                    if j == 0:
                        dve.wait_ge(par_ok, s * RHEADS + h + 1)
                    dve.wait_ge(fth_ok, n + (j + 1))
                    if not first or j >= 1:
                        dve.wait_ge(logf_ok, n + j)
                        dve.wait_ge(kout_ok, n + j)
                    dve.tensor_scalar(f_r[:], f_th[:], 1.0, par[:, 1:2], ALU.add, ALU.mult).then_inc(fr_ok, 1)
                    dve.tensor_scalar(k_f[:], f_th[:], par[:, 2:3], par[:, 1:2], ALU.mult, ALU.add).then_inc(kf_ok, 1)
                if tail:
                    waits = [(ak_ok, n + j)]
                    if not first or j >= 2:
                        waits.append((o_ok, n + (j - 1)))
                    waits_alone(dve, *waits)
                    for b in range(QB):
                        dve.copy_predicated(a_T[:, b, :], causal[:], bank[4][:, b * P:(b + 1) * P]).then_inc(at_ok, 1)
                if head and j == 0 and not first:
                    split_lo(1, w, KT * 2 * RK)
                if head:
                    dve.wait_ge(logf_ok, n + (j + 1))
                    if not first or j >= 1:
                        dve.wait_ge(enb_ok, n + j)
                        dve.wait_ge(rest_ok, n + j)
                    dve.tensor_tensor_scan(b_cum[:], chunk_keep[:], log_f[:], 0.0, ALU.mult, ALU.add).then_inc(bcum_ok, 1)
                if tail:
                    waits_alone(dve, (u_ok, n + j))
                    if jt == 0:
                        dve.tensor_copy(s_in[0][:, 0, :], state[:, bass.ds(ht, 1), :].rearrange("p o v -> p (o v)")
                                        ).then_inc(state_in, 1)
                        dve.wait_ge(state_in, s * RHEADS + ht + 1)
                    for c in range(NCH):
                        if c < NCH - 1:
                            dst = s_in[jt][:, c + 1, :]
                        elif jt < QUADS - 1:
                            dst = s_in[jt + 1][:, 0, :]
                        else:
                            dst = state[:, bass.ds(ht, 1), :].rearrange("p o v -> p (o v)")
                        if c >= 1 or jt >= 1:
                            dve.wait_ge(st_ok, n * NCH + (NCH * (j - 1) + c))
                        dve.scalar_tensor_tensor(dst, s_in[jt][:, c, :], e_b[jt][:, c * CH + CH - 1:c * CH + CH],
                                                 bank[6 - c % 2][:, (c // 2) * P:(c // 2 + 1) * P],
                                                 ALU.mult, ALU.add).then_inc(st_ok, 1)
                if head:
                    dve.wait_ge(eb_ok, n + (j + 1))
                    dve.wait_ge(rq_ok, n + (j + 1))
                    dve.tensor_tensor(q_dec[j % 2][:], bank[1][:, :], e_b[j % 2][:], ALU.mult).then_inc(qdec_ok, 1)
                if tail:
                    dve.wait_ge(orinv_ok, n * 2 + 2 * j)
                    dve.wait_ge(rgw_ok, n + j)
                    if not first or j >= 3:
                        dve.wait_ge(rec_out[jt], n * 8 + 16 * ((j - 1) // 2) + 16)
                    for b in range(QB):
                        dve.scalar_tensor_tensor(r_mix[jt][:, b, :], bank[7][:, b * P:(b + 1) * P], o_rinv[:, b:b + 1],
                                                 rg_w[:, b, :], ALU.mult, ALU.mult).then_inc(rmix_ok, 1)

            with dve.Fori(0, SEGS) as s:
                tv = s * 11
                dve.tensor_tensor(ang[:], pos_f[:, bass.ds(s * NBLK, NBLK)].unsqueeze(2).to_broadcast([P, NBLK, HD // 2]),
                                  freq[:].unsqueeze(1).to_broadcast([P, NBLK, HD // 2]), ALU.mult).then_inc(trig_v, 1)
                dve.wait_ge(trig_v, tv + 1)
                dve.tensor_scalar(turns[:], ang[:], float(1.0 / TWO_PI), ROUND, ALU.mult, ALU.add).then_inc(trig_v, 1)
                dve.wait_ge(trig_v, tv + 2)
                dve.tensor_scalar(turns[:], turns[:], ROUND, None, ALU.subtract).then_inc(trig_v, 1)
                for m, part in enumerate((PI_A, PI_B, PI_C)):
                    dve.wait_ge(trig_v, tv + (3 + m))
                    dve.scalar_tensor_tensor(ang[:].rearrange("p b f -> p (b f)"),
                                             turns[:].rearrange("p b f -> p (b f)"), -part,
                                             ang[:].rearrange("p b f -> p (b f)"), ALU.mult, ALU.add
                                             ).then_inc(trig_v, 1)
                dve.wait_ge(trig_v, tv + 6)
                dve.tensor_scalar(ang[:], ang[:], PI_MAX, -PI_MAX, ALU.min, ALU.max).then_inc(trig_v, 1)
                dve.wait_ge(trig_a, s * 3 + 3)
                HH = HD // 2
                for qk in range(2):
                    w1 = qk_wt[:, qk, 0:HH].unsqueeze(1).to_broadcast([P, NBLK, HH])
                    w2 = qk_wt[:, qk, HH:HD].unsqueeze(1).to_broadcast([P, NBLK, HH])
                    dve.tensor_tensor(rot[:, :, qk, 0, 0:HH], cosv[:], w1, ALU.mult)
                    dve.tensor_tensor(rot[:, :, qk, 0, HH:HD], cosv[:], w2, ALU.mult)
                    dve.scalar_tensor_tensor(rot[:, :, qk, 1, 0:HH], sinv[:], -1.0, w2, ALU.mult, ALU.mult)
                    dve.tensor_tensor(rot[:, :, qk, 1, HH:HD], sinv[:], w1, ALU.mult).then_inc(trig_v, 2)
                dve.tensor_copy(mask_first[:], masks[:, bass.ds(s, 1), :].rearrange("p o t -> p (o t)"))
                with dve.Fori(0, NBLK // 2) as bp:
                    for b in range(2):
                        n = s * NBLK + bp * 2 + b
                        dve.wait_ge(x_rs, n * 2 + 2)
                        dve.tensor_scalar(xn[b][:], xb[b][:], x_rinv[:, b:b + 1], None, ALU.mult).then_inc(x_nrm, 1)
                        tok = bass.ds(bp * (2 * P) + b * P, P)
                        dve.wait_ge(h_mod, n * 2 + 6)
                        dve.tensor_copy(h_hi[:, :, tok], h_f[b][:]).then_inc(h_split, 1)
                        dve.wait_ge(h_split, n * 2 + 5)
                        dve.tensor_tensor(h_lo[:, :, tok], h_f[b][:], h_hi[:, :, tok].bitcast(F32),
                                          ALU.subtract).then_inc(h_split, 1)
                phase_over(dve, seg_phase(s, 1))
                for i in range(NBLK):
                    att_iter(s, 0, i, True, i >= 1, i >= 2, True, 0)
                with dve.Fori(1, GROUPS) as g:
                    for i in range(NBLK):
                        att_iter(s, g, i, True, True, True, False, g - 1 if i == 0 else g)
                att_iter(s, GROUPS - 1, NBLK, False, True, True, False, GROUPS - 1)
                att_iter(s, GROUPS - 1, NBLK + 1, False, False, True, False, GROUPS - 1)
                phase_over(dve, seg_phase(s, 2))
                dve.memset(a_T[:], 0.0)
                for j in range(QUADS):
                    rec_iter(s, 0, j, True, j >= 1, True, 0)
                with dve.Fori(1, RHEADS) as h:
                    for j in range(QUADS):
                        rec_iter(s, h, j, True, True, False, h - 1 if j == 0 else h)
                rec_iter(s, RHEADS - 1, QUADS, False, True, False, RHEADS - 1)
                phase_over(dve, seg_phase(s, 3))

            def m_rest(n, b):
                for q in range(4):
                    dve.wait_ge(mhi_ok, n * 4 + (4 * b + q + 1))
                    dve.tensor_tensor(m_lo[b][:, 4 * q:4 * q + 4, :].rearrange("p f t -> p (f t)"), bank[q % 2][:, :],
                                      m_hi[b][:, 4 * q:4 * q + 4, :].rearrange("p f t -> p (f t)").bitcast(F32),
                                      ALU.subtract).then_inc(mlo_ok, 1)

            def finish_rows(n, b, first):
                dve.wait_ge(y_ok, n + (b + 1))
                dve.wait_ge(xo_in[b], n * 8 + 16)
                y_tmp = [m_y[:, 0:HALF], m_y[:, HALF:D]]
                if not (first and b == 0):
                    dve.wait_ge(yout_ok, n * 2 + 2 * b)
                for c in range(2):
                    dve.tensor_tensor(y_tmp[c], bank[4 + 2 * b + c][:, :], gate_bc[:, c * HALF:(c + 1) * HALF],
                                      ALU.mult).then_inc(ygate_ok, 1)
                for c in range(2):
                    dve.wait_ge(ygate_ok, n * 2 + (2 * b + c + 1))
                    dve.tensor_tensor(xo[b][:, c * HALF:(c + 1) * HALF], xo[b][:, c * HALF:(c + 1) * HALF], y_tmp[c],
                                      ALU.add).then_inc(yout_ok, 1)

            for f in range(FT):
                if f == 1:
                    m_rest(0, 0)
                dve.wait_ge(wohi_ok, f + 1)
                dve.tensor_tensor(wo_lo[:, f, :], wo_raw[:, f, :], wo_hi[:, f, :].bitcast(F32),
                                  ALU.subtract).then_inc(wolo_ok, 1)

            m_rest(0, 1)
            finish_rows(0, 0, True)
            m_rest(2, 0)
            finish_rows(0, 1, True)
            with dve.Fori(1, OUT_BLKS // 2 - 1) as bp:
                m_rest(bp * 2, 1)
                finish_rows(bp * 2, 0, False)
                m_rest(bp * 2 + 2, 0)
                finish_rows(bp * 2, 1, False)
            m_rest(OUT_BLKS - 2, 1)
            finish_rows(OUT_BLKS - 2, 0, False)
            finish_rows(OUT_BLKS - 2, 1, False)

        @block.gpsimd
        def _(pool):
            pool.memset(minus_half[:], -0.5)
            phase_over(pool, 1)

            def inverse_root(dst, var, ss, count, done, base):
                pool.tensor_scalar(var, ss, 1.0 / count, EPS, ALU.mult, ALU.add).then_inc(done, 1)
                pool.wait_ge(done, base + 1)
                pool.tensor_tensor(dst, var, minus_half[:, 0:ss.shape[1]], ALU.pow).then_inc(done, 1)

            def att_iter(s, g, i, head, tail1, first):
                n = s * (GROUPS * NBLK) + g * NBLK
                if head:
                    waits = [(ss_ok, n + (i + 1))]
                    if not first or i >= 1:
                        waits.append((qn_ok, n + i))
                    waits_alone(pool, *waits)
                    inverse_root(q_rinv[:], q_var[:], q_ss[:], HD, rinv_ok, n * 2 + 2 * i)
                    rotate(s, g, i, first)
                if tail1:
                    j = (i - 1) % NBLK
                    pool.wait_ge(rden_ok, n * 3 + 3 * i)
                    pool.wait_ge(gs_ok, n + i)
                    if not first or i >= 3:
                        pool.wait_ge(omix_ok, n + (i - 2))
                    pool.tensor_tensor(g_r[j % 2][:], g_s[j % 2][:],
                                       r_den[j % 2][:].unsqueeze(2).to_broadcast([P, GH, HD]),
                                       ALU.mult).then_inc(gr_ok, 1)

            def rotate(s, g, i, first):
                n = s * (GROUPS * NBLK) + g * NBLK
                H2 = HD // 2
                pool.wait_ge(qn_ok, n + (i + 1))
                if not first or i >= 1:
                    pool.wait_ge(rot_ok, n * 2 + 2 * i)
                x = qn[i % 2]
                cos_q = rot[:, i, 0, 0, :].unsqueeze(1).to_broadcast([P, GH, HD])
                pool.tensor_tensor(rc[:, 0:GH, :], x[:, 0:GH, :], cos_q, ALU.mult).then_inc(rot_parts, 1)
                pool.tensor_tensor(rc[:, GH, :], x[:, GH, :], rot[:, i, 1, 0, :], ALU.mult).then_inc(rot_parts, 1)
                for half in range(2):
                    own, other = slice(half * H2, half * H2 + H2), slice((1 - half) * H2, (1 - half) * H2 + H2)
                    sin_q = rot[:, i, 0, 1, own].unsqueeze(1).to_broadcast([P, GH, H2])
                    pool.tensor_tensor(rs[:, 0:GH, own], x[:, 0:GH, other], sin_q, ALU.mult).then_inc(rot_parts, 1)
                    pool.tensor_tensor(rs[:, GH, own], x[:, GH, other], rot[:, i, 1, 1, own],
                                       ALU.mult).then_inc(rot_parts, 1)
                pool.wait_ge(rot_parts, n * 6 + 6 * (i + 1))
                if not first or i >= 2:
                    pool.wait_ge(t_ok, n + (i - 1))
                pool.tensor_tensor(q_rot[i % 2][:], rc[:, 0:GH, :], rs[:, 0:GH, :], ALU.add).then_inc(rot_ok, 1)
                pool.tensor_tensor(k_rot[i % 2][:], rc[:, GH:GH + 1, :].to_broadcast([P, 2, HD]),
                                   rs[:, GH:GH + 1, :].to_broadcast([P, 2, HD]), ALU.add).then_inc(rot_ok, 1)

            def rec_iter(s, h, j, head, tail, first):
                n = s * (RHEADS * QUADS) + h * QUADS
                if tail:
                    pool.wait_ge(rgs_ok, n * 2 + 2 * j)
                    if not first or j >= 2:
                        pool.wait_ge(rmix_ok, n * QB + QB * (j - 1))
                    pool.tensor_tensor(rg_w[:], rg_s[:], rec_wt[:].unsqueeze(1).to_broadcast([P, QB, RK]),
                                       ALU.mult).then_inc(rgw_ok, 1)
                if head:
                    pool.wait_ge(bcum_ok, n + (j + 1))
                    if not first or j >= 1:
                        pool.wait_ge(kout_ok, n + j)
                    b3 = b_cum[:].rearrange("p (c t) -> p c t", t=CH)
                    pool.tensor_tensor(b_rest[:].rearrange("p (c t) -> p c t", t=CH),
                                       b3[:, :, CH - 1:CH].to_broadcast([P, NCH, CH]), b3, ALU.subtract).then_inc(rest_ok, 1)
                    if not first or j >= 2:
                        pool.wait_ge(ak_ok, n + (j - 1))
                    pool.wait_ge(enb_ok, n + (j + 1))
                    pool.wait_ge(kf_ok, n + (j + 1))
                    pool.tensor_tensor(k_inv[j % 2][:], k_f[:], e_nb[:], ALU.mult).then_inc(kinv_ok, 1)
                    pool.wait_ge(erest_ok, n + (j + 1))
                    pool.tensor_tensor(k_out[j % 2][:], k_f[:], b_rest[:], ALU.mult).then_inc(kout_ok, 1)
                if tail:
                    waits = [(oss_ok, n * QB + QB * j)]
                    if not first or j >= 2:
                        waits.append((rmix_ok, n * QB + QB * (j - 1)))
                    waits_alone(pool, *waits)
                    inverse_root(o_rinv[:], o_var[:], o_ss[:], RK, orinv_ok, n * 2 + 2 * (j - 1))

            with pool.Fori(0, SEGS) as s:
                with pool.Fori(0, NBLK // 2) as bp:
                    for b in range(2):
                        n = s * NBLK + bp * 2 + b
                        waits_alone(pool, (x_sqd, n + 2))
                        inverse_root(x_rinv[:, b:b + 1], x_var[:, b:b + 1], x_ss[:, b:b + 1], D, x_rs, n * 2)
                phase_over(pool, seg_phase(s, 1))
                for i in range(NBLK):
                    att_iter(s, 0, i, True, i >= 1, True)
                with pool.Fori(1, GROUPS) as g:
                    for i in range(NBLK):
                        att_iter(s, g, i, True, True, False)
                att_iter(s, GROUPS - 1, NBLK, False, True, False)
                phase_over(pool, seg_phase(s, 2))
                for j in range(QUADS):
                    rec_iter(s, 0, j, True, j >= 1, True)
                with pool.Fori(1, RHEADS) as h:
                    for j in range(QUADS):
                        rec_iter(s, h, j, True, True, False)
                rec_iter(s, RHEADS - 1, QUADS, False, True, False)
                phase_over(pool, seg_phase(s, 3))


def constants():
    q, k = np.arange(P)[:, None], np.arange(P)[None, :]
    prev = np.where(k > q, 0.0, NEG)
    own = np.where(k <= q, 0.0, NEG)
    first = np.concatenate([np.full((P, P), NEG), own], 1)
    later = np.concatenate([prev, own], 1)
    masks = np.stack([first] + [later] * (SEGS - 1), 1).astype(np.float32)
    s, t = np.arange(P)[:, None], np.arange(P)[None, :]
    causal = ((s <= t) & (s // CH == t // CH)).astype(np.int32)
    inv = (np.float32(10000.0) ** (-np.arange(0, HD, 2, dtype=np.float32) / np.float32(HD))).astype(np.float32)
    sign = np.tile(inv, (P, 1))
    return np.eye(P, dtype=np.float32), masks, causal, sign


def kernel(x, c, positions, norm_w, w_ada, b_ada, w_in, q_norm_w, k_norm_w, sinks, rec_norm_w, lower_bounds, w_out):
    import concourse.bacc as bacc
    from concourse.bass_utils import run_bass_kernel_spmd

    def cols(a, n):
        return np.ascontiguousarray(np.asarray(a).reshape(n, P).T)

    def rows(a):
        return np.ascontiguousarray(np.broadcast_to(np.asarray(a).reshape(1, -1), (P, np.asarray(a).size)))

    ident, masks, causal, freq = constants()
    b = np.asarray(b_ada)[0]
    arrays = {
        "x": np.asarray(x)[0], "cT": cols(c, KT), "pos": cols(positions, SEQ // P), "norm_w": cols(norm_w, KT),
        "w_ada": np.asarray(w_ada)[0], "b_cols": cols(b[:2 * D], 2 * KT), "b_gate": rows(b[2 * D:]),
        "w_in": np.asarray(w_in)[0],
        "qk_w": np.ascontiguousarray(np.stack([rows(q_norm_w), rows(k_norm_w)], 1)),
        "sinks": rows(sinks), "rec_w": rows(rec_norm_w),
        "lbT": np.ascontiguousarray(np.asarray(lower_bounds).reshape(2, RHEADS, P).transpose(2, 0, 1)),
        "w_out": np.asarray(w_out)[0],
        "ident_d": ident, "masks_d": masks, "causal_d": causal, "freq_d": freq,
    }
    arrays = {k: np.ascontiguousarray(a) for k, a in arrays.items()}
    nc = bacc.Bacc("TRN2", target_bir_lowering=False, num_devices=1)
    args = {k: nc.dram_tensor(f"in_{k}", a.shape, mybir.dt.from_np(a.dtype), kind="ExternalInput").ap()
            for k, a in arrays.items()}
    out = nc.dram_tensor("out_rows", (SEQ, D), F32, kind="ExternalOutput").ap()
    mixed = nc.dram_tensor("mixed_rows", (SEQ, MIX), F32, kind="Internal").ap()
    hybrid_layer(nc, out=out, mixed=mixed, **args)
    r = run_bass_kernel_spmd(nc, [{f"in_{k}": a for k, a in arrays.items()}], core_ids=[0])
    return r.results[0]["out_rows"].reshape(1, SEQ, D)
```

```python
from contextlib import ExitStack

import numpy as np

import concourse.bass as bass
from concourse import mybir

F32 = mybir.dt.float32
F32R = mybir.dt.float32r
I32 = mybir.dt.int32
ALU = mybir.AluOpType
ACT = mybir.ActivationFunctionType
AX_X = mybir.AxisListType.X

P = 128
D = 1024
KT = D // P
SEQ = 2048
SEGS = 2
SEG = SEQ // SEGS
NBLK = SEG // P
HEADS, GROUPS, HD = 16, 4, 64
GH = HEADS // GROUPS
QW = GH * HD
ATT = HEADS * HD
RHEADS, RK = 8, 128
QUAD = 512
QUADS = SEG // QUAD
QB = QUAD // P
CH = 64
NCH = QUAD // CH
OUT_BLKS = SEQ // P
UNITS = GROUPS + RHEADS
MIX = ATT + RHEADS * RK
FT = MIX // P
HALF = 512
MOD_T = 3 * D // HALF
WO_PARTS = 8
WO_F = FT // WO_PARTS
EPS = 1e-6
NEG = -1.0e30
COL_Q, COL_K, COL_V, COL_G = 0, ATT, ATT + GROUPS * HD, ATT + 2 * GROUPS * HD
COL_RQ = 2 * ATT + 2 * GROUPS * HD
COL_RF, COL_RI, COL_RG = COL_RQ + RHEADS * RK, COL_RQ + 2 * RHEADS * RK, COL_RQ + 3 * RHEADS * RK
REG = KT * (QW + HD)
TWO_PI = 2.0 * np.pi
PI_A = 6.28125
PI_B = float(np.float32(np.round((TWO_PI - PI_A) * 2.0 ** 21) / 2.0 ** 21))
PI_C = float(TWO_PI - PI_A - PI_B)
PI_MAX = 3.1415925
ROUND = 1.5 * 2.0 ** 23


def hybrid_layer(nc, x, cT, pos, norm_w, w_ada, b_cols, b_gate, w_in, qk_w, sinks, rec_w, lbT, w_out,
                 ident_d, masks_d, causal_d, freq_d, out, mixed):
    with ExitStack() as ctx:
        def sem(name):
            return ctx.enter_context(nc.semaphore(name))

        bank = [ctx.enter_context(nc.psum_tensor(f"bank{i}", [P, 512], F32)) for i in range(8)]

        def sbuf(where, name, shape, dt=F32):
            return where.enter_context(nc.sbuf_tensor(name, shape, dt))

        ident = sbuf(ctx, "ident", [P, P])
        gate_bc = sbuf(ctx, "gate_bc", [P, D])

        unsplit = ExitStack()
        h_f = sbuf(unsplit, "h_f", [P, KT, SEG])
        x_early = sbuf(unsplit, "x_early", [P, KT, SEG])
        wa = [h_f[:, t * KT // 2:(t + 1) * KT // 2, :].rearrange("p k (a n) -> p (k a) n", n=HALF) for t in range(2)]
        wa += [sbuf(unsplit, f"wa{t}", [P, KT, HALF])[:] for t in (2, 3)]
        unsplit.close()
        main = ExitStack()
        h_lo = sbuf(main, "h_lo", [P, KT, SEG], F32R)
        h_hi = sbuf(main, "h_hi", [P, KT, SEG], F32R)
        w_hi = [sbuf(main, f"w_hi{r}", [P, REG], F32R) for r in range(2)]
        w_lo = [sbuf(main, f"w_lo{r}", [P, REG], F32R) for r in range(2)]
        raw = [sbuf(main, f"raw{r}", [P, REG]) for r in range(2)]
        rot = sbuf(main, "rot", [P, NBLK, 2, 2, HD])
        masks = sbuf(main, "masks", [P, SEGS, 2 * P])
        mask_first = sbuf(main, "mask_first", [P, 2 * P])
        k_carry = sbuf(main, "k_carry", [P, GROUPS, 2, P])
        v_carry = sbuf(main, "v_carry", [P, GROUPS, HD])
        mod_a = sbuf(main, "mod_a", [P, KT])
        mod_b = sbuf(main, "mod_b", [P, KT])
        head_par = sbuf(main, "head_par", [P, RHEADS, 4])
        sink_bc = sbuf(main, "sink_bc", [P, HEADS])
        qk_wt = sbuf(main, "qk_wt", [P, 2, HD])
        rec_wt = sbuf(main, "rec_wt", [P, RK])
        minus_half = sbuf(main, "minus_half", [P, 8])
        half_pi = sbuf(main, "half_pi", [P, 1])
        freq = sbuf(main, "freq", [P, HD // 2])
        pos_f = sbuf(main, "pos_f", [P, SEQ // P])
        causal = sbuf(main, "causal", [P, P], I32)
        state = sbuf(main, "state", [P, RHEADS, RK])

        pre = ExitStack()
        wa += [sbuf(pre, f"wa{t}", [P, KT, HALF])[:] for t in (4, 5)]
        wa_sum = [sbuf(pre, f"wa_sum{i}", [P, HALF]) for i in range(2)]
        c_in = sbuf(pre, "c_in", [P, KT])
        c_th = sbuf(pre, "c_th", [P, KT])
        c_act = sbuf(pre, "c_act", [P, KT])
        c_bc = sbuf(pre, "c_bc", [P, KT, P])
        ones = sbuf(pre, "ones", [P, P])
        diag_junk = sbuf(pre, "diag_junk", [P, 4, P])
        mod_cols = sbuf(pre, "mod_cols", [P, 2 * KT])
        b_col = sbuf(pre, "b_col", [P, 2 * KT])
        b_gate_s = sbuf(pre, "b_gate_s", [P, D])
        norm_s = sbuf(pre, "norm_s", [P, KT])
        pos_i = sbuf(pre, "pos_i", [P, SEQ // P], I32)
        lb_in = sbuf(pre, "lb_in", [P, 2, RHEADS])
        lb_t = sbuf(pre, "lb_t", [P, 4, RHEADS])
        pre.close()

        att = ExitStack()
        xb = [sbuf(att, f"xb{i}", [P, D]) for i in range(2)]
        x_ss = sbuf(att, "x_ss", [P, 2])
        x_var = sbuf(att, "x_var", [P, 2])
        x_rinv = sbuf(att, "x_rinv", [P, 2])
        sq = sbuf(att, "sq", [P, GH + 1, HD])
        q_ss = sbuf(att, "q_ss", [P, GH + 1])
        q_var = sbuf(att, "q_var", [P, GH + 1])
        q_rinv = sbuf(att, "q_rinv", [P, GH + 1])
        qn = sbuf(att, "qn", [P, GH + 1, HD])
        rc = sbuf(att, "rc", [P, GH + 1, HD])
        rs = sbuf(att, "rs", [P, GH + 1, HD])
        q_rot = [sbuf(att, f"q_rot{i}", [P, GH, HD]) for i in range(2)]
        k_rot = [sbuf(att, f"k_rot{i}", [P, 2, HD]) for i in range(2)]
        qT_hi = [sbuf(att, f"qT_hi{i}", [P, 2, P], F32R) for i in range(2)]
        qT_lo = [sbuf(att, f"qT_lo{i}", [P, 2, P], F32R) for i in range(2)]
        kT_hi = sbuf(att, "kT_hi", [P, NBLK + 1, P], F32R)
        kT_lo = sbuf(att, "kT_lo", [P, NBLK + 1, P], F32R)
        vv = sbuf(att, "vv", [P, NBLK + 1, 2, HD])
        sm = [sbuf(att, f"sm{i}", [P, GH, 2 * P]) for i in range(2)]
        row_max = sbuf(att, "row_max", [P, GH])
        m_row = sbuf(att, "m_row", [P, GH])
        neg_m = [sbuf(att, f"neg_m{i}", [P, GH]) for i in range(2)]
        sink_d = [sbuf(att, f"sink_d{i}", [P, GH]) for i in range(2)]
        den = [sbuf(att, f"den{i}", [P, GH]) for i in range(2)]
        sink_e = [sbuf(att, f"sink_e{i}", [P, GH]) for i in range(2)]
        den2 = sbuf(att, "den2", [P, GH])
        den3 = sbuf(att, "den3", [P, GH])
        r_den = [sbuf(att, f"r_den{i}", [P, GH]) for i in range(2)]
        pT = [sbuf(att, f"pT{i}", [P, GH, 2, P]) for i in range(2)]
        ang, turns, cosv, sinv = [pT[1][:, q, :, :].rearrange("p a (c f) -> p (a c) f", f=HD // 2) for q in range(4)]
        g_s = [sbuf(att, f"g_s{i}", [P, GH, HD]) for i in range(2)]
        g_r = [sbuf(att, f"g_r{i}", [P, GH, HD]) for i in range(2)]
        o_mix = [sbuf(att, f"o_mix{i}", [P, GH, HD]) for i in range(2)]
        att.close()

        rec = ExitStack()
        par = sbuf(rec, "par", [P, 4])
        chunk_keep = sbuf(rec, "chunk_keep", [P, QUAD])
        f_th = sbuf(rec, "f_th", [P, QUAD])
        f_r = sbuf(rec, "f_r", [P, QUAD])
        k_f = sbuf(rec, "k_f", [P, QUAD])
        b_cum = sbuf(rec, "b_cum", [P, QUAD])
        e_b = [sbuf(rec, f"e_b{i}", [P, QUAD]) for i in range(2)]
        e_nb = sbuf(rec, "e_nb", [P, QUAD])
        b_rest = sbuf(rec, "b_rest", [P, QUAD])
        q_dec = [sbuf(rec, f"q_dec{i}", [P, QUAD]) for i in range(2)]
        k_inv = [sbuf(rec, f"k_inv{i}", [P, QUAD]) for i in range(2)]
        k_out = [sbuf(rec, f"k_out{i}", [P, QUAD]) for i in range(2)]
        k_nat = sbuf(rec, "k_nat", [P, QUAD])
        r_v = sbuf(rec, "r_v", [P, QB, RK])
        rg_th = sbuf(rec, "rg_th", [P, QB, RK])
        rg_s = sbuf(rec, "rg_s", [P, QB, RK])
        rg_w = sbuf(rec, "rg_w", [P, QB, RK])
        a_T = sbuf(rec, "a_T", [P, QB, P])
        s_in = [sbuf(rec, f"s_in{i}", [P, NCH, RK]) for i in range(2)]
        o_sq = sbuf(rec, "o_sq", [P, QB, RK])
        o_ss = sbuf(rec, "o_ss", [P, QB])
        o_var = sbuf(rec, "o_var", [P, QB])
        o_rinv = sbuf(rec, "o_rinv", [P, QB])
        r_mix = [sbuf(rec, f"r_mix{i}", [P, QB, RK]) for i in range(2)]
        rec.close()
        main.close()

        raw_rows = ExitStack()
        wo_raw = sbuf(raw_rows, "wo_raw", [P, FT, D])
        raw_rows.close()
        fin = ExitStack()
        wo_lo = sbuf(fin, "wo_lo", [P, FT, D], F32R)
        wo_hi = sbuf(fin, "wo_hi", [P, FT, D], F32R)
        m_raw = [sbuf(fin, f"m_raw{i}", [P, FT, P]) for i in range(2)]
        m_hi = [sbuf(fin, f"m_hi{i}", [P, FT, P], F32R) for i in range(2)]
        m_lo = [sbuf(fin, f"m_lo{i}", [P, FT, P], F32R) for i in range(2)]
        m_y = sbuf(fin, "m_y", [P, D])
        xo = [sbuf(fin, f"xo{i}", [P, D]) for i in range(2)]
        fin.close()

        phase_end = sem("phase_end")
        const_in = sem("const_in")
        const_ok = sem("const_ok")
        keep_ok = sem("keep_ok")
        wa_in = [sem(f"wa_in{t}") for t in range(MOD_T)]
        wa_sum_ok = sem("wa_sum_ok")
        mod_ok = sem("mod_ok")
        c_in_ok = sem("c_in_ok")
        c_tanh = sem("c_tanh")
        c_step = sem("c_step")
        c_ready = sem("c_ready")
        mod_used = sem("mod_used")
        pre_v = sem("pre_v")
        pre_e = sem("pre_e")
        x_in = [sem(f"x_in{i}") for i in range(2)]
        x_sqd = sem("x_sqd")
        x_rs = sem("x_rs")
        x_nrm = sem("x_nrm")
        x_T = sem("x_T")
        h_mod_a, h_mod_v = sem("h_mod_a"), sem("h_mod_v")
        h_round = sem("h_round")
        h_split = sem("h_split")
        trig_v = sem("trig_v")
        trig_a = sem("trig_a")
        raw_in = [sem(f"raw_in{r}") for r in range(2)]
        hi_ok = [sem(f"hi_ok{r}") for r in range(2)]
        lo_ok = [sem(f"lo_ok{r}") for r in range(2)]
        qk_ok, vg_ok = sem("qk_ok"), sem("vg_ok")
        sq_ok, ss_ok, rinv_ok, qn_ok = sem("sq_ok"), sem("ss_ok"), sem("rinv_ok"), sem("qn_ok")
        rot_parts, rot_ok = sem("rot_parts"), sem("rot_ok")
        t_ok, thi_ok, tcopy_ok = sem("t_ok"), sem("thi_ok"), sem("tcopy_ok")
        s_ok, masked_ok, max_ok, exp_ok = sem("s_ok"), sem("masked_ok"), sem("max_ok"), sem("exp_ok")
        rden_ok = sem("rden_ok")
        vg_read, gs_ok, gr_ok = sem("vg_read"), sem("gs_ok"), sem("gr_ok")
        pt_ok, pta_ok, ptv_ok = sem("pt_ok"), sem("pta_ok"), sem("ptv_ok")
        pv_ok, omix_ok = sem("pv_ok"), sem("omix_ok")
        att_out = [sem(f"att_out{i}") for i in range(2)]
        carry_ok = sem("carry_ok")
        rf_ok, rq_ok, nat_ok = sem("rf_ok"), sem("rq_ok"), sem("nat_ok")
        par_ok, fth_ok, fr_ok, kf_ok = sem("par_ok"), sem("fth_ok"), sem("fr_ok"), sem("kf_ok")
        logf_ok, bcum_ok, eb_ok, enb_ok = sem("logf_ok"), sem("bcum_ok"), sem("eb_ok"), sem("enb_ok")
        rest_ok, erest_ok = sem("rest_ok"), sem("erest_ok")
        qdec_ok, kinv_ok, kout_ok = sem("qdec_ok"), sem("kinv_ok"), sem("kout_ok")
        nat_read, rgs_ok, rgw_ok = sem("nat_read"), sem("rgs_ok"), sem("rgw_ok")
        ak_ok, at_ok, knat_ok = sem("ak_ok"), sem("at_ok"), sem("knat_ok")
        state_in = sem("state_in")
        u_ok, st_ok, o_ok = sem("u_ok"), sem("st_ok"), sem("o_ok")
        oss_ok, orinv_ok, rmix_ok = sem("oss_ok"), sem("orinv_ok"), sem("rmix_ok")
        rec_out = [sem(f"rec_out{i}") for i in range(2)]
        wo_in = [sem(f"wo_in{i}") for i in range(WO_PARTS)]
        wohi_ok, wolo_ok = sem("wohi_ok"), sem("wolo_ok")
        m_in = [sem(f"m_in{i}") for i in range(2)]
        xo_in = [sem(f"xo_in{i}") for i in range(2)]
        mt_ok, mhi_ok, mlo_ok = sem("mt_ok"), sem("mhi_ok"), sem("mlo_ok")
        y_ok, ygate_ok, yout_ok = sem("y_ok"), sem("ygate_ok"), sem("yout_ok")
        y_out = [sem(f"y_out{i}") for i in range(2)]

        x_b = x.rearrange("(b p) d -> b p d", p=P)
        out_b = out.rearrange("(b p) d -> b p d", p=P)
        mixed_b = mixed.rearrange("(b p) f -> b p f", p=P)
        wi = w_in.rearrange("(k p) n -> p k n", p=P)
        wad = w_ada.rearrange("(k p) n -> p k n", p=P)
        wo_d = w_out.rearrange("(f p) n -> p f n", p=P)

        def waits_alone(eng, *waits):
            values = [v if isinstance(v, int) else eng.to_reg(v) for _, v in waits]
            eng.wait_ge(const_in, 16)
            for (semaphore, _), v in zip(waits, values):
                eng.wait_ge(semaphore, v)

        def phase_over(eng, k):
            eng.drain().then_inc(phase_end, 1)
            waits_alone(eng, (phase_end, 5 * k))

        def seg_phase(s, j):
            return s * 2 + (1 + j)

        def tokens(m):
            return slice(m * P, (m + 1) * P)

        def x_rows(m):
            if m < 2:
                return x_early[:, :, tokens(NBLK - 1 - m)]
            return xb[m % 2][:].rearrange("p (k c) -> p k c", k=KT)

        def x_banks(m):
            return (bank[5], bank[6]) if m == 1 else (bank[2], bank[3])

        def region(t, width):
            return t[:, 0:KT * width].rearrange("p (k n) -> p k n", k=KT)

        block = ctx.enter_context(nc.Block())

        @block.sync
        def _(sp):
            def load(r, pieces):
                at = 0
                width = sum(n for _, n in pieces)
                dst = region(raw[r], width)
                for col, n in pieces:
                    sp.dma_start(dst[:, :, at:at + n], wi[:, :, bass.ds(col, n)]).then_inc(raw_in[r], 16)
                    at += n

            def load_att(g):
                load(0, [(g * QW + COL_Q, QW), (g * HD + COL_K, HD)])

            def load_att_b(g):
                load(1, [(g * HD + COL_V, HD), (g * QW + COL_G, QW)])

            def load_rec(h):
                load(0, [(h * RK + COL_RF, RK), (h * RK + COL_RQ, RK)])

            def load_rec_b(h):
                load(1, [(h * RK + COL_RI, RK), (h * RK + COL_RG, RK)])

            for j in range(QUADS):
                sp.sem_inc(rec_out[j], 16)
            def load_mod(t):
                sp.dma_start(wa[t], wad[:, :, t * HALF:(t + 1) * HALF]).then_inc(wa_in[t], 16)

            sp.dma_start(c_in[:], cT).then_inc(c_in_ok, 16)
            sp.dma_start(ident[:], ident_d).then_inc(c_in_ok, 16)
            load_mod(0)
            load_mod(1)
            for dst, src in ((masks[:], masks_d), (causal[:], causal_d), (freq[:], freq_d),
                             (pos_i[:], pos), (norm_s[:], norm_w), (b_col[:], b_cols),
                             (b_gate_s[:], b_gate), (qk_wt[:], qk_w), (sink_bc[:], sinks), (rec_wt[:], rec_w),
                             (lb_in[:], lbT)):
                sp.dma_start(dst, src).then_inc(const_in, 16)
            def load_x(s, m):
                sp.dma_start(x_rows(m), x_b[bass.ds(s * NBLK + m, 1)].rearrange("o p (k c) -> (o p) k c", k=KT)
                             ).then_inc(x_in[m % 2], 16)

            load_mod(2)
            load_mod(3)
            load_x(0, 0)
            load_x(0, 1)
            load_mod(4)
            load_mod(5)
            load_att(0)
            load_att_b(0)
            phase_over(sp, 1)

            def segment(s, last):
                def att_spill(g, i):
                    n = s * (GROUPS * NBLK) + g * NBLK
                    sp.wait_ge(omix_ok, n + (i + 1))
                    sp.dma_start(mixed_b[bass.ds(s * NBLK + i, 1), :, bass.ds(g * QW, QW)]
                                 .rearrange("o p f -> (o p) f"),
                                 o_mix[i % 2][:].rearrange("p h d -> p (h d)")).then_inc(att_out[i % 2], 16)

                def prefetch(w, load_a, load_b, arg):
                    for r, fn in ((0, load_a), (1, load_b)):
                        sp.wait_ge(lo_ok[r], w + 1)
                        fn(arg)

                for m in range(2, NBLK):
                    if m >= 4:
                        sp.wait_ge(x_T, s * NBLK + (m - 1))
                    load_x(s, m)
                    if m == 3:
                        prefetch(s * UNITS, load_att, load_att_b, 1)
                    if m >= 6:
                        att_spill(0, m - 6)
                for i in range(2, NBLK):
                    att_spill(0, i)
                with sp.Fori(1, GROUPS - 1) as g:
                    prefetch(s * UNITS + g, load_att, load_att_b, g + 1)
                    for i in range(NBLK):
                        att_spill(g, i)
                prefetch(s * UNITS + (GROUPS - 1), load_rec, load_rec_b, 0)
                for i in range(NBLK):
                    att_spill(GROUPS - 1, i)
                waits_alone(sp, *((att_out[i], (s + 1) * (16 * GROUPS * NBLK // 2)) for i in range(2)))
                phase_over(sp, seg_phase(s, 1))

                def rec_spill(h, j):
                    sp.wait_ge(rmix_ok, (s * (RHEADS * QUADS) + h * QUADS) * QB + (j + 1) * QB)
                    sp.dma_start(mixed_b[bass.ds(s * NBLK + j * QB, QB), :, bass.ds(h * RK + ATT, RK)]
                                 .rearrange("b p f -> p b f"), r_mix[j][:]).then_inc(rec_out[j], 16)

                with sp.Fori(0, RHEADS - 1) as h:
                    prefetch(s * UNITS + h + GROUPS, load_rec, load_rec_b, h + 1)
                    for j in range(QUADS):
                        rec_spill(h, j)
                if not last:
                    prefetch(s * UNITS + (UNITS - 1), load_att, load_att_b, 0)
                sp.wait_ge(nat_ok, (s + 1) * (RHEADS * QUADS))
                if not last:
                    load_x(s + 1, 0)
                    load_x(s + 1, 1)
                else:
                    load_mixed(0, 0)
                    for t in range(WO_PARTS):
                        fs = slice(t * WO_F, (t + 1) * WO_F)
                        sp.dma_start(wo_raw[:, fs, :], wo_d[:, fs, :]).then_inc(wo_in[t], 16)
                for j in range(QUADS):
                    rec_spill(RHEADS - 1, j)
                if not last:
                    waits_alone(sp, *((rec_out[j], (s + 1) * (16 * RHEADS) + 16) for j in range(QUADS)))
                phase_over(sp, seg_phase(s, 2))

            def load_mixed(m, b):
                sp.dma_start(m_raw[b][:].rearrange("p f t -> p (f t)"),
                             mixed_b[bass.ds(m, 1)].rearrange("o p f -> (o p) f")).then_inc(m_in[b], 16)

            def load_residual(m, b):
                sp.dma_start(xo[b][:], x_b[bass.ds(m, 1)].rearrange("o p d -> (o p) d")).then_inc(xo_in[b], 16)

            with sp.Fori(0, SEGS - 1) as s:
                segment(s, False)
            segment(SEGS - 1, True)

            load_mixed(1, 1)
            for b in range(2):
                load_residual(b, b)
            for j in range(QUADS):
                sp.wait_ge(rec_out[j], SEGS * 16 * RHEADS + 16)
            sp.wait_ge(mt_ok, 4)
            load_mixed(2, 0)

            def rows_out(n, b, ahead):
                if ahead >= 3:
                    sp.wait_ge(mt_ok, n * 4 + 4 * (b + 2))
                    load_mixed(n + (b + 3), 1 - b)
                sp.wait_ge(yout_ok, n * 2 + 2 * (b + 1))
                sp.dma_start(out_b[bass.ds(n + b, 1)].rearrange("o p d -> (o p) d"), xo[b][:]).then_inc(y_out[b], 16)
                if ahead >= 2:
                    sp.wait_ge(y_out[b], n * 8 + 16)
                    load_residual(n + (b + 2), b)

            with sp.Fori(0, OUT_BLKS // 2 - 2) as bp:
                for b in range(2):
                    rows_out(bp * 2, b, 3)
            for m in range(OUT_BLKS - 4, OUT_BLKS):
                rows_out(m - m % 2, m % 2, OUT_BLKS - 1 - m)
            for b in range(2):
                sp.wait_ge(y_out[b], 16 * (SEQ // P // 2))

        @block.tensor
        def _(pe):
            pe.wait_ge(c_ready, 1)
            for t in range(MOD_T):
                pe.wait_ge(wa_in[t], 16)
                if t >= 2:
                    pe.wait_ge(mod_used, t - 1)
                for k in range(KT // 2, KT):
                    pe.matmul(bank[t % 2][:, :], c_bc[:, k, :], wa[t][:, k, :], start=(k == KT // 2), stop=False)
                pe.wait_ge(wa_sum_ok, (KT // 2) * (t + 1))
                pe.matmul(bank[t % 2][:, :], ones[:], wa_sum[t % 2][:], start=False, stop=True).then_inc(mod_ok, 1)
            phase_over(pe, 1)

            def split_products(dst, pairs, first, last):
                mm = None
                for m, (a, b) in enumerate(pairs):
                    mm = pe.matmul(dst, a, b, start=(first and m == 0), stop=(last and m == 2))
                return mm

            def project_rows(dst, r, i, c0, c1, width, k):
                wh, wl = region(w_hi[r], width)[:, k, c0:c1], region(w_lo[r], width)[:, k, c0:c1]
                ah, al = h_hi[:, k, i * P:(i + 1) * P], h_lo[:, k, i * P:(i + 1) * P]
                return split_products(dst, ((ah, wh), (ah, wl), (al, wh)), k == 0, k == KT - 1)

            def project_cols(dst, c0, j, k):
                wh, wl = region(w_hi[0], 2 * RK)[:, k, c0:c0 + RK], region(w_lo[0], 2 * RK)[:, k, c0:c0 + RK]
                ah, al = h_hi[:, k, j * QUAD:(j + 1) * QUAD], h_lo[:, k, j * QUAD:(j + 1) * QUAD]
                return split_products(dst, ((wh, ah), (wl, ah), (wh, al)), k == 0, k == KT - 1)

            def weights_ready(r, w):
                pe.wait_ge(hi_ok[r], w + 1)
                pe.wait_ge(lo_ok[r], w + 1)

            def transpose_x(s, m):
                pe.wait_ge(x_nrm, s * NBLK + (m + 1))
                for k in range(KT):
                    mm = pe.transpose(x_banks(m)[k // 4][:, (k % 4) * P:(k % 4 + 1) * P],
                                      x_rows(m)[:, k, :], ident[:])
                mm.then_inc(x_T, 1)

            def x_banks_read(s, m):
                pe.wait_ge(h_mod_a, s * NBLK + (m + 1))
                pe.wait_ge(h_mod_v, s * NBLK + (m + 1))

            def att_iter(s, g, i, head, tail1, tail2, first):
                n = s * (GROUPS * NBLK) + g * NBLK
                w = s * UNITS + g
                steady = not first
                if head and first:
                    pe.wait_ge(h_split, s * NBLK + (i + 1))
                if head:
                    if i == 0:
                        weights_ready(0, w)
                    if steady or i >= 1:
                        pe.wait_ge(sq_ok, n + i)
                        pe.wait_ge(qn_ok, n + i)
                    for k in range(KT):
                        mm = project_rows(bank[0][:, 0:QW + HD], 0, i, 0, QW + HD, QW + HD, k)
                    mm.then_inc(qk_ok, 1)
                if tail1:
                    j = (i - 1) % NBLK
                    pe.wait_ge(tcopy_ok, n * 2 + 2 * i)
                    if first and i + 1 < NBLK:
                        x_banks_read(s, i + 1)
                    if steady or i >= 2:
                        pe.wait_ge(masked_ok, n * GH + GH * (i - 1))
                    for h in range(GH):
                        lo = HD * (h % 2)
                        qh, ql = qT_hi[j % 2][lo:lo + HD, h // 2, :], qT_lo[j % 2][lo:lo + HD, h // 2, :]
                        kh, kl = kT_hi[lo:lo + HD, j:j + 2, :], kT_lo[lo:lo + HD, j:j + 2, :]
                        mm = split_products(bank[2 + h % 2][:, (h // 2) * 2 * P:(h // 2 + 1) * 2 * P],
                                            ((qh, kh), (qh, kl), (ql, kh)), True, True)
                    mm.then_inc(s_ok, 1)
                if head:
                    if i == 0:
                        weights_ready(1, w)
                    if steady or i >= 1:
                        pe.wait_ge(vg_read, n * 2 + 2 * i)
                        pe.wait_ge(gs_ok, n + i)
                    for k in range(KT):
                        mm = project_rows(bank[1][:, 0:QW + HD], 1, i, 0, QW + HD, QW + HD, k)
                    mm.then_inc(vg_ok, 1)
                if tail2:
                    j = (i - 2) % NBLK
                    pe.wait_ge(pta_ok, n + (i - 1))
                    pe.wait_ge(ptv_ok, n + (i - 1))
                    if steady or i >= 3:
                        pe.wait_ge(omix_ok, n + (i - 2))
                    for h in range(GH):
                        for half in range(2):
                            mm = pe.matmul(bank[7][:, h * P:(h + 1) * P], pT[j % 2][:, h, half, :],
                                           vv[:, j + half, :, :].rearrange("p a d -> p (a d)"),
                                           start=(half == 0), stop=(half == 1))
                    mm.then_inc(pv_ok, 1)
                if tail1:
                    j = (i - 1) % NBLK
                    pe.wait_ge(exp_ok, n * (GH + 1) + (GH + 1) * i)
                    if steady or i >= 2:
                        pe.wait_ge(pta_ok, n + (i - 1))
                        pe.wait_ge(ptv_ok, n + (i - 1))
                    if first and i == 1:
                        x_banks_read(s, 1)
                    for h in range(GH):
                        for half in range(2):
                            at = ((h % 2) * 2 + half) * P
                            mm = pe.transpose(bank[5 + h // 2][:, at:at + P],
                                              sm[j % 2][:, h, half * P:(half + 1) * P], ident[:])
                    mm.then_inc(pt_ok, 1)
                if head and first and i + 2 < NBLK:
                    if i == 0:
                        x_banks_read(s, 0)
                    else:
                        pe.wait_ge(masked_ok, n * GH + GH * i)
                    transpose_x(s, i + 2)
                if head:
                    pe.wait_ge(rot_ok, n * 2 + (2 * i + 1))
                    if steady or i >= 1:
                        pe.wait_ge(tcopy_ok, n * 2 + 2 * i)
                    for h in range(2):
                        pe.transpose(bank[4][:, h * P:(h + 1) * P],
                                     q_rot[i % 2][:, 2 * h:2 * h + 2, :].rearrange("p a d -> p (a d)"), ident[:])
                    pe.wait_ge(rot_ok, n * 2 + (2 * i + 2))
                    pe.transpose(bank[4][:, 2 * P:3 * P], k_rot[i % 2][:].rearrange("p a d -> p (a d)"),
                                 ident[:]).then_inc(t_ok, 1)

            def rec_iter(s, h, j, head, tail, first):
                n = s * (RHEADS * QUADS) + h * QUADS
                w = s * UNITS + h + GROUPS
                steady = not first
                jt = (j - 1) % QUADS
                if head:
                    if j == 0:
                        weights_ready(0, w)
                    if steady or j >= 1:
                        pe.wait_ge(fth_ok, n + j)
                    for k in range(KT):
                        mm = project_cols(bank[0][:, :], 0, j, k)
                    mm.then_inc(rf_ok, 1)
                if tail:
                    pe.wait_ge(qdec_ok, n + j)
                    pe.wait_ge(kinv_ok, n + j)
                    pe.wait_ge(kout_ok, n + j)
                    if steady or j >= 2:
                        pe.wait_ge(at_ok, n * QB + QB * (j - 1))
                        pe.wait_ge(st_ok, n * NCH + NCH * (j - 1))
                    for b in range(QB):
                        pe.matmul(bank[4][:, b * P:(b + 1) * P], k_inv[jt][:, b * P:(b + 1) * P],
                                  q_dec[jt][:, b * P:(b + 1) * P], start=True, stop=True)
                    for b in range(QB):
                        mm = pe.transpose(bank[5][:, b * P:(b + 1) * P], k_out[jt][:, b * P:(b + 1) * P], ident[:])
                    mm.then_inc(ak_ok, 1)
                if head:
                    if steady or j >= 1:
                        pe.wait_ge(qdec_ok, n + j)
                    for k in range(KT):
                        mm = project_cols(bank[1][:, :], RK, j, k)
                    mm.then_inc(rq_ok, 1)
                if tail:
                    pe.wait_ge(knat_ok, n + j)
                    pe.wait_ge(nat_read, n * 4 + 4 * j)
                    for c in range(NCH):
                        lo, b = CH * (c % 2), c // 2
                        mm = pe.matmul(bank[6 - c % 2][:, b * P:(b + 1) * P], k_nat[lo:lo + CH, b * P:(b + 1) * P],
                                       r_v[lo:lo + CH, b, :], start=True, stop=True)
                    mm.then_inc(u_ok, 1)
                for half in range(2):
                    if head:
                        if half == 0:
                            if j == 0:
                                weights_ready(1, w)
                            if steady or j >= 1:
                                pe.wait_ge(nat_read, n * 4 + 4 * j)
                                pe.wait_ge(rgs_ok, n * 2 + 2 * j)
                        for b in range(2):
                            for k in range(KT):
                                mm = project_rows(bank[2 + half][:, b * 2 * RK:(b + 1) * 2 * RK], 1,
                                                  j * QB + half * 2 + b, 0, 2 * RK, 2 * RK, k)
                        if half == 1:
                            mm.then_inc(nat_ok, 1)
                    if tail and half == 0:
                        pe.wait_ge(at_ok, n * QB + QB * j)
                        pe.wait_ge(st_ok, n * NCH + NCH * j)
                        if steady or j >= 2:
                            pe.wait_ge(rmix_ok, n * QB + QB * (j - 1))
                        for b in range(QB):
                            dst = bank[7][:, b * P:(b + 1) * P]
                            pe.matmul(dst, a_T[:, b, :], r_v[:, b, :], start=True, stop=False,
                                      skip_group_check=True)
                            for c in range(2):
                                t0 = b * P + c * CH
                                mm = pe.matmul(bank[7][c * CH:(c + 1) * CH, b * P:(b + 1) * P],
                                               q_dec[jt][:, t0:t0 + CH], s_in[jt][:, 2 * b + c, :],
                                               start=False, stop=True, skip_group_check=True)
                        mm.then_inc(o_ok, 1)

            with pe.Fori(0, SEGS) as s:
                transpose_x(s, 0)
                transpose_x(s, 1)
                for i in range(NBLK):
                    att_iter(s, 0, i, True, i >= 1, i >= 2, True)
                with pe.Fori(1, GROUPS) as g:
                    for i in range(NBLK):
                        att_iter(s, g, i, True, True, True, False)
                att_iter(s, GROUPS - 1, NBLK, False, True, True, False)
                att_iter(s, GROUPS - 1, NBLK + 1, False, False, True, False)
                phase_over(pe, seg_phase(s, 1))
                for j in range(QUADS):
                    rec_iter(s, 0, j, True, j >= 1, True)
                with pe.Fori(1, RHEADS) as h:
                    for j in range(QUADS):
                        rec_iter(s, h, j, True, True, False)
                rec_iter(s, RHEADS - 1, QUADS, False, True, False)
                phase_over(pe, seg_phase(s, 2))

            def transposes(n, b, q):
                if q == 0:
                    pe.wait_ge(m_in[b], n * 8 + 16)
                if not isinstance(n, int) or n + b > 0 or q >= 2:
                    pe.wait_ge(mlo_ok, n * 4 + (4 * b + q - 1))
                for f in range(4):
                    mm = pe.transpose(bank[q % 2][:, f * P:(f + 1) * P], m_raw[b][:, q * 4 + f, :], ident[:])
                mm.then_inc(mt_ok, 1)

            def out_rows(n, b, first, last):
                pe.wait_ge(mlo_ok, n * 4 + 4 * (b + 1))
                if not first:
                    pe.wait_ge(ygate_ok, n * 2 + 2 * (b - 1))
                for f in range(FT):
                    if first and b == 0:
                        pe.wait_ge(wolo_ok, f + 1)
                    mh, ml = m_hi[b][:, f, :], m_lo[b][:, f, :]
                    for c in range(2):
                        wh, wl = wo_hi[:, f, c * HALF:(c + 1) * HALF], wo_lo[:, f, c * HALF:(c + 1) * HALF]
                        mm = split_products(bank[4 + 2 * b + c][:, :], ((mh, wh), (mh, wl), (ml, wh)), f == 0, f == FT - 1)
                    if not last and f % 4 == 2:
                        transposes(n + 2 * b, 1 - b, f // 4)
                mm.then_inc(y_ok, 1)

            for q in range(4):
                transposes(0, 0, q)
            out_rows(0, 0, True, False)
            out_rows(0, 1, True, False)
            with pe.Fori(1, OUT_BLKS // 2 - 1) as bp:
                out_rows(bp * 2, 0, False, False)
                out_rows(bp * 2, 1, False, False)
            out_rows(OUT_BLKS - 2, 0, False, False)
            out_rows(OUT_BLKS - 2, 1, False, True)

        @block.scalar
        def _(act):
            act.wait_ge(c_in_ok, 32)
            act.activation(c_th[:], c_in[:], ACT.Tanh, scale=0.5).then_inc(c_tanh, 1)
            act.wait_ge(pre_v, 2)
            act.activation(lb_t[:, 2:4, :], lb_t[:, 0:2, :], ACT.Exp).then_inc(pre_e, 1)
            phase_over(act, 1)

            def split_hi(r, w, size=REG):
                act.wait_ge(raw_in[r], w * 32 + 32)
                act.activation(w_hi[r][:, 0:size], raw[r][:, 0:size], ACT.Copy).then_inc(hi_ok[r], 1)

            def square_x(s, m):
                act.wait_ge(x_in[m % 2], (s * (NBLK // 2) + m // 2) * 16 + 16)
                act.activation(h_f[:, :, tokens(m)], x_rows(m),
                               ACT.Square, accum_out=x_ss[:, m % 2:m % 2 + 1]).then_inc(x_sqd, 1)

            def modulate_x(s, m):
                act.wait_ge(x_T, s * NBLK + (m + 1))
                for k in range(KT // 2):
                    a = act.activation(h_f[:, k, tokens(m)], x_banks(m)[0][:, k * P:(k + 1) * P],
                                       ACT.Identity, bias=mod_b[:, k:k + 1], scale=mod_a[:, k:k + 1])
                a.then_inc(h_mod_a, 1)
                act.wait_ge(h_mod_a, s * NBLK + (m + 1))
                act.wait_ge(h_mod_v, s * NBLK + (m + 1))
                act.activation(h_hi[:, :, tokens(m)], h_f[:, :, tokens(m)], ACT.Copy
                               ).then_inc(h_round, 1)

            def att_iter(s, g, i, head, tail1, tail2, first):
                n = s * (GROUPS * NBLK) + g * NBLK
                w = s * UNITS + g
                if head:
                    act.wait_ge(qk_ok, n + (i + 1))
                    if not first or i >= 1:
                        act.wait_ge(ss_ok, n + i)
                    act.activation(sq[:].rearrange("p h d -> p (h d)"), bank[0][:, 0:QW + HD],
                                   ACT.Square).then_inc(sq_ok, 1)
                if head and i == NBLK - 1:
                    split_hi(0, w + 1)
                if tail1:
                    j = (i - 1) % NBLK
                    act.wait_ge(max_ok, n * 3 + 3 * i)
                    if not first or i >= 3:
                        act.wait_ge(rden_ok, n * 3 + 3 * (i - 2))
                    for h in range(GH):
                        act.activation(sm[j % 2][:, h, :], sm[j % 2][:, h, :], ACT.Exp,
                                       bias=neg_m[j % 2][:, h:h + 1],
                                       accum_out=den[j % 2][:, h:h + 1]).then_inc(exp_ok, 1)
                    act.activation(sink_e[j % 2][:], sink_d[j % 2][:], ACT.Exp).then_inc(exp_ok, 1)
                if head:
                    act.wait_ge(vg_ok, n + (i + 1))
                    if not first or i >= 2:
                        act.wait_ge(gr_ok, n + (i - 1))
                    if i == 0 and not first:
                        act.wait_ge(carry_ok, s * GROUPS + g)
                    act.activation(vv[:, i + 1, :, :], bank[1][:, 0:HD].unsqueeze(1).to_broadcast([P, 2, HD]),
                                   ACT.Copy).then_inc(vg_read, 1)
                    act.activation(g_s[i % 2][:].rearrange("p h d -> p (h d)"), bank[1][:, HD:HD + QW],
                                   ACT.Tanh, scale=0.5).then_inc(vg_read, 1)
                if head and first and i + 3 < NBLK:
                    square_x(s, i + 3)
                if tail1:
                    j = (i - 1) % NBLK
                    act.wait_ge(pt_ok, n + i)
                    if not first or i >= 3:
                        act.wait_ge(pv_ok, n + (i - 2))
                    act.activation(pT[j % 2][:, 0:2, :, :].rearrange("p h a q -> p (h a q)"), bank[5][:, :],
                                   ACT.Copy).then_inc(pta_ok, 1)
                if head and first and i + 2 < NBLK:
                    modulate_x(s, i + 2)
                if head:
                    act.wait_ge(t_ok, n + (i + 1))
                    if not first or i >= 2:
                        act.wait_ge(s_ok, n + (i - 1))
                    act.activation(qT_hi[i % 2][:].rearrange("p a t -> p (a t)"), bank[4][:, 0:2 * P],
                                   ACT.Copy).then_inc(thi_ok, 1)
                    act.activation(kT_hi[:, i + 1, :], bank[4][:, 2 * P:3 * P], ACT.Copy).then_inc(thi_ok, 1)
                if head and i == NBLK - 1:
                    split_hi(1, w + 1)

            def rec_iter(s, h, j, head, tail, first):
                n = s * (RHEADS * QUADS) + h * QUADS
                w = s * UNITS + h + GROUPS
                jt = (j - 1) % QUADS
                if head and j == 0 and not first:
                    act.wait_ge(rq_ok, n)
                    split_hi(0, w, KT * 2 * RK)
                if tail:
                    act.wait_ge(nat_ok, n + j)
                    if not first or j >= 2:
                        act.wait_ge(o_ok, n + (j - 1))
                        act.wait_ge(rgs_ok, n * 2 + 2 * (j - 1))
                    for half in range(2):
                        nat = bank[2 + half][:, :].rearrange("p (b n) -> p b n", b=2)
                        act.activation(r_v[:, 2 * half:2 * half + 2, :], nat[:, :, 0:RK],
                                       ACT.Copy).then_inc(nat_read, 1)
                        act.activation(rg_s[:, 2 * half:2 * half + 2, :], nat[:, :, RK:2 * RK],
                                       ACT.Tanh, scale=0.5).then_inc(nat_read, 1)
                if head:
                    act.wait_ge(rf_ok, n + (j + 1))
                    if not first or j >= 1:
                        act.wait_ge(kf_ok, n + j)
                    act.activation(f_th[:], bank[0][:, :], ACT.Tanh, scale=0.5).then_inc(fth_ok, 1)
                if tail:
                    act.wait_ge(ak_ok, n + j)
                    act.activation(k_nat[:], bank[5][:, :], ACT.Copy).then_inc(knat_ok, 1)
                if head and j == 0 and not first:
                    act.wait_ge(nat_ok, n)
                    split_hi(1, w, KT * 2 * RK)
                if head:
                    act.wait_ge(fr_ok, n + (j + 1))
                    act.activation(f_r[:], f_r[:], ACT.Ln, bias=par[:, 0:1]).then_inc(logf_ok, 1)
                    act.wait_ge(bcum_ok, n + (j + 1))
                    if not first or j >= 2:
                        act.wait_ge(st_ok, n * NCH + NCH * (j - 1))
                    act.activation(e_b[j % 2][:], b_cum[:], ACT.Exp).then_inc(eb_ok, 1)
                    if not first or j >= 1:
                        act.wait_ge(kinv_ok, n + j)
                    act.activation(e_nb[:], b_cum[:], ACT.Exp, scale=-1.0).then_inc(enb_ok, 1)
                    act.wait_ge(rest_ok, n + (j + 1))
                    act.activation(b_rest[:], b_rest[:], ACT.Exp).then_inc(erest_ok, 1)
                if tail:
                    act.wait_ge(o_ok, n + j)
                    if not first or j >= 2:
                        act.wait_ge(orinv_ok, n * 2 + 2 * (j - 1))
                    for b in range(QB):
                        act.activation(o_sq[:, b, :], bank[7][:, b * P:(b + 1) * P], ACT.Square,
                                       accum_out=o_ss[:, b:b + 1]).then_inc(oss_ok, 1)

            with act.Fori(0, SEGS) as s:
                square_x(s, 0)
                square_x(s, 1)
                split_hi(0, s * UNITS, REG)
                modulate_x(s, 0)
                modulate_x(s, 1)
                split_hi(1, s * UNITS, REG)
                square_x(s, 2)
                act.wait_ge(trig_v, s * 11 + 7)
                act.activation(sinv[:].rearrange("p b f -> p (b f)"), ang[:].rearrange("p b f -> p (b f)"),
                               ACT.Sin).then_inc(trig_a, 1)
                act.activation(turns[:].rearrange("p b f -> p (b f)"), ang[:].rearrange("p b f -> p (b f)"),
                               ACT.Abs).then_inc(trig_a, 1)
                act.wait_ge(trig_a, s * 3 + 2)
                act.activation(cosv[:].rearrange("p b f -> p (b f)"), turns[:].rearrange("p b f -> p (b f)"),
                               ACT.Sin, bias=half_pi[:, 0:1], scale=-1.0).then_inc(trig_a, 1)
                for i in range(NBLK):
                    att_iter(s, 0, i, True, i >= 1, i >= 2, True)
                with act.Fori(1, GROUPS) as g:
                    for i in range(NBLK):
                        att_iter(s, g, i, True, True, True, False)
                att_iter(s, GROUPS - 1, NBLK, False, True, True, False)
                phase_over(act, seg_phase(s, 1))
                for j in range(QUADS):
                    rec_iter(s, 0, j, True, j >= 1, True)
                with act.Fori(1, RHEADS) as h:
                    for j in range(QUADS):
                        rec_iter(s, h, j, True, True, False)
                rec_iter(s, RHEADS - 1, QUADS, False, True, False)
                phase_over(act, seg_phase(s, 2))

            def m_rounded(n, b, first):
                for q in range(4):
                    act.wait_ge(mt_ok, n * 4 + (4 * b + q + 1))
                    if not first:
                        act.wait_ge(y_ok, n + (b - 1))
                    act.activation(m_hi[b][:, 4 * q:4 * q + 4, :].rearrange("p f t -> p (f t)"), bank[q % 2][:, :],
                                   ACT.Copy).then_inc(mhi_ok, 1)

            for f in range(FT):
                if f == 1:
                    m_rounded(0, 0, True)
                if f % WO_F == 0:
                    act.wait_ge(wo_in[f // WO_F], 16)
                act.activation(wo_hi[:, f, :], wo_raw[:, f, :], ACT.Copy).then_inc(wohi_ok, 1)

            m_rounded(0, 1, True)
            with act.Fori(1, OUT_BLKS // 2) as bp:
                for b in range(2):
                    m_rounded(bp * 2, b, False)

        @block.vector
        def _(dve):
            for t, v in ((ones, 1.0), (half_pi, float(np.pi / 2)), (state, 0.0), (k_carry, 0.0), (v_carry, 0.0)):
                dve.memset(t[:], v).then_inc(const_ok, 1)
            dve.wait_ge(const_ok, 5)
            dve.wait_ge(c_in_ok, 32)
            dve.wait_ge(c_tanh, 1)
            dve.scalar_tensor_tensor(c_act[:], c_th[:], 1.0, c_in[:], ALU.add, ALU.mult).then_inc(c_step, 1)
            dve.wait_ge(c_step, 1)
            dve.tensor_scalar(c_act[:], c_act[:], 0.5, None, ALU.mult).then_inc(c_step, 1)
            dve.wait_ge(c_step, 2)
            for k in range(KT // 2, KT):
                a = dve.tensor_scalar(c_bc[:, k, :], ones[:], c_act[:, k:k + 1], None, ALU.mult)
            a.then_inc(c_ready, 1)

            def mod_sum(t):
                dve.wait_ge(wa_in[t], 16)
                if t >= 2:
                    dve.wait_ge(mod_ok, t - 1)
                total = wa_sum[t % 2][:]
                dve.tensor_scalar(total, wa[t][:, 0, :], c_act[:, 0:1], None, ALU.mult).then_inc(wa_sum_ok, 1)
                for k in range(1, KT // 2):
                    dve.wait_ge(wa_sum_ok, (KT // 2) * t + k)
                    dve.scalar_tensor_tensor(total, wa[t][:, k, :], c_act[:, k:k + 1], total,
                                             ALU.mult, ALU.add).then_inc(wa_sum_ok, 1)

            def mod_read(t):
                dve.wait_ge(mod_ok, t + 1)
                if t < 4:
                    if t >= 1:
                        dve.wait_ge(mod_used, t)
                    for q in range(4):
                        a = dve.tensor_tensor_reduce(diag_junk[:, q, :], bank[t % 2][:, q * P:(q + 1) * P], ident[:],
                                                     1.0, 0.0, ALU.mult, ALU.add, mod_cols[:, 4 * t + q:4 * t + q + 1])
                else:
                    g0 = (t - 4) * HALF
                    a = dve.tensor_tensor(gate_bc[:, g0:g0 + HALF], bank[t % 2][:, :], b_gate_s[:, g0:g0 + HALF], ALU.add)
                a.then_inc(mod_used, 1)

            mod_sum(0)
            mod_sum(1)
            mod_read(0)
            dve.wait_ge(const_in, 16 * 11)
            dve.tensor_tensor(lb_t[:, 2, :], lb_in[:, 0, :], lb_in[:, 1, :], ALU.max).then_inc(pre_v, 1)
            dve.wait_ge(pre_v, 1)
            dve.tensor_tensor(lb_t[:, 0:2, :], lb_in[:], lb_t[:, 2:3, :].to_broadcast([P, 2, RHEADS]),
                              ALU.subtract).then_inc(pre_v, 1)
            dve.tensor_copy(pos_f[:], pos_i[:]).then_inc(pre_v, 1)
            dve.wait_ge(pre_e, 1)
            dve.tensor_tensor(lb_t[:, 0, :], lb_t[:, 2, :], lb_t[:, 3, :], ALU.add).then_inc(pre_v, 1)
            dve.wait_ge(pre_v, 4)
            dve.reciprocal(lb_t[:, 1, :], lb_t[:, 0, :]).then_inc(pre_v, 1)
            dve.wait_ge(pre_v, 5)
            dve.tensor_tensor(head_par[:, :, 0], lb_t[:, 2, :], lb_t[:, 1, :], ALU.mult).then_inc(pre_v, 1)
            dve.wait_ge(pre_v, 6)
            dve.tensor_scalar(head_par[:, :, 1], head_par[:, :, 0], -0.5, 0.5, ALU.mult, ALU.add).then_inc(pre_v, 1)
            dve.tensor_scalar(head_par[:, :, 2], head_par[:, :, 0], 0.5, -0.5, ALU.mult, ALU.add).then_inc(pre_v, 1)
            dve.memset(head_par[:, :, 3], 0.0).then_inc(pre_v, 1)
            dve.tensor_scalar(qk_wt[:, 0, :], qk_wt[:, 0, :], float(HD) ** -0.5, None, ALU.mult).then_inc(pre_v, 1)
            dve.tensor_scalar(rec_wt[:], rec_wt[:], 0.5, None, ALU.mult).then_inc(pre_v, 1)
            for t in range(2, MOD_T):
                mod_sum(t)
                mod_read(t - 1)
                if t == 4:
                    dve.wait_ge(mod_used, 4)
                    dve.tensor_tensor(mod_b[:], mod_cols[:, 0:KT], b_col[:, 0:KT], ALU.add).then_inc(pre_v, 1)
                    dve.tensor_tensor(mod_a[:], mod_cols[:, KT:2 * KT], b_col[:, KT:2 * KT], ALU.add).then_inc(pre_v, 1)
                    dve.wait_ge(pre_v, 13)
                    dve.scalar_tensor_tensor(mod_a[:], mod_a[:], 1.0, norm_s[:], ALU.add, ALU.mult).then_inc(pre_v, 1)
            mod_read(MOD_T - 1)
            phase_over(dve, 1)

            def split_lo(r, w, size=REG):
                dve.wait_ge(hi_ok[r], w + 1)
                dve.tensor_tensor(w_lo[r][:, 0:size], raw[r][:, 0:size], w_hi[r][:, 0:size].bitcast(F32),
                                  ALU.subtract).then_inc(lo_ok[r], 1)

            def normalize_x(s, m):
                b = m % 2
                dve.wait_ge(x_rs, (s * NBLK + m) * 2 + 2)
                dve.tensor_scalar(x_rows(m), x_rows(m), x_rinv[:, b:b + 1], None, ALU.mult).then_inc(x_nrm, 1)

            def modulate_x(s, m):
                dve.wait_ge(x_T, s * NBLK + (m + 1))
                for k in range(KT // 2, KT):
                    at = (k - KT // 2) * P
                    a = dve.tensor_scalar(h_f[:, k, tokens(m)], x_banks(m)[1][:, at:at + P],
                                          mod_a[:, k:k + 1], mod_b[:, k:k + 1], ALU.mult, ALU.add)
                a.then_inc(h_mod_v, 1)

            def rest_x(s, m):
                dve.wait_ge(h_round, s * NBLK + (m + 1))
                dve.tensor_tensor(h_lo[:, :, tokens(m)], h_f[:, :, tokens(m)], h_hi[:, :, tokens(m)].bitcast(F32),
                                  ALU.subtract).then_inc(h_split, 1)

            def att_iter(s, g, i, head, tail1, tail2, first, gt):
                n = s * (GROUPS * NBLK) + g * NBLK
                w = s * UNITS + g
                if head and first and 1 <= i and i + 2 < NBLK:
                    normalize_x(s, i + 2)
                if head and i == 0:
                    kept = k_carry[:, bass.ds(g, 1), :, :]
                    dve.tensor_copy(kT_hi[:, 0:1, :], kept[:, :, 0, :])
                    dve.tensor_copy(kT_lo[:, 0:1, :], kept[:, :, 1, :])
                    dve.tensor_copy(vv[:, 0, :, :], v_carry[:, bass.ds(g, 1), :].to_broadcast([P, 2, HD]))
                if head:
                    dve.wait_ge(sq_ok, n + (i + 1))
                    dve.reduce_sum(q_ss[:], sq[:], AX_X).then_inc(ss_ok, 1)
                if tail1:
                    j = (i - 1) % NBLK
                    waits = [(s_ok, n + i)]
                    if not first or i >= 2:
                        waits.append((max_ok, n * 3 + 3 * (i - 1)))
                    if not first or i >= 3:
                        waits.append((pt_ok, n + (i - 2)))
                    waits_alone(dve, *waits)
                    mask = mask_first[:] if j == 0 else masks[:, SEGS - 1, :]
                    for h in range(GH):
                        dve.tensor_tensor_reduce(sm[j % 2][:, h, :],
                                                 bank[2 + h % 2][:, (h // 2) * 2 * P:(h // 2 + 1) * 2 * P],
                                                 mask, 1.0, NEG, ALU.add, ALU.max,
                                                 row_max[:, h:h + 1]).then_inc(masked_ok, 1)
                if head:
                    dve.wait_ge(rinv_ok, n * 2 + 2 * (i + 1))
                    if not first or i >= 1:
                        dve.wait_ge(rot_ok, n * 2 + 2 * i)
                    dve.tensor_tensor(qn[:], bank[0][:, 0:QW + HD].rearrange("p (h d) -> p h d", d=HD),
                                      q_rinv[:].unsqueeze(2).to_broadcast([P, GH + 1, HD]),
                                      ALU.mult).then_inc(qn_ok, 1)
                if tail1:
                    dve.wait_ge(masked_ok, n * GH + GH * i)
                    sink = sink_bc[:, bass.ds(gt * GH, GH)]
                    dve.tensor_tensor(m_row[:], row_max[:], sink, ALU.max).then_inc(max_ok, 1)
                    dve.wait_ge(max_ok, n * 3 + (3 * i - 2))
                    dve.tensor_scalar(neg_m[j % 2][:], m_row[:], -1.0, None, ALU.mult).then_inc(max_ok, 1)
                    dve.tensor_tensor(sink_d[j % 2][:], sink, m_row[:], ALU.subtract).then_inc(max_ok, 1)
                if head and i == NBLK - 1:
                    split_lo(0, w + 1)
                if tail1:
                    j = (i - 1) % NBLK
                    dve.wait_ge(exp_ok, n * (GH + 1) + (GH + 1) * i)
                    dve.tensor_tensor(den2[:], den[j % 2][:], sink_e[j % 2][:], ALU.add).then_inc(rden_ok, 1)
                    dve.wait_ge(rden_ok, n * 3 + (3 * i - 2))
                    dve.tensor_scalar(den3[:], den2[:], 2.0, None, ALU.mult).then_inc(rden_ok, 1)
                    dve.wait_ge(rden_ok, n * 3 + (3 * i - 1))
                    if not first or i >= 3:
                        dve.wait_ge(gr_ok, n + (i - 2))
                    dve.reciprocal(r_den[j % 2][:], den3[:]).then_inc(rden_ok, 1)
                if head:
                    dve.wait_ge(vg_read, n * 2 + 2 * (i + 1))
                    if not first or i >= 2:
                        dve.wait_ge(gr_ok, n + (i - 1))
                    dve.scalar_tensor_tensor(g_s[i % 2][:].rearrange("p h d -> p (h d)"),
                                             g_s[i % 2][:].rearrange("p h d -> p (h d)"), 1.0,
                                             bank[1][:, HD:HD + QW], ALU.add, ALU.mult).then_inc(gs_ok, 1)
                if tail2:
                    j = (i - 2) % NBLK
                    dve.wait_ge(pv_ok, n + (i - 1))
                    dve.wait_ge(gr_ok, n + (i - 1))
                    if not first or i >= 4:
                        dve.wait_ge(att_out[j % 2], n * 8 + 16 * ((i - 2) // 2))
                    dve.tensor_tensor(o_mix[j % 2][:], bank[7][:, :].rearrange("p (h d) -> p h d", d=P)[:, :, 0:HD],
                                      g_r[j % 2][:], ALU.mult).then_inc(omix_ok, 1)
                if tail1:
                    j = (i - 1) % NBLK
                    dve.wait_ge(pt_ok, n + i)
                    if not first or i >= 3:
                        dve.wait_ge(pv_ok, n + (i - 2))
                    dve.tensor_copy(pT[j % 2][:, 2:4, :, :].rearrange("p h a q -> p (h a q)"),
                                    bank[6][:, :]).then_inc(ptv_ok, 1)
                if head and first and i + 2 < NBLK:
                    modulate_x(s, i + 2)
                if head:
                    dve.wait_ge(thi_ok, n * 2 + 2 * (i + 1))
                    dve.tensor_tensor(qT_lo[i % 2][:].rearrange("p a t -> p (a t)"), bank[4][:, 0:2 * P],
                                      qT_hi[i % 2][:].rearrange("p a t -> p (a t)").bitcast(F32),
                                      ALU.subtract).then_inc(tcopy_ok, 1)
                    dve.tensor_tensor(kT_lo[:, i + 1, :], bank[4][:, 2 * P:3 * P], kT_hi[:, i + 1, :].bitcast(F32),
                                      ALU.subtract).then_inc(tcopy_ok, 1)
                if head and first and i + 2 < NBLK:
                    rest_x(s, i + 2)
                if head and i == NBLK - 1:
                    split_lo(1, w + 1)
                    waits_alone(dve, (tcopy_ok, n * 2 + 2 * (i + 1)))
                    kept = k_carry[:, bass.ds(g, 1), :, :]
                    dve.tensor_copy(kept[:, :, 0, :], kT_hi[:, NBLK:NBLK + 1, :].bitcast(F32))
                    dve.tensor_copy(kept[:, :, 1, :], kT_lo[:, NBLK:NBLK + 1, :].bitcast(F32))
                    dve.tensor_copy(v_carry[:, bass.ds(g, 1), :], vv[:, NBLK, 0:1, :]).then_inc(carry_ok, 1)

            def rec_iter(s, h, j, head, tail, first, ht):
                n = s * (RHEADS * QUADS) + h * QUADS
                w = s * UNITS + h + GROUPS
                jt = (j - 1) % QUADS
                if head and j == 0:
                    if not first:
                        split_lo(0, w, KT * 2 * RK)
                        waits_alone(dve, (logf_ok, n))
                    dve.tensor_copy(par[:], head_par[:, bass.ds(h, 1), :].rearrange("p o c -> p (o c)")
                                    ).then_inc(par_ok, 1)
                if tail:
                    dve.wait_ge(nat_read, n * 4 + 4 * j)
                    if not first or j >= 2:
                        dve.wait_ge(rgw_ok, n + (j - 1))
                    for half in range(2):
                        nat = bank[2 + half][:, :].rearrange("p (b n) -> p b n", b=2)
                        dve.scalar_tensor_tensor(rg_s[:, 2 * half:2 * half + 2, :], rg_s[:, 2 * half:2 * half + 2, :],
                                                 1.0, nat[:, :, RK:2 * RK], ALU.add, ALU.mult).then_inc(rgs_ok, 1)
                if head:
                    if j == 0:
                        dve.wait_ge(par_ok, s * RHEADS + h + 1)
                    dve.wait_ge(fth_ok, n + (j + 1))
                    if not first or j >= 1:
                        dve.wait_ge(bcum_ok, n + j)
                        dve.wait_ge(kout_ok, n + j)
                    dve.tensor_scalar(f_r[:], f_th[:], 1.0, par[:, 1:2], ALU.add, ALU.mult).then_inc(fr_ok, 1)
                    dve.tensor_scalar(k_f[:], f_th[:], par[:, 2:3], par[:, 1:2], ALU.mult, ALU.add).then_inc(kf_ok, 1)
                if tail:
                    waits = [(ak_ok, n + j)]
                    if not first or j >= 2:
                        waits.append((o_ok, n + (j - 1)))
                    waits_alone(dve, *waits)
                    for b in range(QB):
                        dve.copy_predicated(a_T[:, b, :], causal[:], bank[4][:, b * P:(b + 1) * P]).then_inc(at_ok, 1)
                if head and j == 0 and not first:
                    split_lo(1, w, KT * 2 * RK)
                if head:
                    dve.wait_ge(logf_ok, n + (j + 1))
                    if not first or j >= 1:
                        dve.wait_ge(enb_ok, n + j)
                        dve.wait_ge(rest_ok, n + j)
                    dve.tensor_tensor_scan(b_cum[:], chunk_keep[:], f_r[:], 0.0, ALU.mult, ALU.add).then_inc(bcum_ok, 1)
                if tail:
                    waits_alone(dve, (u_ok, n + j))
                    if jt == 0:
                        dve.tensor_copy(s_in[0][:, 0, :], state[:, bass.ds(ht, 1), :].rearrange("p o v -> p (o v)")
                                        ).then_inc(state_in, 1)
                        dve.wait_ge(state_in, s * RHEADS + ht + 1)
                    for c in range(NCH):
                        if c < NCH - 1:
                            dst = s_in[jt][:, c + 1, :]
                        elif jt < QUADS - 1:
                            dst = s_in[jt + 1][:, 0, :]
                        else:
                            dst = state[:, bass.ds(ht, 1), :].rearrange("p o v -> p (o v)")
                        if c >= 1 or jt >= 1:
                            dve.wait_ge(st_ok, n * NCH + (NCH * (j - 1) + c))
                        dve.scalar_tensor_tensor(dst, s_in[jt][:, c, :], e_b[jt][:, c * CH + CH - 1:c * CH + CH],
                                                 bank[6 - c % 2][:, (c // 2) * P:(c // 2 + 1) * P],
                                                 ALU.mult, ALU.add).then_inc(st_ok, 1)
                if head:
                    dve.wait_ge(eb_ok, n + (j + 1))
                    dve.wait_ge(rq_ok, n + (j + 1))
                    dve.tensor_tensor(q_dec[j % 2][:], bank[1][:, :], e_b[j % 2][:], ALU.mult).then_inc(qdec_ok, 1)
                if tail:
                    dve.wait_ge(orinv_ok, n * 2 + 2 * j)
                    dve.wait_ge(rgw_ok, n + j)
                    if not first or j >= 3:
                        dve.wait_ge(rec_out[jt], n * 8 + 16 * ((j - 1) // 2) + 16)
                    for b in range(QB):
                        dve.scalar_tensor_tensor(r_mix[jt][:, b, :], bank[7][:, b * P:(b + 1) * P], o_rinv[:, b:b + 1],
                                                 rg_w[:, b, :], ALU.mult, ALU.mult).then_inc(rmix_ok, 1)

            with dve.Fori(0, SEGS) as s:
                tv = s * 11
                dve.tensor_tensor(ang[:], pos_f[:, bass.ds(s * NBLK, NBLK)].unsqueeze(2).to_broadcast([P, NBLK, HD // 2]),
                                  freq[:].unsqueeze(1).to_broadcast([P, NBLK, HD // 2]), ALU.mult).then_inc(trig_v, 1)
                dve.wait_ge(trig_v, tv + 1)
                dve.tensor_scalar(turns[:], ang[:], float(1.0 / TWO_PI), ROUND, ALU.mult, ALU.add).then_inc(trig_v, 1)
                dve.wait_ge(trig_v, tv + 2)
                dve.tensor_scalar(turns[:], turns[:], ROUND, None, ALU.subtract).then_inc(trig_v, 1)
                for m, part in enumerate((PI_A, PI_B, PI_C)):
                    dve.wait_ge(trig_v, tv + (3 + m))
                    dve.scalar_tensor_tensor(ang[:].rearrange("p b f -> p (b f)"),
                                             turns[:].rearrange("p b f -> p (b f)"), -part,
                                             ang[:].rearrange("p b f -> p (b f)"), ALU.mult, ALU.add
                                             ).then_inc(trig_v, 1)
                dve.wait_ge(trig_v, tv + 6)
                dve.tensor_scalar(ang[:], ang[:], PI_MAX, -PI_MAX, ALU.min, ALU.max).then_inc(trig_v, 1)
                normalize_x(s, 0)
                normalize_x(s, 1)
                split_lo(0, s * UNITS, REG)
                for m in range(2):
                    modulate_x(s, m)
                    rest_x(s, m)
                split_lo(1, s * UNITS, REG)
                normalize_x(s, 2)
                dve.wait_ge(trig_a, s * 3 + 3)
                HH = HD // 2
                for qk in range(2):
                    w1 = qk_wt[:, qk, 0:HH].unsqueeze(1).to_broadcast([P, NBLK, HH])
                    w2 = qk_wt[:, qk, HH:HD].unsqueeze(1).to_broadcast([P, NBLK, HH])
                    dve.tensor_tensor(rot[:, :, qk, 0, 0:HH], cosv[:], w1, ALU.mult)
                    dve.tensor_tensor(rot[:, :, qk, 0, HH:HD], cosv[:], w2, ALU.mult)
                    dve.scalar_tensor_tensor(rot[:, :, qk, 1, 0:HH], sinv[:], -1.0, w2, ALU.mult, ALU.mult)
                    dve.tensor_tensor(rot[:, :, qk, 1, HH:HD], sinv[:], w1, ALU.mult).then_inc(trig_v, 2)
                dve.tensor_copy(mask_first[:], masks[:, bass.ds(s, 1), :].rearrange("p o t -> p (o t)"))
                for i in range(NBLK):
                    att_iter(s, 0, i, True, i >= 1, i >= 2, True, 0)
                with dve.Fori(1, GROUPS) as g:
                    for i in range(NBLK):
                        att_iter(s, g, i, True, True, True, False, g - 1 if i == 0 else g)
                att_iter(s, GROUPS - 1, NBLK, False, True, True, False, GROUPS - 1)
                att_iter(s, GROUPS - 1, NBLK + 1, False, False, True, False, GROUPS - 1)
                phase_over(dve, seg_phase(s, 1))
                dve.memset(a_T[:], 0.0)
                dve.memset(chunk_keep[:], 1.0).then_inc(keep_ok, 1)
                dve.wait_ge(keep_ok, s + 1)
                dve.memset(chunk_keep[:].rearrange("p (c t) -> p c t", t=CH)[:, :, 0:1], 0.0)
                for j in range(QUADS):
                    rec_iter(s, 0, j, True, j >= 1, True, 0)
                with dve.Fori(1, RHEADS) as h:
                    for j in range(QUADS):
                        rec_iter(s, h, j, True, True, False, h - 1 if j == 0 else h)
                rec_iter(s, RHEADS - 1, QUADS, False, True, False, RHEADS - 1)
                phase_over(dve, seg_phase(s, 2))

            def m_rest(n, b):
                for q in range(4):
                    dve.wait_ge(mhi_ok, n * 4 + (4 * b + q + 1))
                    dve.tensor_tensor(m_lo[b][:, 4 * q:4 * q + 4, :].rearrange("p f t -> p (f t)"), bank[q % 2][:, :],
                                      m_hi[b][:, 4 * q:4 * q + 4, :].rearrange("p f t -> p (f t)").bitcast(F32),
                                      ALU.subtract).then_inc(mlo_ok, 1)

            def finish_rows(n, b, first):
                dve.wait_ge(y_ok, n + (b + 1))
                dve.wait_ge(xo_in[b], n * 8 + 16)
                y_tmp = [m_y[:, 0:HALF], m_y[:, HALF:D]]
                if not (first and b == 0):
                    dve.wait_ge(yout_ok, n * 2 + 2 * b)
                for c in range(2):
                    dve.tensor_tensor(y_tmp[c], bank[4 + 2 * b + c][:, :], gate_bc[:, c * HALF:(c + 1) * HALF],
                                      ALU.mult).then_inc(ygate_ok, 1)
                for c in range(2):
                    dve.wait_ge(ygate_ok, n * 2 + (2 * b + c + 1))
                    dve.tensor_tensor(xo[b][:, c * HALF:(c + 1) * HALF], xo[b][:, c * HALF:(c + 1) * HALF], y_tmp[c],
                                      ALU.add).then_inc(yout_ok, 1)

            for f in range(FT):
                if f == 1:
                    m_rest(0, 0)
                dve.wait_ge(wohi_ok, f + 1)
                dve.tensor_tensor(wo_lo[:, f, :], wo_raw[:, f, :], wo_hi[:, f, :].bitcast(F32),
                                  ALU.subtract).then_inc(wolo_ok, 1)

            m_rest(0, 1)
            finish_rows(0, 0, True)
            m_rest(2, 0)
            finish_rows(0, 1, True)
            with dve.Fori(1, OUT_BLKS // 2 - 1) as bp:
                m_rest(bp * 2, 1)
                finish_rows(bp * 2, 0, False)
                m_rest(bp * 2 + 2, 0)
                finish_rows(bp * 2, 1, False)
            m_rest(OUT_BLKS - 2, 1)
            finish_rows(OUT_BLKS - 2, 0, False)
            finish_rows(OUT_BLKS - 2, 1, False)

        @block.gpsimd
        def _(pool):
            pool.memset(minus_half[:], -0.5)
            phase_over(pool, 1)

            def inverse_root(dst, var, ss, count, done, base):
                pool.tensor_scalar(var, ss, 1.0 / count, EPS, ALU.mult, ALU.add).then_inc(done, 1)
                pool.wait_ge(done, base + 1)
                pool.tensor_tensor(dst, var, minus_half[:, 0:ss.shape[1]], ALU.pow).then_inc(done, 1)

            def root_x(s, m):
                b = m % 2
                waits_alone(pool, (x_sqd, s * NBLK + (m + 1)))
                inverse_root(x_rinv[:, b:b + 1], x_var[:, b:b + 1], x_ss[:, b:b + 1], D, x_rs, (s * NBLK + m) * 2)

            def att_iter(s, g, i, head, tail1, first):
                n = s * (GROUPS * NBLK) + g * NBLK
                if head:
                    waits = [(ss_ok, n + (i + 1))]
                    if not first or i >= 1:
                        waits.append((qn_ok, n + i))
                    waits_alone(pool, *waits)
                    inverse_root(q_rinv[:], q_var[:], q_ss[:], HD, rinv_ok, n * 2 + 2 * i)
                    rotate(s, g, i, first)
                if tail1:
                    j = (i - 1) % NBLK
                    pool.wait_ge(rden_ok, n * 3 + 3 * i)
                    pool.wait_ge(gs_ok, n + i)
                    if not first or i >= 3:
                        pool.wait_ge(omix_ok, n + (i - 2))
                    pool.tensor_tensor(g_r[j % 2][:], g_s[j % 2][:],
                                       r_den[j % 2][:].unsqueeze(2).to_broadcast([P, GH, HD]),
                                       ALU.mult).then_inc(gr_ok, 1)
                if head and first and i + 3 < NBLK:
                    root_x(s, i + 3)

            def rotate(s, g, i, first):
                n = s * (GROUPS * NBLK) + g * NBLK
                H2 = HD // 2
                if first and i == 0:
                    waits_alone(pool, (trig_v, s * 11 + 11))
                pool.wait_ge(qn_ok, n + (i + 1))
                if not first or i >= 1:
                    pool.wait_ge(rot_ok, n * 2 + 2 * i)
                x = qn
                cos_q = rot[:, i, 0, 0, :].unsqueeze(1).to_broadcast([P, GH, HD])
                pool.tensor_tensor(rc[:, 0:GH, :], x[:, 0:GH, :], cos_q, ALU.mult).then_inc(rot_parts, 1)
                pool.tensor_tensor(rc[:, GH, :], x[:, GH, :], rot[:, i, 1, 0, :], ALU.mult).then_inc(rot_parts, 1)
                for half in range(2):
                    own, other = slice(half * H2, half * H2 + H2), slice((1 - half) * H2, (1 - half) * H2 + H2)
                    sin_q = rot[:, i, 0, 1, own].unsqueeze(1).to_broadcast([P, GH, H2])
                    pool.tensor_tensor(rs[:, 0:GH, own], x[:, 0:GH, other], sin_q, ALU.mult).then_inc(rot_parts, 1)
                    pool.tensor_tensor(rs[:, GH, own], x[:, GH, other], rot[:, i, 1, 1, own],
                                       ALU.mult).then_inc(rot_parts, 1)
                pool.wait_ge(rot_parts, n * 6 + 6 * (i + 1))
                if not first or i >= 2:
                    pool.wait_ge(t_ok, n + (i - 1))
                pool.tensor_tensor(q_rot[i % 2][:], rc[:, 0:GH, :], rs[:, 0:GH, :], ALU.add).then_inc(rot_ok, 1)
                pool.tensor_tensor(k_rot[i % 2][:], rc[:, GH:GH + 1, :].to_broadcast([P, 2, HD]),
                                   rs[:, GH:GH + 1, :].to_broadcast([P, 2, HD]), ALU.add).then_inc(rot_ok, 1)

            def rec_iter(s, h, j, head, tail, first):
                n = s * (RHEADS * QUADS) + h * QUADS
                if tail:
                    pool.wait_ge(rgs_ok, n * 2 + 2 * j)
                    if not first or j >= 2:
                        pool.wait_ge(rmix_ok, n * QB + QB * (j - 1))
                    pool.tensor_tensor(rg_w[:], rg_s[:], rec_wt[:].unsqueeze(1).to_broadcast([P, QB, RK]),
                                       ALU.mult).then_inc(rgw_ok, 1)
                if head:
                    pool.wait_ge(bcum_ok, n + (j + 1))
                    if not first or j >= 1:
                        pool.wait_ge(kout_ok, n + j)
                    b3 = b_cum[:].rearrange("p (c t) -> p c t", t=CH)
                    pool.tensor_tensor(b_rest[:].rearrange("p (c t) -> p c t", t=CH),
                                       b3[:, :, CH - 1:CH].to_broadcast([P, NCH, CH]), b3, ALU.subtract).then_inc(rest_ok, 1)
                    if not first or j >= 2:
                        pool.wait_ge(ak_ok, n + (j - 1))
                    pool.wait_ge(enb_ok, n + (j + 1))
                    pool.wait_ge(kf_ok, n + (j + 1))
                    pool.tensor_tensor(k_inv[j % 2][:], k_f[:], e_nb[:], ALU.mult).then_inc(kinv_ok, 1)
                    pool.wait_ge(erest_ok, n + (j + 1))
                    pool.tensor_tensor(k_out[j % 2][:], k_f[:], b_rest[:], ALU.mult).then_inc(kout_ok, 1)
                if tail:
                    waits = [(oss_ok, n * QB + QB * j)]
                    if not first or j >= 2:
                        waits.append((rmix_ok, n * QB + QB * (j - 1)))
                    waits_alone(pool, *waits)
                    inverse_root(o_rinv[:], o_var[:], o_ss[:], RK, orinv_ok, n * 2 + 2 * (j - 1))

            with pool.Fori(0, SEGS) as s:
                for m in range(3):
                    root_x(s, m)
                for i in range(NBLK):
                    att_iter(s, 0, i, True, i >= 1, True)
                with pool.Fori(1, GROUPS) as g:
                    for i in range(NBLK):
                        att_iter(s, g, i, True, True, False)
                att_iter(s, GROUPS - 1, NBLK, False, True, False)
                phase_over(pool, seg_phase(s, 1))
                for j in range(QUADS):
                    rec_iter(s, 0, j, True, j >= 1, True)
                with pool.Fori(1, RHEADS) as h:
                    for j in range(QUADS):
                        rec_iter(s, h, j, True, True, False)
                rec_iter(s, RHEADS - 1, QUADS, False, True, False)
                phase_over(pool, seg_phase(s, 2))


def constants():
    q, k = np.arange(P)[:, None], np.arange(P)[None, :]
    prev = np.where(k > q, 0.0, NEG)
    own = np.where(k <= q, 0.0, NEG)
    first = np.concatenate([np.full((P, P), NEG), own], 1)
    later = np.concatenate([prev, own], 1)
    masks = np.stack([first] + [later] * (SEGS - 1), 1).astype(np.float32)
    s, t = np.arange(P)[:, None], np.arange(P)[None, :]
    causal = ((s <= t) & (s // CH == t // CH)).astype(np.int32)
    inv = (np.float32(10000.0) ** (-np.arange(0, HD, 2, dtype=np.float32) / np.float32(HD))).astype(np.float32)
    sign = np.tile(inv, (P, 1))
    return np.eye(P, dtype=np.float32), masks, causal, sign


def kernel(x, c, positions, norm_w, w_ada, b_ada, w_in, q_norm_w, k_norm_w, sinks, rec_norm_w, lower_bounds, w_out):
    import concourse.bacc as bacc
    from concourse.bass_utils import run_bass_kernel_spmd

    def cols(a, n):
        return np.ascontiguousarray(np.asarray(a).reshape(n, P).T)

    def rows(a):
        return np.ascontiguousarray(np.broadcast_to(np.asarray(a).reshape(1, -1), (P, np.asarray(a).size)))

    ident, masks, causal, freq = constants()
    b = np.asarray(b_ada)[0]
    arrays = {
        "x": np.asarray(x)[0], "cT": cols(c, KT), "pos": cols(positions, SEQ // P), "norm_w": cols(norm_w, KT),
        "w_ada": np.asarray(w_ada)[0], "b_cols": cols(b[:2 * D], 2 * KT), "b_gate": rows(b[2 * D:]),
        "w_in": np.asarray(w_in)[0],
        "qk_w": np.ascontiguousarray(np.stack([rows(q_norm_w), rows(k_norm_w)], 1)),
        "sinks": rows(sinks), "rec_w": rows(rec_norm_w),
        "lbT": np.ascontiguousarray(np.asarray(lower_bounds).reshape(2, RHEADS, P).transpose(2, 0, 1)),
        "w_out": np.asarray(w_out)[0],
        "ident_d": ident, "masks_d": masks, "causal_d": causal, "freq_d": freq,
    }
    arrays = {k: np.ascontiguousarray(a) for k, a in arrays.items()}
    nc = bacc.Bacc("TRN2", target_bir_lowering=False, num_devices=1)
    args = {k: nc.dram_tensor(f"in_{k}", a.shape, mybir.dt.from_np(a.dtype), kind="ExternalInput").ap()
            for k, a in arrays.items()}
    out = nc.dram_tensor("out_rows", (SEQ, D), F32, kind="ExternalOutput").ap()
    mixed = nc.dram_tensor("mixed_rows", (SEQ, MIX), F32, kind="Internal").ap()
    hybrid_layer(nc, out=out, mixed=mixed, **args)
    r = run_bass_kernel_spmd(nc, [{f"in_{k}": a for k, a in arrays.items()}], core_ids=[0])
    return r.results[0]["out_rows"].reshape(1, SEQ, D)
```

```python
from contextlib import ExitStack

import numpy as np

import concourse.bass as bass
from concourse import mybir

F32 = mybir.dt.float32
F32R = mybir.dt.float32r
I32 = mybir.dt.int32
ALU = mybir.AluOpType
ACT = mybir.ActivationFunctionType
AX_X = mybir.AxisListType.X

P = 128
D = 1024
KT = D // P
SEQ = 2048
SEGS = 2
SEG = SEQ // SEGS
NBLK = SEG // P
HEADS, GROUPS, HD = 16, 4, 64
GH = HEADS // GROUPS
QW = GH * HD
ATT = HEADS * HD
RHEADS, RK = 8, 128
QUAD = 512
QUADS = SEG // QUAD
QB = QUAD // P
CH = 64
NCH = QUAD // CH
OUT_BLKS = SEQ // P
UNITS = GROUPS + RHEADS
MIX = ATT + RHEADS * RK
FT = MIX // P
HALF = 512
MOD_T = 3 * D // HALF
WO_PARTS = 8
WO_F = FT // WO_PARTS
WO_EARLY = 5
EPS = 1e-6
NEG = -1.0e30
COL_Q, COL_K, COL_V, COL_G = 0, ATT, ATT + GROUPS * HD, ATT + 2 * GROUPS * HD
COL_RQ = 2 * ATT + 2 * GROUPS * HD
COL_RF, COL_RI, COL_RG = COL_RQ + RHEADS * RK, COL_RQ + 2 * RHEADS * RK, COL_RQ + 3 * RHEADS * RK
REG = KT * (QW + HD)
TWO_PI = 2.0 * np.pi
PI_A = 6.28125
PI_B = float(np.float32(np.round((TWO_PI - PI_A) * 2.0 ** 21) / 2.0 ** 21))
PI_C = float(TWO_PI - PI_A - PI_B)
PI_MAX = 3.1415925
ROUND = 1.5 * 2.0 ** 23


def hybrid_layer(nc, x, cT, pos, norm_w, w_ada, b_cols, b_gate, w_in, qk_w, sinks, rec_w, lbT, w_out,
                 ident_d, masks_d, causal_d, freq_d, out, mixed):
    with ExitStack() as ctx:
        def sem(name):
            return ctx.enter_context(nc.semaphore(name))

        bank = [ctx.enter_context(nc.psum_tensor(f"bank{i}", [P, 512], F32)) for i in range(8)]

        def sbuf(where, name, shape, dt=F32):
            return where.enter_context(nc.sbuf_tensor(name, shape, dt))

        ident = sbuf(ctx, "ident", [P, P])
        gate_bc = sbuf(ctx, "gate_bc", [P, D])

        unsplit = ExitStack()
        h_f = sbuf(unsplit, "h_f", [P, KT, SEG])
        x_early = sbuf(unsplit, "x_early", [P, KT, SEG])
        ang, turns, cosv, sinv = [x_early[:, :, (NBLK - 3) * P + q * (HD // 2):(NBLK - 3) * P + (q + 1) * (HD // 2)]
                                  for q in range(4)]
        wa = [h_f[:, t * KT // 2:(t + 1) * KT // 2, :].rearrange("p k (a n) -> p (k a) n", n=HALF) for t in range(2)]
        wa += [sbuf(unsplit, f"wa{t}", [P, KT, HALF])[:] for t in (2, 3)]
        unsplit.close()
        main = ExitStack()
        h_lo = sbuf(main, "h_lo", [P, KT, SEG], F32R)
        h_hi = sbuf(main, "h_hi", [P, KT, SEG], F32R)
        w_hi = [sbuf(main, f"w_hi{r}", [P, REG], F32R) for r in range(2)]
        w_lo = [sbuf(main, f"w_lo{r}", [P, REG], F32R) for r in range(2)]
        raw = [sbuf(main, f"raw{r}", [P, REG]) for r in range(2)]
        rot = sbuf(main, "rot", [P, NBLK, 2, 2, HD])
        masks = sbuf(main, "masks", [P, SEGS, 2 * P])
        mask_first = sbuf(main, "mask_first", [P, 2 * P])
        k_carry = sbuf(main, "k_carry", [P, GROUPS, 2, P])
        v_carry = sbuf(main, "v_carry", [P, GROUPS, HD])
        mod_a = sbuf(main, "mod_a", [P, KT])
        x_ss = sbuf(main, "x_ss", [P, 2])
        x_var = sbuf(main, "x_var", [P, 2])
        x_rinv = sbuf(main, "x_rinv", [P, 2])
        mod_b = sbuf(main, "mod_b", [P, KT])
        head_par = sbuf(main, "head_par", [P, RHEADS, 4])
        sink_bc = sbuf(main, "sink_bc", [P, HEADS])
        qk_wt = sbuf(main, "qk_wt", [P, 2, HD])
        rec_wt = sbuf(main, "rec_wt", [P, RK])
        minus_half = sbuf(main, "minus_half", [P, 8])
        half_pi = sbuf(main, "half_pi", [P, 1])
        freq = sbuf(main, "freq", [P, HD // 2])
        pos_f = sbuf(main, "pos_f", [P, SEQ // P])
        causal = sbuf(main, "causal", [P, P], I32)
        state = sbuf(main, "state", [P, RHEADS, RK])

        pre = ExitStack()
        wa += [sbuf(pre, f"wa{t}", [P, KT, HALF])[:] for t in (4, 5)]
        wa_sum = [sbuf(pre, f"wa_sum{i}", [P, HALF]) for i in range(2)]
        c_in = sbuf(pre, "c_in", [P, KT])
        c_th = sbuf(pre, "c_th", [P, KT])
        c_act = sbuf(pre, "c_act", [P, KT])
        c_bc = sbuf(pre, "c_bc", [P, KT, P])
        ones = sbuf(pre, "ones", [P, P])
        diag_junk = sbuf(pre, "diag_junk", [P, 4, P])
        mod_cols = sbuf(pre, "mod_cols", [P, 2 * KT])
        b_col = sbuf(pre, "b_col", [P, 2 * KT])
        b_gate_s = sbuf(pre, "b_gate_s", [P, D])
        norm_s = sbuf(pre, "norm_s", [P, KT])
        pos_i = sbuf(pre, "pos_i", [P, SEQ // P], I32)
        lb_in = sbuf(pre, "lb_in", [P, 2, RHEADS])
        lb_t = sbuf(pre, "lb_t", [P, 4, RHEADS])
        pre.close()

        att = ExitStack()
        xb = [sbuf(att, f"xb{i}", [P, D]) for i in range(2)]
        sq = sbuf(att, "sq", [P, GH + 1, HD])
        q_ss = sbuf(att, "q_ss", [P, GH + 1])
        q_var = sbuf(att, "q_var", [P, GH + 1])
        q_rinv = sbuf(att, "q_rinv", [P, GH + 1])
        qn = sbuf(att, "qn", [P, GH + 1, HD])
        rc = sbuf(att, "rc", [P, GH + 1, HD])
        rs = sbuf(att, "rs", [P, GH + 1, HD])
        q_rot = [sbuf(att, f"q_rot{i}", [P, GH, HD]) for i in range(2)]
        k_rot = [sbuf(att, f"k_rot{i}", [P, 2, HD]) for i in range(2)]
        qT_hi = [sbuf(att, f"qT_hi{i}", [P, 2, P], F32R) for i in range(2)]
        qT_lo = [sbuf(att, f"qT_lo{i}", [P, 2, P], F32R) for i in range(2)]
        kT_hi = sbuf(att, "kT_hi", [P, NBLK + 1, P], F32R)
        kT_lo = sbuf(att, "kT_lo", [P, NBLK + 1, P], F32R)
        vv = sbuf(att, "vv", [P, NBLK + 1, 2, HD])
        sm = [sbuf(att, f"sm{i}", [P, GH, 2 * P]) for i in range(2)]
        row_max = sbuf(att, "row_max", [P, GH])
        m_row = sbuf(att, "m_row", [P, GH])
        neg_m = [sbuf(att, f"neg_m{i}", [P, GH]) for i in range(2)]
        sink_d = [sbuf(att, f"sink_d{i}", [P, GH]) for i in range(2)]
        den = [sbuf(att, f"den{i}", [P, GH]) for i in range(2)]
        sink_e = [sbuf(att, f"sink_e{i}", [P, GH]) for i in range(2)]
        den2 = sbuf(att, "den2", [P, GH])
        den3 = sbuf(att, "den3", [P, GH])
        r_den = [sbuf(att, f"r_den{i}", [P, GH]) for i in range(2)]
        pT = [sbuf(att, f"pT{i}", [P, GH, 2, P]) for i in range(2)]
        g_s = [sbuf(att, f"g_s{i}", [P, GH, HD]) for i in range(2)]
        g_r = [sbuf(att, f"g_r{i}", [P, GH, HD]) for i in range(2)]
        o_mix = [sbuf(att, f"o_mix{i}", [P, GH, HD]) for i in range(2)]
        att.close()

        rec = ExitStack()
        par = sbuf(rec, "par", [P, 4])
        chunk_keep = sbuf(rec, "chunk_keep", [P, QUAD])
        f_th = sbuf(rec, "f_th", [P, QUAD])
        f_r = sbuf(rec, "f_r", [P, QUAD])
        k_f = sbuf(rec, "k_f", [P, QUAD])
        b_cum = sbuf(rec, "b_cum", [P, QUAD])
        e_b = [sbuf(rec, f"e_b{i}", [P, QUAD]) for i in range(2)]
        e_nb = sbuf(rec, "e_nb", [P, QUAD])
        b_rest = sbuf(rec, "b_rest", [P, QUAD])
        q_dec = [sbuf(rec, f"q_dec{i}", [P, QUAD]) for i in range(2)]
        k_inv = [sbuf(rec, f"k_inv{i}", [P, QUAD]) for i in range(2)]
        k_out = [sbuf(rec, f"k_out{i}", [P, QUAD]) for i in range(2)]
        k_nat = sbuf(rec, "k_nat", [P, QUAD])
        r_v = sbuf(rec, "r_v", [P, QB, RK])
        rg_th = sbuf(rec, "rg_th", [P, QB, RK])
        rg_s = sbuf(rec, "rg_s", [P, QB, RK])
        rg_w = sbuf(rec, "rg_w", [P, QB, RK])
        a_T = sbuf(rec, "a_T", [P, QB, P])
        s_in = [sbuf(rec, f"s_in{i}", [P, NCH, RK]) for i in range(2)]
        o_sq = sbuf(rec, "o_sq", [P, QB, RK])
        o_ss = sbuf(rec, "o_ss", [P, QB])
        o_var = sbuf(rec, "o_var", [P, QB])
        o_rinv = sbuf(rec, "o_rinv", [P, QB])
        r_mix = [sbuf(rec, f"r_mix{i}", [P, QB, RK]) for i in range(2)]
        rec.close()
        main.close()

        raw_rows = ExitStack()
        wo_raw = sbuf(raw_rows, "wo_raw", [P, FT, D])
        raw_rows.close()
        fin = ExitStack()
        wo_lo = sbuf(fin, "wo_lo", [P, FT, D], F32R)
        wo_hi = sbuf(fin, "wo_hi", [P, FT, D], F32R)
        m_raw = [sbuf(fin, f"m_raw{i}", [P, FT, P]) for i in range(2)]
        m_hi = [sbuf(fin, f"m_hi{i}", [P, FT, P], F32R) for i in range(2)]
        m_lo = [sbuf(fin, f"m_lo{i}", [P, FT, P], F32R) for i in range(2)]
        m_y = sbuf(fin, "m_y", [P, D])
        xo = [sbuf(fin, f"xo{i}", [P, D]) for i in range(2)]
        fin.close()

        phase_end = sem("phase_end")
        const_in = sem("const_in")
        gate_in = sem("gate_in")
        late_in = sem("late_in")
        const_ok = sem("const_ok")
        keep_ok = sem("keep_ok")
        wa_in = [[sem(f"wa_in{half}_{t}") for t in range(MOD_T)] for half in range(2)]
        wa_sum_ok = sem("wa_sum_ok")
        mod_ok = sem("mod_ok")
        c_in_ok = sem("c_in_ok")
        c_tanh = sem("c_tanh")
        c_step = sem("c_step")
        c_ready = sem("c_ready")
        mod_used = sem("mod_used")
        pre_v = sem("pre_v")
        pre_e = sem("pre_e")
        x_in = [sem(f"x_in{i}") for i in range(2)]
        x_sqd = sem("x_sqd")
        x_rs = sem("x_rs")
        x_nrm = sem("x_nrm")
        x_T = sem("x_T")
        h_mod_a, h_mod_v = sem("h_mod_a"), sem("h_mod_v")
        h_round = sem("h_round")
        h_split = sem("h_split")
        trig_step = sem("trig_step")
        rot_tables = sem("rot_tables")
        trig_a = sem("trig_a")
        raw_in = [sem(f"raw_in{r}") for r in range(2)]
        hi_ok = [sem(f"hi_ok{r}") for r in range(2)]
        lo_ok = [sem(f"lo_ok{r}") for r in range(2)]
        qk_ok, vg_ok = sem("qk_ok"), sem("vg_ok")
        sq_ok, ss_ok, rinv_ok, qn_ok = sem("sq_ok"), sem("ss_ok"), sem("rinv_ok"), sem("qn_ok")
        rot_parts, rot_ok = sem("rot_parts"), sem("rot_ok")
        krot_parts, krot_ok = sem("krot_parts"), sem("krot_ok")
        t_ok, thi_ok, tcopy_ok = sem("t_ok"), sem("thi_ok"), sem("tcopy_ok")
        s_ok, masked_ok, max_ok, exp_ok = sem("s_ok"), sem("masked_ok"), sem("max_ok"), sem("exp_ok")
        rden_ok = sem("rden_ok")
        vg_read, gs_ok, gr_ok = sem("vg_read"), sem("gs_ok"), sem("gr_ok")
        pt_ok, pta_ok, ptv_ok = sem("pt_ok"), sem("pta_ok"), sem("ptv_ok")
        pv_ok, omix_ok = sem("pv_ok"), sem("omix_ok")
        att_out = [sem(f"att_out{i}") for i in range(2)]
        carry_ok = sem("carry_ok")
        rf_ok, rq_ok, nat_ok = sem("rf_ok"), sem("rq_ok"), sem("nat_ok")
        par_ok, fth_ok, fr_ok, kf_ok = sem("par_ok"), sem("fth_ok"), sem("fr_ok"), sem("kf_ok")
        logf_ok, bcum_ok, eb_ok, enb_ok = sem("logf_ok"), sem("bcum_ok"), sem("eb_ok"), sem("enb_ok")
        rest_ok, erest_ok = sem("rest_ok"), sem("erest_ok")
        qdec_ok, kinv_ok, kout_ok = sem("qdec_ok"), sem("kinv_ok"), sem("kout_ok")
        nat_read, rgs_ok, rgw_ok = sem("nat_read"), sem("rgs_ok"), sem("rgw_ok")
        ak_ok, at_ok, knat_ok = sem("ak_ok"), sem("at_ok"), sem("knat_ok")
        state_in = sem("state_in")
        u_ok, st_ok, o_ok = sem("u_ok"), sem("st_ok"), sem("o_ok")
        oss_ok, orinv_ok, rmix_ok = sem("oss_ok"), sem("orinv_ok"), sem("rmix_ok")
        rec_out = [sem(f"rec_out{i}") for i in range(2)]
        wo_in = [sem(f"wo_in{i}") for i in range(WO_PARTS)]
        wohi_ok, wolo_ok = sem("wohi_ok"), sem("wolo_ok")
        m_in = [sem(f"m_in{i}") for i in range(2)]
        xo_in = [sem(f"xo_in{i}") for i in range(2)]
        mt_ok, mhi_ok, mlo_ok = sem("mt_ok"), sem("mhi_ok"), sem("mlo_ok")
        y_half = sem("y_half")
        y_ok, ygate_ok, yout_ok = sem("y_ok"), sem("ygate_ok"), sem("yout_ok")
        y_out = [sem(f"y_out{i}") for i in range(2)]

        x_b = x.rearrange("(b p) d -> b p d", p=P)
        out_b = out.rearrange("(b p) d -> b p d", p=P)
        mixed_b = mixed.rearrange("(b p) f -> b p f", p=P)
        wi = w_in.rearrange("(k p) n -> p k n", p=P)
        wad = w_ada.rearrange("(k p) n -> p k n", p=P)
        wo_d = w_out.rearrange("(f p) n -> p f n", p=P)

        def waits_alone(eng, *waits):
            values = [v if isinstance(v, int) else eng.to_reg(v) for _, v in waits]
            eng.wait_ge(const_in, 16)
            for (semaphore, _), v in zip(waits, values):
                eng.wait_ge(semaphore, v)

        def arrive(eng):
            eng.drain().then_inc(phase_end, 1)

        def meet(eng, k):
            waits_alone(eng, (phase_end, 5 * k))

        def phase_over(eng, k):
            arrive(eng)
            meet(eng, k)

        def seg_phase(s, j):
            return s * 2 + (1 + j)

        LAST_PHASE = SEGS * 2 + 1

        def tokens(m):
            return slice(m * P, (m + 1) * P)

        def x_rows(m):
            if m < 2:
                return x_early[:, :, tokens(NBLK - 1 - m)]
            return xb[m % 2][:].rearrange("p (k c) -> p k c", k=KT)

        def x_banks(m):
            return (bank[5], bank[6]) if m == 1 else (bank[2], bank[3])

        def region(t, width):
            return t[:, 0:KT * width].rearrange("p (k n) -> p k n", k=KT)

        block = ctx.enter_context(nc.Block())

        @block.sync
        def _(sp):
            def load(r, pieces):
                at = 0
                width = sum(n for _, n in pieces)
                dst = region(raw[r], width)
                for col, n in pieces:
                    sp.dma_start(dst[:, :, at:at + n], wi[:, :, bass.ds(col, n)]).then_inc(raw_in[r], 16)
                    at += n

            def load_att(g):
                load(0, [(g * QW + COL_Q, QW), (g * HD + COL_K, HD)])

            def load_att_b(g):
                load(1, [(g * HD + COL_V, HD), (g * QW + COL_G, QW)])

            def load_rec(h):
                load(0, [(h * RK + COL_RF, RK), (h * RK + COL_RQ, RK)])

            def load_rec_b(h):
                load(1, [(h * RK + COL_RI, RK), (h * RK + COL_RG, RK)])

            for j in range(QUADS):
                sp.sem_inc(rec_out[j], 16)
            def load_mod(t):
                for half in range(2):
                    k = slice(half * KT // 2, (half + 1) * KT // 2)
                    sp.dma_start(wa[t][:, k, :], wad[:, k, t * HALF:(t + 1) * HALF]).then_inc(wa_in[half][t], 16)

            sp.dma_start(c_in[:], cT).then_inc(c_in_ok, 16)
            sp.dma_start(ident[:], ident_d).then_inc(c_in_ok, 16)
            load_mod(0)
            load_mod(1)
            def load_x(s, m):
                sp.dma_start(x_rows(m), x_b[bass.ds(s * NBLK + m, 1)].rearrange("o p (k c) -> (o p) k c", k=KT)
                             ).then_inc(x_in[m % 2], 16)

            load_mod(2)
            load_mod(3)
            for dst, src in ((freq[:], freq_d), (pos_i[:], pos), (norm_s[:], norm_w), (b_col[:], b_cols),
                             (qk_wt[:], qk_w), (sink_bc[:], sinks), (rec_wt[:], rec_w), (lb_in[:], lbT)):
                sp.dma_start(dst, src).then_inc(const_in, 16)
            load_mod(4)
            load_mod(5)
            sp.dma_start(b_gate_s[:], b_gate).then_inc(gate_in, 16)
            sp.wait_ge(mod_ok, 2)
            load_x(0, 0)
            load_x(0, 1)
            sp.wait_ge(mod_ok, 4)
            load_att(0)
            for dst, src in ((masks[:], masks_d), (causal[:], causal_d)):
                sp.dma_start(dst, src).then_inc(late_in, 16)
            load_att_b(0)
            arrive(sp)

            def segment(s, last):
                meet(sp, seg_phase(s, 0))
                def att_spill(g, i):
                    n = s * (GROUPS * NBLK) + g * NBLK
                    sp.wait_ge(omix_ok, n + (i + 1))
                    sp.dma_start(mixed_b[bass.ds(s * NBLK + i, 1), :, bass.ds(g * QW, QW)]
                                 .rearrange("o p f -> (o p) f"),
                                 o_mix[i % 2][:].rearrange("p h d -> p (h d)")).then_inc(att_out[i % 2], 16)

                def prefetch(w, load_a, load_b, arg):
                    for r, fn in ((0, load_a), (1, load_b)):
                        sp.wait_ge(lo_ok[r], w * 2 + 2)
                        fn(arg)

                for m in range(2, NBLK):
                    if m < 4:
                        sp.wait_ge(x_sqd, s * NBLK + (m - 1))
                    else:
                        sp.wait_ge(x_T, s * NBLK + (m - 1))
                    load_x(s, m)
                    if m == 3:
                        prefetch(s * UNITS, load_att, load_att_b, 1)
                    if m >= 6:
                        att_spill(0, m - 6)
                for i in range(2, NBLK):
                    att_spill(0, i)
                with sp.Fori(1, GROUPS - 1) as g:
                    prefetch(s * UNITS + g, load_att, load_att_b, g + 1)
                    for i in range(NBLK):
                        att_spill(g, i)
                prefetch(s * UNITS + (GROUPS - 1), load_rec, load_rec_b, 0)
                for i in range(NBLK):
                    att_spill(GROUPS - 1, i)
                waits_alone(sp, *((att_out[i], (s + 1) * (16 * GROUPS * NBLK // 2)) for i in range(2)))
                phase_over(sp, seg_phase(s, 1))

                def rec_spill(h, j):
                    sp.wait_ge(rmix_ok, (s * (RHEADS * QUADS) + h * QUADS) * QB + (j + 1) * QB)
                    sp.dma_start(mixed_b[bass.ds(s * NBLK + j * QB, QB), :, bass.ds(h * RK + ATT, RK)]
                                 .rearrange("b p f -> p b f"), r_mix[j][:]).then_inc(rec_out[j], 16)

                with sp.Fori(0, RHEADS - 1) as h:
                    prefetch(s * UNITS + h + GROUPS, load_rec, load_rec_b, h + 1)
                    for j in range(QUADS):
                        rec_spill(h, j)
                if not last:
                    prefetch(s * UNITS + (UNITS - 1), load_att, load_att_b, 0)
                sp.wait_ge(nat_ok, (s + 1) * (RHEADS * QUADS))
                if not last:
                    load_x(s + 1, 0)
                    load_x(s + 1, 1)
                else:
                    load_mixed(0, 0)
                    load_out_weights(range(WO_EARLY))
                for j in range(QUADS):
                    rec_spill(RHEADS - 1, j)
                arrive(sp)

            def load_out_weights(parts):
                for t in parts:
                    fs = slice(t * WO_F, (t + 1) * WO_F)
                    sp.dma_start(wo_raw[:, fs, :], wo_d[:, fs, :]).then_inc(wo_in[t], 16)

            def load_mixed(m, b):
                sp.dma_start(m_raw[b][:].rearrange("p f t -> p (f t)"),
                             mixed_b[bass.ds(m, 1)].rearrange("o p f -> (o p) f")).then_inc(m_in[b], 16)

            def load_residual(m, b):
                sp.dma_start(xo[b][:], x_b[bass.ds(m, 1)].rearrange("o p d -> (o p) d")).then_inc(xo_in[b], 16)

            with sp.Fori(0, SEGS - 1) as s:
                segment(s, False)
            segment(SEGS - 1, True)

            meet(sp, LAST_PHASE)
            load_mixed(1, 1)
            load_out_weights(range(WO_EARLY, WO_PARTS))
            for b in range(2):
                load_residual(b, b)
            for j in range(QUADS):
                sp.wait_ge(rec_out[j], SEGS * 16 * RHEADS + 16)
            sp.wait_ge(mt_ok, 4)
            load_mixed(2, 0)

            def rows_out(n, b, ahead):
                if ahead >= 3:
                    sp.wait_ge(mt_ok, n * 4 + 4 * (b + 2))
                    load_mixed(n + (b + 3), 1 - b)
                sp.wait_ge(yout_ok, n * 2 + 2 * (b + 1))
                sp.dma_start(out_b[bass.ds(n + b, 1)].rearrange("o p d -> (o p) d"), xo[b][:]).then_inc(y_out[b], 16)
                if ahead >= 2:
                    sp.wait_ge(y_out[b], n * 8 + 16)
                    load_residual(n + (b + 2), b)

            with sp.Fori(0, OUT_BLKS // 2 - 2) as bp:
                for b in range(2):
                    rows_out(bp * 2, b, 3)
            for m in range(OUT_BLKS - 4, OUT_BLKS - 1):
                rows_out(m - m % 2, m % 2, OUT_BLKS - 1 - m)
            for c in range(2):
                m, at = OUT_BLKS - 1, slice(c * HALF, (c + 1) * HALF)
                sp.wait_ge(yout_ok, 2 * m + c + 1)
                sp.dma_start(out_b[m, :, at], xo[m % 2][:, at]).then_inc(y_out[m % 2], 16)
            for b in range(2):
                sp.wait_ge(y_out[b], 16 * (OUT_BLKS // 2 + b))

        @block.tensor
        def _(pe):
            pe.wait_ge(c_ready, 1)
            for t in range(MOD_T):
                pe.wait_ge(wa_in[1][t], 16)
                if t >= 2:
                    pe.wait_ge(mod_used, t - 1)
                for k in range(KT // 2, KT):
                    pe.matmul(bank[t % 2][:, :], c_bc[:, k, :], wa[t][:, k, :], start=(k == KT // 2), stop=False)
                pe.wait_ge(wa_sum_ok, (KT // 2) * (t + 1))
                pe.matmul(bank[t % 2][:, :], ones[:], wa_sum[t % 2][:], start=False, stop=True).then_inc(mod_ok, 1)
            arrive(pe)

            def split_products(dst, pairs, first, last):
                mm = None
                for m, (a, b) in enumerate(pairs):
                    mm = pe.matmul(dst, a, b, start=(first and m == 0), stop=(last and m == 2))
                return mm

            def project_rows(dst, r, i, c0, c1, width, k):
                wh, wl = region(w_hi[r], width)[:, k, c0:c1], region(w_lo[r], width)[:, k, c0:c1]
                ah, al = h_hi[:, k, i * P:(i + 1) * P], h_lo[:, k, i * P:(i + 1) * P]
                return split_products(dst, ((ah, wh), (ah, wl), (al, wh)), k == 0, k == KT - 1)

            def project_cols(dst, c0, j, k):
                wh, wl = region(w_hi[0], 2 * RK)[:, k, c0:c0 + RK], region(w_lo[0], 2 * RK)[:, k, c0:c0 + RK]
                ah, al = h_hi[:, k, j * QUAD:(j + 1) * QUAD], h_lo[:, k, j * QUAD:(j + 1) * QUAD]
                return split_products(dst, ((wh, ah), (wl, ah), (wh, al)), k == 0, k == KT - 1)

            def weights_ready(r, w, half):
                pe.wait_ge(lo_ok[r], w * 2 + (half + 1))

            def project(r, w, fresh, one_k):
                for k in range(KT):
                    if fresh and k % (KT // 2) == 0:
                        weights_ready(r, w, k // (KT // 2))
                    mm = one_k(k)
                return mm

            def project_f(w, j, fresh):
                project(0, w, fresh, lambda k: project_cols(bank[0][:, :], 0, j, k)).then_inc(rf_ok, 1)

            def project_q(j):
                project(0, 0, False, lambda k: project_cols(bank[1][:, :], RK, j, k)).then_inc(rq_ok, 1)

            def project_nat(w, j, half, fresh):
                for b in range(2):
                    mm = project(1, w, fresh and half == 0 and b == 0,
                                 lambda k: project_rows(bank[2 + half][:, b * 2 * RK:(b + 1) * 2 * RK], 1,
                                                        j * QB + half * 2 + b, 0, 2 * RK, 2 * RK, k))
                if half == 1:
                    mm.then_inc(nat_ok, 1)

            def transpose_x(s, m):
                pe.wait_ge(x_nrm, s * NBLK + (m + 1))
                for k in range(KT):
                    mm = pe.transpose(x_banks(m)[k // 4][:, (k % 4) * P:(k % 4 + 1) * P],
                                      x_rows(m)[:, k, :], ident[:])
                mm.then_inc(x_T, 1)

            def x_banks_read(s, m):
                pe.wait_ge(h_mod_a, s * NBLK + (m + 1))
                pe.wait_ge(h_mod_v, s * NBLK + (m + 1))

            def att_iter(s, g, i, head, tail1, tail2, first):
                n = s * (GROUPS * NBLK) + g * NBLK
                w = s * UNITS + g
                steady = not first
                if head and first:
                    pe.wait_ge(h_split, s * NBLK + (i + 1))
                if head:
                    if steady or i >= 1:
                        pe.wait_ge(sq_ok, n + i)
                        pe.wait_ge(qn_ok, n + i)
                    project(0, w, i == 0, lambda k: project_rows(bank[0][:, 0:QW + HD], 0, i, 0, QW + HD, QW + HD, k)
                            ).then_inc(qk_ok, 1)
                if tail1:
                    j = (i - 1) % NBLK
                    pe.wait_ge(tcopy_ok, n * 2 + 2 * i)
                    if first and i + 1 < NBLK:
                        x_banks_read(s, i + 1)
                    if steady or i >= 2:
                        pe.wait_ge(masked_ok, n * GH + GH * (i - 1))
                    for pair in range(0, GH, 2):
                        for m, (tq, tk) in enumerate(((qT_hi, kT_hi), (qT_hi, kT_lo), (qT_lo, kT_hi))):
                            for h in (pair, pair + 1):
                                lo = HD * (h % 2)
                                mm = pe.matmul(bank[2 + h % 2][:, (h // 2) * 2 * P:(h // 2 + 1) * 2 * P],
                                               tq[j % 2][lo:lo + HD, h // 2, :], tk[lo:lo + HD, j:j + 2, :],
                                               start=(m == 0), stop=(m == 2))
                    mm.then_inc(s_ok, 1)
                if i == NBLK and not head:
                    pe.wait_ge(sq_ok, n + NBLK)
                    pe.wait_ge(qn_ok, n + NBLK)
                    project_f(w + 1, 0, True)
                if i > NBLK:
                    pe.wait_ge(vg_read, n * 2 + 2 * NBLK)
                    pe.wait_ge(gs_ok, n + NBLK)
                    project_q(0)
                if head:
                    if steady or i >= 1:
                        pe.wait_ge(vg_read, n * 2 + 2 * i)
                        pe.wait_ge(gs_ok, n + i)
                    project(1, w, i == 0, lambda k: project_rows(bank[1][:, 0:QW + HD], 1, i, 0, QW + HD, QW + HD, k)
                            ).then_inc(vg_ok, 1)
                if head and first and i + 2 < NBLK:
                    if i == 0:
                        x_banks_read(s, 0)
                    else:
                        pe.wait_ge(masked_ok, n * GH + GH * i)
                    transpose_x(s, i + 2)
                if tail2:
                    j = (i - 2) % NBLK
                    pe.wait_ge(pta_ok, n + (i - 1))
                    pe.wait_ge(ptv_ok, n + (i - 1))
                    if steady or i >= 3:
                        pe.wait_ge(omix_ok, n + (i - 2))
                    for h in range(GH):
                        for half in range(2):
                            mm = pe.matmul(bank[7][:, h * P:(h + 1) * P], pT[j % 2][:, h, half, :],
                                           vv[:, j + half, :, :].rearrange("p a d -> p (a d)"),
                                           start=(half == 0), stop=(half == 1))
                    mm.then_inc(pv_ok, 1)
                if tail1:
                    j = (i - 1) % NBLK
                    pe.wait_ge(exp_ok, n * (GH + 1) + (GH + 1) * i)
                    if steady or i >= 2:
                        pe.wait_ge(pta_ok, n + (i - 1))
                        pe.wait_ge(ptv_ok, n + (i - 1))
                    if first and i == 1:
                        x_banks_read(s, 1)
                    for h in range(GH):
                        for half in range(2):
                            at = ((h % 2) * 2 + half) * P
                            mm = pe.transpose(bank[5 + h // 2][:, at:at + P],
                                              sm[j % 2][:, h, half * P:(half + 1) * P], ident[:])
                    mm.then_inc(pt_ok, 1)
                if head:
                    pe.wait_ge(rot_ok, n + (i + 1))
                    if steady or i >= 1:
                        pe.wait_ge(tcopy_ok, n * 2 + 2 * i)
                    for h in range(2):
                        pe.transpose(bank[4][:, h * P:(h + 1) * P],
                                     q_rot[i % 2][:, 2 * h:2 * h + 2, :].rearrange("p a d -> p (a d)"), ident[:])
                    pe.wait_ge(krot_ok, n + (i + 1))
                    pe.transpose(bank[4][:, 2 * P:3 * P], k_rot[i % 2][:].rearrange("p a d -> p (a d)"),
                                 ident[:]).then_inc(t_ok, 1)

            def rec_iter(s, h, j, head, tail, first):
                n = s * (RHEADS * QUADS) + h * QUADS
                w = s * UNITS + h + GROUPS
                steady = not first
                jt = (j - 1) % QUADS
                if head:
                    if steady or j >= 1:
                        pe.wait_ge(fth_ok, n + j)
                    project_f(w, j, j == 0)
                if tail:
                    pe.wait_ge(qdec_ok, n + j)
                    pe.wait_ge(kinv_ok, n + j)
                    pe.wait_ge(kout_ok, n + j)
                    if steady or j >= 2:
                        pe.wait_ge(at_ok, n * QB + QB * (j - 1))
                        pe.wait_ge(st_ok, n * NCH + NCH * (j - 1))
                    for b in range(QB):
                        pe.matmul(bank[4][:, b * P:(b + 1) * P], k_inv[jt][:, b * P:(b + 1) * P],
                                  q_dec[jt][:, b * P:(b + 1) * P], start=True, stop=True)
                    for b in range(QB):
                        mm = pe.transpose(bank[5][:, b * P:(b + 1) * P], k_out[jt][:, b * P:(b + 1) * P], ident[:])
                    mm.then_inc(ak_ok, 1)
                if head:
                    if steady or j >= 1:
                        pe.wait_ge(qdec_ok, n + j)
                    project_q(j)
                if tail:
                    pe.wait_ge(knat_ok, n + j)
                    pe.wait_ge(nat_read, n * 4 + 4 * j)
                    for c in range(NCH):
                        lo, b = CH * (c % 2), c // 2
                        mm = pe.matmul(bank[6 - c % 2][:, b * P:(b + 1) * P], k_nat[lo:lo + CH, b * P:(b + 1) * P],
                                       r_v[lo:lo + CH, b, :], start=True, stop=True)
                    mm.then_inc(u_ok, 1)
                for half in range(2):
                    if head:
                        if half == 0 and (steady or j >= 1):
                            pe.wait_ge(nat_read, n * 4 + 4 * j)
                            pe.wait_ge(rgs_ok, n * 2 + 2 * j)
                        project_nat(w, j, half, j == 0)
                    if tail and half == 0:
                        pe.wait_ge(at_ok, n * QB + QB * j)
                        if steady or j >= 2:
                            pe.wait_ge(rmix_ok, n * QB + QB * (j - 1))
                        for b in range(QB):
                            pe.matmul(bank[7][:, b * P:(b + 1) * P], a_T[:, b, :], r_v[:, b, :], start=(b == 0),
                                      stop=False, skip_group_check=True)
                        pe.wait_ge(st_ok, n * NCH + NCH * j)
                        for b in range(QB):
                            for c in range(2):
                                t0 = b * P + c * CH
                                mm = pe.matmul(bank[7][c * CH:(c + 1) * CH, b * P:(b + 1) * P],
                                               q_dec[jt][:, t0:t0 + CH], s_in[jt][:, 2 * b + c, :],
                                               start=False, stop=True, skip_group_check=True)
                        mm.then_inc(o_ok, 1)

            with pe.Fori(0, SEGS) as s:
                meet(pe, seg_phase(s, 0))
                transpose_x(s, 0)
                transpose_x(s, 1)
                for i in range(NBLK):
                    att_iter(s, 0, i, True, i >= 1, i >= 2, True)
                with pe.Fori(1, GROUPS) as g:
                    for i in range(NBLK):
                        att_iter(s, g, i, True, True, True, False)
                att_iter(s, GROUPS - 1, NBLK, False, True, True, False)
                att_iter(s, GROUPS - 1, NBLK + 1, False, False, True, False)
                arrive(pe)
                pe.wait_ge(masked_ok, (s + 1) * (GROUPS * NBLK * GH))
                for half in range(2):
                    project_nat(s * UNITS + GROUPS, 0, half, True)
                meet(pe, seg_phase(s, 1))
                for j in range(1, QUADS):
                    rec_iter(s, 0, j, True, True, True)
                with pe.Fori(1, RHEADS) as h:
                    for j in range(QUADS):
                        rec_iter(s, h, j, True, True, False)
                rec_iter(s, RHEADS - 1, QUADS, False, True, False)
                arrive(pe)

            def transposes(n, b, q):
                if q == 0:
                    pe.wait_ge(m_in[b], n * 8 + 16)
                if not isinstance(n, int) or n + b > 0 or q >= 2:
                    pe.wait_ge(mlo_ok, n * 4 + (4 * b + q - 1))
                for f in range(4):
                    mm = pe.transpose(bank[q % 2][:, f * P:(f + 1) * P], m_raw[b][:, q * 4 + f, :], ident[:])
                mm.then_inc(mt_ok, 1)

            def out_rows(n, b, first):
                pe.wait_ge(mlo_ok, n * 4 + 4 * (b + 1))
                if not first:
                    pe.wait_ge(ygate_ok, n * 2 + 2 * (b - 1))
                for f in range(FT):
                    if first and b == 0:
                        pe.wait_ge(wolo_ok, f + 1)
                    mh, ml = m_hi[b][:, f, :], m_lo[b][:, f, :]
                    for c in range(2):
                        wh, wl = wo_hi[:, f, c * HALF:(c + 1) * HALF], wo_lo[:, f, c * HALF:(c + 1) * HALF]
                        mm = split_products(bank[4 + 2 * b + c][:, :], ((mh, wh), (mh, wl), (ml, wh)), f == 0, f == FT - 1)
                    if f % 4 == 1:
                        transposes(n + 2 * b, 1 - b, f // 4)
                mm.then_inc(y_ok, 1)

            def last_rows(m):
                b = m % 2
                pe.wait_ge(mlo_ok, 4 * (m + 1))
                pe.wait_ge(ygate_ok, 2 * (m - 1))
                for c in range(2):
                    for f in range(FT):
                        mh, ml = m_hi[b][:, f, :], m_lo[b][:, f, :]
                        wh, wl = wo_hi[:, f, c * HALF:(c + 1) * HALF], wo_lo[:, f, c * HALF:(c + 1) * HALF]
                        mm = split_products(bank[4 + 2 * b + c][:, :], ((mh, wh), (mh, wl), (ml, wh)), f == 0, f == FT - 1)
                    mm.then_inc(y_half, 1)

            for q in range(4):
                if q == 2:
                    meet(pe, LAST_PHASE)
                transposes(0, 0, q)
            out_rows(0, 0, True)
            out_rows(0, 1, True)
            with pe.Fori(1, OUT_BLKS // 2 - 1) as bp:
                out_rows(bp * 2, 0, False)
                out_rows(bp * 2, 1, False)
            out_rows(OUT_BLKS - 2, 0, False)
            last_rows(OUT_BLKS - 1)

        @block.scalar
        def _(act):
            act.wait_ge(c_in_ok, 32)
            act.activation(c_th[:], c_in[:], ACT.Tanh, scale=0.5).then_inc(c_tanh, 1)
            act.wait_ge(pre_v, 2)
            act.activation(lb_t[:, 2:4, :], lb_t[:, 0:2, :], ACT.Exp).then_inc(pre_e, 1)
            arrive(act)

            def split_hi(r, w, size=REG):
                act.wait_ge(raw_in[r], w * 32 + 32)
                for half in (slice(0, size // 2), slice(size // 2, size)):
                    act.activation(w_hi[r][:, half], raw[r][:, half], ACT.Copy).then_inc(hi_ok[r], 1)

            def square_x(s, m):
                act.wait_ge(x_in[m % 2], (s * (NBLK // 2) + m // 2) * 16 + 16)
                act.activation(h_f[:, :, tokens(m)], x_rows(m),
                               ACT.Square, accum_out=x_ss[:, m % 2:m % 2 + 1]).then_inc(x_sqd, 1)

            def modulate_x(s, m):
                act.wait_ge(x_T, s * NBLK + (m + 1))
                for k in range(KT // 2):
                    a = act.activation(h_f[:, k, tokens(m)], x_banks(m)[0][:, k * P:(k + 1) * P],
                                       ACT.Identity, bias=mod_b[:, k:k + 1], scale=mod_a[:, k:k + 1])
                a.then_inc(h_mod_a, 1)

            def round_x(s, m):
                act.wait_ge(h_mod_a, s * NBLK + (m + 1))
                act.wait_ge(h_mod_v, s * NBLK + (m + 1))
                act.activation(h_hi[:, :, tokens(m)], h_f[:, :, tokens(m)], ACT.Copy
                               ).then_inc(h_round, 1)

            def att_iter(s, g, i, head, tail1, tail2, first):
                n = s * (GROUPS * NBLK) + g * NBLK
                w = s * UNITS + g
                if head:
                    act.wait_ge(qk_ok, n + (i + 1))
                    if not first or i >= 1:
                        act.wait_ge(ss_ok, n + i)
                    act.activation(sq[:].rearrange("p h d -> p (h d)"), bank[0][:, 0:QW + HD],
                                   ACT.Square).then_inc(sq_ok, 1)
                if head and first and i == 0:
                    square_x(s, 2)
                if head and i == NBLK - 1:
                    split_hi(0, w + 1)
                if tail1:
                    j = (i - 1) % NBLK
                    act.wait_ge(max_ok, n * 3 + 3 * i)
                    if not first or i >= 3:
                        act.wait_ge(rden_ok, n * 3 + 3 * (i - 2))
                    for h in range(GH):
                        act.activation(sm[j % 2][:, h, :], sm[j % 2][:, h, :], ACT.Exp,
                                       bias=neg_m[j % 2][:, h:h + 1],
                                       accum_out=den[j % 2][:, h:h + 1]).then_inc(exp_ok, 1)
                    act.activation(sink_e[j % 2][:], sink_d[j % 2][:], ACT.Exp).then_inc(exp_ok, 1)
                if head:
                    act.wait_ge(vg_ok, n + (i + 1))
                    if not first or i >= 2:
                        act.wait_ge(gr_ok, n + (i - 1))
                    if i == 0 and not first:
                        act.wait_ge(carry_ok, s * GROUPS + g)
                    act.activation(vv[:, i + 1, :, :], bank[1][:, 0:HD].unsqueeze(1).to_broadcast([P, 2, HD]),
                                   ACT.Copy).then_inc(vg_read, 1)
                    act.activation(g_s[i % 2][:].rearrange("p h d -> p (h d)"), bank[1][:, HD:HD + QW],
                                   ACT.Tanh, scale=0.5).then_inc(vg_read, 1)
                if head and first and i == 0:
                    modulate_x(s, 1)
                    round_x(s, 1)
                if head and first and i + 2 < NBLK:
                    modulate_x(s, i + 2)
                if tail1:
                    j = (i - 1) % NBLK
                    act.wait_ge(pt_ok, n + i)
                    if not first or i >= 3:
                        act.wait_ge(pv_ok, n + (i - 2))
                    act.activation(pT[j % 2][:, 0:2, :, :].rearrange("p h a q -> p (h a q)"), bank[5][:, :],
                                   ACT.Copy).then_inc(pta_ok, 1)
                if head:
                    act.wait_ge(t_ok, n + (i + 1))
                    if not first or i >= 2:
                        act.wait_ge(s_ok, n + (i - 1))
                    act.activation(qT_hi[i % 2][:].rearrange("p a t -> p (a t)"), bank[4][:, 0:2 * P],
                                   ACT.Copy).then_inc(thi_ok, 1)
                    act.activation(kT_hi[:, i + 1, :], bank[4][:, 2 * P:3 * P], ACT.Copy).then_inc(thi_ok, 1)
                if head and first and i + 2 < NBLK:
                    round_x(s, i + 2)
                if head and first and i + 3 < NBLK:
                    square_x(s, i + 3)
                if head and i == NBLK - 1:
                    split_hi(1, w + 1)

            def rec_iter(s, h, j, head, tail, first):
                n = s * (RHEADS * QUADS) + h * QUADS
                w = s * UNITS + h + GROUPS
                jt = (j - 1) % QUADS
                if head and j == 0 and not first:
                    act.wait_ge(rq_ok, n)
                    split_hi(0, w, KT * 2 * RK)
                if tail:
                    act.wait_ge(nat_ok, n + j)
                    if not first or j >= 2:
                        act.wait_ge(o_ok, n + (j - 1))
                        act.wait_ge(rgs_ok, n * 2 + 2 * (j - 1))
                    for half in range(2):
                        nat = bank[2 + half][:, :].rearrange("p (b n) -> p b n", b=2)
                        act.activation(r_v[:, 2 * half:2 * half + 2, :], nat[:, :, 0:RK],
                                       ACT.Copy).then_inc(nat_read, 1)
                        act.activation(rg_s[:, 2 * half:2 * half + 2, :], nat[:, :, RK:2 * RK],
                                       ACT.Tanh, scale=0.5).then_inc(nat_read, 1)
                if head:
                    act.wait_ge(rf_ok, n + (j + 1))
                    if not first or j >= 1:
                        act.wait_ge(kf_ok, n + j)
                    act.activation(f_th[:], bank[0][:, :], ACT.Tanh, scale=0.5).then_inc(fth_ok, 1)
                if tail:
                    act.wait_ge(ak_ok, n + j)
                    act.activation(k_nat[:], bank[5][:, :], ACT.Copy).then_inc(knat_ok, 1)
                if head and j == 0 and not first:
                    act.wait_ge(nat_ok, n)
                    split_hi(1, w, KT * 2 * RK)
                if head:
                    act.wait_ge(fr_ok, n + (j + 1))
                    act.activation(f_r[:], f_r[:], ACT.Ln, bias=par[:, 0:1]).then_inc(logf_ok, 1)
                    act.wait_ge(bcum_ok, n + (j + 1))
                    if not first or j >= 2:
                        act.wait_ge(st_ok, n * NCH + NCH * (j - 1))
                    act.activation(e_b[j % 2][:], b_cum[:], ACT.Exp).then_inc(eb_ok, 1)
                    if not first or j >= 1:
                        act.wait_ge(kinv_ok, n + j)
                    act.activation(e_nb[:], b_cum[:], ACT.Exp, scale=-1.0).then_inc(enb_ok, 1)
                    act.wait_ge(rest_ok, n + (j + 1))
                    act.activation(b_rest[:], b_rest[:], ACT.Exp).then_inc(erest_ok, 1)
                if tail:
                    act.wait_ge(o_ok, n + j)
                    if not first or j >= 2:
                        act.wait_ge(orinv_ok, n * 2 + 2 * (j - 1))
                    for b in range(QB):
                        act.activation(o_sq[:, b, :], bank[7][:, b * P:(b + 1) * P], ACT.Square,
                                       accum_out=o_ss[:, b:b + 1]).then_inc(oss_ok, 1)

            with act.Fori(0, SEGS) as s:
                square_x(s, 0)
                square_x(s, 1)
                meet(act, seg_phase(s, 0))
                modulate_x(s, 0)
                round_x(s, 0)
                split_hi(0, s * UNITS)
                split_hi(1, s * UNITS)
                act.wait_ge(trig_step, s * 10 + 10)
                act.activation(sinv, ang,
                               ACT.Sin).then_inc(trig_a, 1)
                act.activation(turns, ang,
                               ACT.Abs).then_inc(trig_a, 1)
                act.wait_ge(trig_a, s * 3 + 2)
                act.activation(cosv, turns,
                               ACT.Sin, bias=half_pi[:, 0:1], scale=-1.0).then_inc(trig_a, 1)
                for i in range(NBLK):
                    att_iter(s, 0, i, True, i >= 1, i >= 2, True)
                with act.Fori(1, GROUPS) as g:
                    for i in range(NBLK):
                        att_iter(s, g, i, True, True, True, False)
                att_iter(s, GROUPS - 1, NBLK, False, True, True, False)
                phase_over(act, seg_phase(s, 1))
                for j in range(QUADS):
                    rec_iter(s, 0, j, True, j >= 1, True)
                with act.Fori(1, RHEADS) as h:
                    for j in range(QUADS):
                        rec_iter(s, h, j, True, True, False)
                rec_iter(s, RHEADS - 1, QUADS, False, True, False)
                arrive(act)

            def m_rounded(n, b, first):
                for q in range(4):
                    act.wait_ge(mt_ok, n * 4 + (4 * b + q + 1))
                    if not first:
                        act.wait_ge(y_ok, n + (b - 1))
                    act.activation(m_hi[b][:, 4 * q:4 * q + 4, :].rearrange("p f t -> p (f t)"), bank[q % 2][:, :],
                                   ACT.Copy).then_inc(mhi_ok, 1)

            for f in range(FT):
                if f == 2:
                    meet(act, LAST_PHASE)
                    m_rounded(0, 0, True)
                if f % WO_F == 0:
                    act.wait_ge(wo_in[f // WO_F], 16)
                act.activation(wo_hi[:, f, :], wo_raw[:, f, :], ACT.Copy).then_inc(wohi_ok, 1)

            m_rounded(0, 1, True)
            with act.Fori(1, OUT_BLKS // 2) as bp:
                for b in range(2):
                    m_rounded(bp * 2, b, False)

        @block.vector
        def _(dve):
            for t, v in ((ones, 1.0), (half_pi, float(np.pi / 2)), (state, 0.0), (k_carry, 0.0), (v_carry, 0.0)):
                dve.memset(t[:], v).then_inc(const_ok, 1)
            dve.wait_ge(const_ok, 5)
            dve.wait_ge(c_in_ok, 32)
            dve.wait_ge(c_tanh, 1)
            dve.scalar_tensor_tensor(c_act[:], c_th[:], 1.0, c_in[:], ALU.add, ALU.mult).then_inc(c_step, 1)
            dve.wait_ge(c_step, 1)
            dve.tensor_scalar(c_act[:], c_act[:], 0.5, None, ALU.mult).then_inc(c_step, 1)
            dve.wait_ge(c_step, 2)
            for k in range(KT // 2, KT):
                a = dve.tensor_scalar(c_bc[:, k, :], ones[:], c_act[:, k:k + 1], None, ALU.mult)
            a.then_inc(c_ready, 1)

            def mod_sum(t):
                dve.wait_ge(wa_in[0][t], 16)
                if t >= 2:
                    dve.wait_ge(mod_ok, t - 1)
                total = wa_sum[t % 2][:]
                dve.tensor_scalar(total, wa[t][:, 0, :], c_act[:, 0:1], None, ALU.mult).then_inc(wa_sum_ok, 1)
                for k in range(1, KT // 2):
                    dve.wait_ge(wa_sum_ok, (KT // 2) * t + k)
                    dve.scalar_tensor_tensor(total, wa[t][:, k, :], c_act[:, k:k + 1], total,
                                             ALU.mult, ALU.add).then_inc(wa_sum_ok, 1)

            def mod_read(t):
                dve.wait_ge(mod_ok, t + 1)
                if t < 4:
                    if t >= 1:
                        dve.wait_ge(mod_used, t)
                    for q in range(4):
                        a = dve.tensor_tensor_reduce(diag_junk[:, q, :], bank[t % 2][:, q * P:(q + 1) * P], ident[:],
                                                     1.0, 0.0, ALU.mult, ALU.add, mod_cols[:, 4 * t + q:4 * t + q + 1])
                else:
                    dve.wait_ge(gate_in, 16)
                    g0 = (t - 4) * HALF
                    a = dve.tensor_tensor(gate_bc[:, g0:g0 + HALF], bank[t % 2][:, :], b_gate_s[:, g0:g0 + HALF], ALU.add)
                a.then_inc(mod_used, 1)

            mod_sum(0)
            mod_sum(1)
            mod_read(0)
            for t in range(2, MOD_T):
                mod_sum(t)
                mod_read(t - 1)
                if t == 4:
                    dve.wait_ge(const_in, 16 * 8)
                    dve.tensor_tensor(lb_t[:, 2, :], lb_in[:, 0, :], lb_in[:, 1, :], ALU.max).then_inc(pre_v, 1)
                    dve.wait_ge(pre_v, 1)
                    dve.tensor_tensor(lb_t[:, 0:2, :], lb_in[:], lb_t[:, 2:3, :].to_broadcast([P, 2, RHEADS]),
                                      ALU.subtract).then_inc(pre_v, 1)
                    dve.tensor_copy(pos_f[:], pos_i[:]).then_inc(pre_v, 1)
                    dve.wait_ge(pre_e, 1)
                    dve.tensor_tensor(lb_t[:, 0, :], lb_t[:, 2, :], lb_t[:, 3, :], ALU.add).then_inc(pre_v, 1)
                    dve.wait_ge(pre_v, 4)
                    dve.reciprocal(lb_t[:, 1, :], lb_t[:, 0, :]).then_inc(pre_v, 1)
                    dve.wait_ge(pre_v, 5)
                    dve.tensor_tensor(head_par[:, :, 0], lb_t[:, 2, :], lb_t[:, 1, :], ALU.mult).then_inc(pre_v, 1)
                    dve.wait_ge(pre_v, 6)
                    dve.tensor_scalar(head_par[:, :, 1], head_par[:, :, 0], -0.5, 0.5, ALU.mult, ALU.add).then_inc(pre_v, 1)
                    dve.tensor_scalar(head_par[:, :, 2], head_par[:, :, 0], 0.5, -0.5, ALU.mult, ALU.add).then_inc(pre_v, 1)
                    dve.memset(head_par[:, :, 3], 0.0).then_inc(pre_v, 1)
                    dve.tensor_scalar(qk_wt[:, 0, :], qk_wt[:, 0, :], float(HD) ** -0.5, None, ALU.mult).then_inc(pre_v, 1)
                    dve.tensor_scalar(rec_wt[:], rec_wt[:], 0.5, None, ALU.mult).then_inc(pre_v, 1)
                    dve.wait_ge(mod_used, 4)
                    dve.tensor_tensor(mod_b[:], mod_cols[:, 0:KT], b_col[:, 0:KT], ALU.add).then_inc(pre_v, 1)
                    dve.tensor_tensor(mod_a[:], mod_cols[:, KT:2 * KT], b_col[:, KT:2 * KT], ALU.add).then_inc(pre_v, 1)
                    dve.wait_ge(pre_v, 13)
                    dve.scalar_tensor_tensor(mod_a[:], mod_a[:], 1.0, norm_s[:], ALU.add, ALU.mult).then_inc(pre_v, 1)
            mod_read(MOD_T - 1)
            arrive(dve)

            def split_lo(r, w, size=REG):
                for m in range(2):
                    half = slice(m * (size // 2), (m + 1) * (size // 2))
                    dve.wait_ge(hi_ok[r], w * 2 + (m + 1))
                    dve.tensor_tensor(w_lo[r][:, half], raw[r][:, half], w_hi[r][:, half].bitcast(F32),
                                      ALU.subtract).then_inc(lo_ok[r], 1)

            def normalize_x(s, m):
                b = m % 2
                dve.wait_ge(x_rs, (s * NBLK + m) * 2 + 2)
                dve.tensor_scalar(x_rows(m), x_rows(m), x_rinv[:, b:b + 1], None, ALU.mult).then_inc(x_nrm, 1)

            def modulate_x(s, m):
                dve.wait_ge(x_T, s * NBLK + (m + 1))
                for k in range(KT // 2, KT):
                    at = (k - KT // 2) * P
                    a = dve.tensor_scalar(h_f[:, k, tokens(m)], x_banks(m)[1][:, at:at + P],
                                          mod_a[:, k:k + 1], mod_b[:, k:k + 1], ALU.mult, ALU.add)
                a.then_inc(h_mod_v, 1)

            def rest_x(s, m):
                dve.wait_ge(h_round, s * NBLK + (m + 1))
                dve.tensor_tensor(h_lo[:, :, tokens(m)], h_f[:, :, tokens(m)], h_hi[:, :, tokens(m)].bitcast(F32),
                                  ALU.subtract).then_inc(h_split, 1)

            def rotary_tables(s):
                dve.wait_ge(trig_a, s * 3 + 3)
                H2 = HD // 2
                for qk in range(2):
                    w1 = qk_wt[:, qk, 0:H2].unsqueeze(1).to_broadcast([P, NBLK, H2])
                    w2 = qk_wt[:, qk, H2:HD].unsqueeze(1).to_broadcast([P, NBLK, H2])
                    dve.tensor_tensor(rot[:, :, qk, 0, 0:H2], cosv, w1, ALU.mult)
                    dve.tensor_tensor(rot[:, :, qk, 0, H2:HD], cosv, w2, ALU.mult)
                    dve.scalar_tensor_tensor(rot[:, :, qk, 1, 0:H2], sinv, -1.0, w2, ALU.mult, ALU.mult)
                    dve.tensor_tensor(rot[:, :, qk, 1, H2:HD], sinv, w1, ALU.mult).then_inc(rot_tables, 1)

            def att_iter(s, g, i, head, tail1, tail2, first, gt):
                n = s * (GROUPS * NBLK) + g * NBLK
                w = s * UNITS + g
                if head and first and 1 <= i and i + 2 < NBLK:
                    normalize_x(s, i + 2)
                if head and i == 0:
                    kept = k_carry[:, bass.ds(g, 1), :, :]
                    dve.tensor_copy(kT_hi[:, 0:1, :], kept[:, :, 0, :])
                    dve.tensor_copy(kT_lo[:, 0:1, :], kept[:, :, 1, :])
                    dve.tensor_copy(vv[:, 0, :, :], v_carry[:, bass.ds(g, 1), :].to_broadcast([P, 2, HD]))
                if head:
                    dve.wait_ge(sq_ok, n + (i + 1))
                    dve.reduce_sum(q_ss[:], sq[:], AX_X).then_inc(ss_ok, 1)
                if head and first and i == 0:
                    rotary_tables(s)
                if tail1:
                    j = (i - 1) % NBLK
                    waits = [(s_ok, n + i)]
                    if not first or i >= 2:
                        waits.append((max_ok, n * 3 + 3 * (i - 1)))
                    if not first or i >= 3:
                        waits.append((pt_ok, n + (i - 2)))
                    waits_alone(dve, *waits)
                    mask = mask_first[:] if j == 0 else masks[:, SEGS - 1, :]
                    for h in range(GH):
                        dve.tensor_tensor_reduce(sm[j % 2][:, h, :],
                                                 bank[2 + h % 2][:, (h // 2) * 2 * P:(h // 2 + 1) * 2 * P],
                                                 mask, 1.0, NEG, ALU.add, ALU.max,
                                                 row_max[:, h:h + 1]).then_inc(masked_ok, 1)
                if head:
                    dve.wait_ge(rinv_ok, n * 2 + 2 * (i + 1))
                    if not first or i >= 1:
                        dve.wait_ge(rot_ok, n + i)
                    dve.tensor_tensor(qn[:], bank[0][:, 0:QW + HD].rearrange("p (h d) -> p h d", d=HD),
                                      q_rinv[:].unsqueeze(2).to_broadcast([P, GH + 1, HD]),
                                      ALU.mult).then_inc(qn_ok, 1)
                if tail1:
                    dve.wait_ge(masked_ok, n * GH + GH * i)
                    sink = sink_bc[:, bass.ds(gt * GH, GH)]
                    dve.tensor_tensor(m_row[:], row_max[:], sink, ALU.max).then_inc(max_ok, 1)
                    dve.wait_ge(max_ok, n * 3 + (3 * i - 2))
                    dve.tensor_scalar(neg_m[j % 2][:], m_row[:], -1.0, None, ALU.mult).then_inc(max_ok, 1)
                    dve.tensor_tensor(sink_d[j % 2][:], sink, m_row[:], ALU.subtract).then_inc(max_ok, 1)
                if head and i == NBLK - 1:
                    split_lo(0, w + 1)
                if head:
                    H2 = HD // 2
                    dve.wait_ge(qn_ok, n + (i + 1))
                    if not first or i >= 1:
                        dve.wait_ge(krot_ok, n + i)
                    if first and i == 0:
                        dve.wait_ge(rot_tables, s * 2 + 2)
                    dve.tensor_tensor(rc[:, GH, :], qn[:, GH, :], rot[:, i, 1, 0, :], ALU.mult).then_inc(krot_parts, 1)
                    for own, other in ((slice(0, H2), slice(H2, HD)), (slice(H2, HD), slice(0, H2))):
                        dve.tensor_tensor(rs[:, GH, own], qn[:, GH, other], rot[:, i, 1, 1, own],
                                          ALU.mult).then_inc(krot_parts, 1)
                    dve.wait_ge(krot_parts, n * 3 + 3 * (i + 1))
                    if not first or i >= 2:
                        dve.wait_ge(t_ok, n + (i - 1))
                    dve.tensor_tensor(k_rot[i % 2][:], rc[:, GH:GH + 1, :].to_broadcast([P, 2, HD]),
                                      rs[:, GH:GH + 1, :].to_broadcast([P, 2, HD]), ALU.add).then_inc(krot_ok, 1)
                if head and first and i == 0:
                    normalize_x(s, 2)
                    modulate_x(s, 1)
                    rest_x(s, 1)
                if tail1:
                    j = (i - 1) % NBLK
                    dve.wait_ge(exp_ok, n * (GH + 1) + (GH + 1) * i)
                    dve.tensor_tensor(den2[:], den[j % 2][:], sink_e[j % 2][:], ALU.add).then_inc(rden_ok, 1)
                    dve.wait_ge(rden_ok, n * 3 + (3 * i - 2))
                    dve.tensor_scalar(den3[:], den2[:], 2.0, None, ALU.mult).then_inc(rden_ok, 1)
                    dve.wait_ge(rden_ok, n * 3 + (3 * i - 1))
                    if not first or i >= 3:
                        dve.wait_ge(gr_ok, n + (i - 2))
                    dve.reciprocal(r_den[j % 2][:], den3[:]).then_inc(rden_ok, 1)
                if head:
                    dve.wait_ge(vg_read, n * 2 + 2 * (i + 1))
                    if not first or i >= 2:
                        dve.wait_ge(gr_ok, n + (i - 1))
                    dve.scalar_tensor_tensor(g_s[i % 2][:].rearrange("p h d -> p (h d)"),
                                             g_s[i % 2][:].rearrange("p h d -> p (h d)"), 1.0,
                                             bank[1][:, HD:HD + QW], ALU.add, ALU.mult).then_inc(gs_ok, 1)
                if head and first and i + 2 < NBLK:
                    modulate_x(s, i + 2)
                if tail2:
                    j = (i - 2) % NBLK
                    dve.wait_ge(pv_ok, n + (i - 1))
                    dve.wait_ge(gr_ok, n + (i - 1))
                    if not first or i >= 4:
                        dve.wait_ge(att_out[j % 2], n * 8 + 16 * ((i - 2) // 2))
                    dve.tensor_tensor(o_mix[j % 2][:], bank[7][:, :].rearrange("p (h d) -> p h d", d=P)[:, :, 0:HD],
                                      g_r[j % 2][:], ALU.mult).then_inc(omix_ok, 1)
                if tail1:
                    j = (i - 1) % NBLK
                    dve.wait_ge(pt_ok, n + i)
                    if not first or i >= 3:
                        dve.wait_ge(pv_ok, n + (i - 2))
                    dve.tensor_copy(pT[j % 2][:, 2:4, :, :].rearrange("p h a q -> p (h a q)"),
                                    bank[6][:, :]).then_inc(ptv_ok, 1)
                if head:
                    dve.wait_ge(thi_ok, n * 2 + 2 * (i + 1))
                    dve.tensor_tensor(qT_lo[i % 2][:].rearrange("p a t -> p (a t)"), bank[4][:, 0:2 * P],
                                      qT_hi[i % 2][:].rearrange("p a t -> p (a t)").bitcast(F32),
                                      ALU.subtract).then_inc(tcopy_ok, 1)
                    dve.tensor_tensor(kT_lo[:, i + 1, :], bank[4][:, 2 * P:3 * P], kT_hi[:, i + 1, :].bitcast(F32),
                                      ALU.subtract).then_inc(tcopy_ok, 1)
                if head and first and i + 2 < NBLK:
                    rest_x(s, i + 2)
                if head and i == NBLK - 1:
                    split_lo(1, w + 1)
                    waits_alone(dve, (tcopy_ok, n * 2 + 2 * (i + 1)))
                    kept = k_carry[:, bass.ds(g, 1), :, :]
                    dve.tensor_copy(kept[:, :, 0, :], kT_hi[:, NBLK:NBLK + 1, :].bitcast(F32))
                    dve.tensor_copy(kept[:, :, 1, :], kT_lo[:, NBLK:NBLK + 1, :].bitcast(F32))
                    dve.tensor_copy(v_carry[:, bass.ds(g, 1), :], vv[:, NBLK, 0:1, :]).then_inc(carry_ok, 1)

            def rec_iter(s, h, j, head, tail, first, ht):
                n = s * (RHEADS * QUADS) + h * QUADS
                w = s * UNITS + h + GROUPS
                jt = (j - 1) % QUADS
                if head and j == 0:
                    if not first:
                        split_lo(0, w, KT * 2 * RK)
                        waits_alone(dve, (logf_ok, n))
                    dve.tensor_copy(par[:], head_par[:, bass.ds(h, 1), :].rearrange("p o c -> p (o c)")
                                    ).then_inc(par_ok, 1)
                if tail:
                    dve.wait_ge(nat_read, n * 4 + 4 * j)
                    if not first or j >= 2:
                        dve.wait_ge(rgw_ok, n + (j - 1))
                    for half in range(2):
                        nat = bank[2 + half][:, :].rearrange("p (b n) -> p b n", b=2)
                        dve.scalar_tensor_tensor(rg_s[:, 2 * half:2 * half + 2, :], rg_s[:, 2 * half:2 * half + 2, :],
                                                 1.0, nat[:, :, RK:2 * RK], ALU.add, ALU.mult).then_inc(rgs_ok, 1)
                if head:
                    if j == 0:
                        dve.wait_ge(par_ok, s * RHEADS + h + 1)
                    dve.wait_ge(fth_ok, n + (j + 1))
                    if not first or j >= 1:
                        dve.wait_ge(bcum_ok, n + j)
                        dve.wait_ge(kout_ok, n + j)
                    dve.tensor_scalar(f_r[:], f_th[:], 1.0, par[:, 1:2], ALU.add, ALU.mult).then_inc(fr_ok, 1)
                    dve.tensor_scalar(k_f[:], f_th[:], par[:, 2:3], par[:, 1:2], ALU.mult, ALU.add).then_inc(kf_ok, 1)
                if tail:
                    waits = [(ak_ok, n + j)]
                    if not first or j >= 2:
                        waits.append((o_ok, n + (j - 1)))
                    waits_alone(dve, *waits)
                    for b in range(QB):
                        dve.copy_predicated(a_T[:, b, :], causal[:], bank[4][:, b * P:(b + 1) * P]).then_inc(at_ok, 1)
                if head and j == 0 and not first:
                    split_lo(1, w, KT * 2 * RK)
                if head:
                    dve.wait_ge(logf_ok, n + (j + 1))
                    if not first or j >= 1:
                        dve.wait_ge(enb_ok, n + j)
                        dve.wait_ge(rest_ok, n + j)
                    dve.tensor_tensor_scan(b_cum[:], chunk_keep[:], f_r[:], 0.0, ALU.mult, ALU.add).then_inc(bcum_ok, 1)
                if tail:
                    waits_alone(dve, (u_ok, n + j))
                    if jt == 0:
                        dve.tensor_copy(s_in[0][:, 0, :], state[:, bass.ds(ht, 1), :].rearrange("p o v -> p (o v)")
                                        ).then_inc(state_in, 1)
                        dve.wait_ge(state_in, s * RHEADS + ht + 1)
                    for c in range(NCH):
                        if c < NCH - 1:
                            dst = s_in[jt][:, c + 1, :]
                        elif jt < QUADS - 1:
                            dst = s_in[jt + 1][:, 0, :]
                        else:
                            dst = state[:, bass.ds(ht, 1), :].rearrange("p o v -> p (o v)")
                        if c >= 1 or jt >= 1:
                            dve.wait_ge(st_ok, n * NCH + (NCH * (j - 1) + c))
                        dve.scalar_tensor_tensor(dst, s_in[jt][:, c, :], e_b[jt][:, c * CH + CH - 1:c * CH + CH],
                                                 bank[6 - c % 2][:, (c // 2) * P:(c // 2 + 1) * P],
                                                 ALU.mult, ALU.add).then_inc(st_ok, 1)
                if head:
                    dve.wait_ge(eb_ok, n + (j + 1))
                    dve.wait_ge(rq_ok, n + (j + 1))
                    dve.tensor_tensor(q_dec[j % 2][:], bank[1][:, :], e_b[j % 2][:], ALU.mult).then_inc(qdec_ok, 1)
                if tail:
                    dve.wait_ge(orinv_ok, n * 2 + 2 * j)
                    dve.wait_ge(rgw_ok, n + j)
                    if not first or j >= 3:
                        dve.wait_ge(rec_out[jt], n * 8 + 16 * ((j - 1) // 2) + 16)
                    for b in range(QB):
                        dve.scalar_tensor_tensor(r_mix[jt][:, b, :], bank[7][:, b * P:(b + 1) * P], o_rinv[:, b:b + 1],
                                                 rg_w[:, b, :], ALU.mult, ALU.mult).then_inc(rmix_ok, 1)

            with dve.Fori(0, SEGS) as s:
                normalize_x(s, 0)
                normalize_x(s, 1)
                meet(dve, seg_phase(s, 0))
                modulate_x(s, 0)
                rest_x(s, 0)
                split_lo(0, s * UNITS)
                split_lo(1, s * UNITS)
                dve.wait_ge(late_in, 16 * 2)
                dve.tensor_copy(mask_first[:], masks[:, bass.ds(s, 1), :].rearrange("p o t -> p (o t)"))
                for i in range(NBLK):
                    att_iter(s, 0, i, True, i >= 1, i >= 2, True, 0)
                with dve.Fori(1, GROUPS) as g:
                    for i in range(NBLK):
                        att_iter(s, g, i, True, True, True, False, g - 1 if i == 0 else g)
                att_iter(s, GROUPS - 1, NBLK, False, True, True, False, GROUPS - 1)
                att_iter(s, GROUPS - 1, NBLK + 1, False, False, True, False, GROUPS - 1)
                phase_over(dve, seg_phase(s, 1))
                dve.memset(a_T[:], 0.0)
                dve.memset(chunk_keep[:], 1.0).then_inc(keep_ok, 1)
                dve.wait_ge(keep_ok, s + 1)
                dve.memset(chunk_keep[:].rearrange("p (c t) -> p c t", t=CH)[:, :, 0:1], 0.0)
                for j in range(QUADS):
                    rec_iter(s, 0, j, True, j >= 1, True, 0)
                with dve.Fori(1, RHEADS) as h:
                    for j in range(QUADS):
                        rec_iter(s, h, j, True, True, False, h - 1 if j == 0 else h)
                rec_iter(s, RHEADS - 1, QUADS, False, True, False, RHEADS - 1)
                arrive(dve)

            def m_rest(n, b):
                for q in range(4):
                    dve.wait_ge(mhi_ok, n * 4 + (4 * b + q + 1))
                    dve.tensor_tensor(m_lo[b][:, 4 * q:4 * q + 4, :].rearrange("p f t -> p (f t)"), bank[q % 2][:, :],
                                      m_hi[b][:, 4 * q:4 * q + 4, :].rearrange("p f t -> p (f t)").bitcast(F32),
                                      ALU.subtract).then_inc(mlo_ok, 1)

            def finish_rows(n, b, first):
                dve.wait_ge(y_ok, n + (b + 1))
                dve.wait_ge(xo_in[b], n * 8 + 16)
                y_tmp = [m_y[:, 0:HALF], m_y[:, HALF:D]]
                if not (first and b == 0):
                    dve.wait_ge(yout_ok, n * 2 + 2 * b)
                for c in range(2):
                    dve.tensor_tensor(y_tmp[c], bank[4 + 2 * b + c][:, :], gate_bc[:, c * HALF:(c + 1) * HALF],
                                      ALU.mult).then_inc(ygate_ok, 1)
                for c in range(2):
                    dve.wait_ge(ygate_ok, n * 2 + (2 * b + c + 1))
                    dve.tensor_tensor(xo[b][:, c * HALF:(c + 1) * HALF], xo[b][:, c * HALF:(c + 1) * HALF], y_tmp[c],
                                      ALU.add).then_inc(yout_ok, 1)

            for f in range(FT):
                if f == 2:
                    meet(dve, LAST_PHASE)
                    m_rest(0, 0)
                dve.wait_ge(wohi_ok, f + 1)
                dve.tensor_tensor(wo_lo[:, f, :], wo_raw[:, f, :], wo_hi[:, f, :].bitcast(F32),
                                  ALU.subtract).then_inc(wolo_ok, 1)

            m_rest(0, 1)
            finish_rows(0, 0, True)
            m_rest(2, 0)
            finish_rows(0, 1, True)
            with dve.Fori(1, OUT_BLKS // 2 - 1) as bp:
                m_rest(bp * 2, 1)
                finish_rows(bp * 2, 0, False)
                m_rest(bp * 2 + 2, 0)
                finish_rows(bp * 2, 1, False)
            m_rest(OUT_BLKS - 2, 1)
            finish_rows(OUT_BLKS - 2, 0, False)
            for c in range(2):
                m, at = OUT_BLKS - 1, slice(c * HALF, (c + 1) * HALF)
                dve.wait_ge(y_half, c + 1)
                if c == 0:
                    dve.wait_ge(xo_in[m % 2], 16 * (m // 2 + 1))
                    dve.wait_ge(yout_ok, 2 * m)
                dve.tensor_tensor(m_y[:, at], bank[4 + 2 * (m % 2) + c][:, :], gate_bc[:, at], ALU.mult
                                  ).then_inc(ygate_ok, 1)
                dve.wait_ge(ygate_ok, 2 * m + c + 1)
                dve.tensor_tensor(xo[m % 2][:, at], xo[m % 2][:, at], m_y[:, at], ALU.add).then_inc(yout_ok, 1)

        @block.gpsimd
        def _(pool):
            H2 = HD // 2
            pool.memset(minus_half[:], -0.5)
            arrive(pool)

            def inverse_root(dst, var, ss, count, done, base):
                pool.tensor_scalar(var, ss, 1.0 / count, EPS, ALU.mult, ALU.add).then_inc(done, 1)
                pool.wait_ge(done, base + 1)
                pool.tensor_tensor(dst, var, minus_half[:, 0:ss.shape[1]], ALU.pow).then_inc(done, 1)

            def root_x(s, m):
                b = m % 2
                waits_alone(pool, (x_sqd, s * NBLK + (m + 1)))
                inverse_root(x_rinv[:, b:b + 1], x_var[:, b:b + 1], x_ss[:, b:b + 1], D, x_rs, (s * NBLK + m) * 2)

            def att_iter(s, g, i, head, tail1, first):
                n = s * (GROUPS * NBLK) + g * NBLK
                if head:
                    waits = [(ss_ok, n + (i + 1))]
                    if not first or i >= 1:
                        waits.append((qn_ok, n + i))
                    waits_alone(pool, *waits)
                    inverse_root(q_rinv[:], q_var[:], q_ss[:], HD, rinv_ok, n * 2 + 2 * i)
                    if first and i == 0:
                        root_x(s, 2)
                    rotate(s, g, i, first)
                if tail1:
                    j = (i - 1) % NBLK
                    pool.wait_ge(rden_ok, n * 3 + 3 * i)
                    pool.wait_ge(gs_ok, n + i)
                    if not first or i >= 3:
                        pool.wait_ge(omix_ok, n + (i - 2))
                    pool.tensor_tensor(g_r[j % 2][:], g_s[j % 2][:],
                                       r_den[j % 2][:].unsqueeze(2).to_broadcast([P, GH, HD]),
                                       ALU.mult).then_inc(gr_ok, 1)
                if head and first and i + 3 < NBLK:
                    root_x(s, i + 3)

            def rotate(s, g, i, first):
                n = s * (GROUPS * NBLK) + g * NBLK
                if first and i == 0:
                    waits_alone(pool, (rot_tables, s * 2 + 2))
                pool.wait_ge(qn_ok, n + (i + 1))
                if not first or i >= 1:
                    pool.wait_ge(rot_ok, n + i)
                cos_q = rot[:, i, 0, 0, :].unsqueeze(1).to_broadcast([P, GH, HD])
                pool.tensor_tensor(rc[:, 0:GH, :], qn[:, 0:GH, :], cos_q, ALU.mult).then_inc(rot_parts, 1)
                for own, other in ((slice(0, H2), slice(H2, HD)), (slice(H2, HD), slice(0, H2))):
                    sin_q = rot[:, i, 0, 1, own].unsqueeze(1).to_broadcast([P, GH, H2])
                    pool.tensor_tensor(rs[:, 0:GH, own], qn[:, 0:GH, other], sin_q, ALU.mult).then_inc(rot_parts, 1)
                pool.wait_ge(rot_parts, n * 3 + 3 * (i + 1))
                if not first or i >= 2:
                    pool.wait_ge(t_ok, n + (i - 1))
                pool.tensor_tensor(q_rot[i % 2][:], rc[:, 0:GH, :], rs[:, 0:GH, :], ALU.add).then_inc(rot_ok, 1)

            def rec_iter(s, h, j, head, tail, first):
                n = s * (RHEADS * QUADS) + h * QUADS
                if tail:
                    pool.wait_ge(rgs_ok, n * 2 + 2 * j)
                    if not first or j >= 2:
                        pool.wait_ge(rmix_ok, n * QB + QB * (j - 1))
                    pool.tensor_tensor(rg_w[:], rg_s[:], rec_wt[:].unsqueeze(1).to_broadcast([P, QB, RK]),
                                       ALU.mult).then_inc(rgw_ok, 1)
                if head:
                    pool.wait_ge(bcum_ok, n + (j + 1))
                    if not first or j >= 1:
                        pool.wait_ge(kout_ok, n + j)
                    b3 = b_cum[:].rearrange("p (c t) -> p c t", t=CH)
                    pool.tensor_tensor(b_rest[:].rearrange("p (c t) -> p c t", t=CH),
                                       b3[:, :, CH - 1:CH].to_broadcast([P, NCH, CH]), b3, ALU.subtract).then_inc(rest_ok, 1)
                    if not first or j >= 2:
                        pool.wait_ge(ak_ok, n + (j - 1))
                    pool.wait_ge(enb_ok, n + (j + 1))
                    pool.wait_ge(kf_ok, n + (j + 1))
                    pool.tensor_tensor(k_inv[j % 2][:], k_f[:], e_nb[:], ALU.mult).then_inc(kinv_ok, 1)
                    pool.wait_ge(erest_ok, n + (j + 1))
                    pool.tensor_tensor(k_out[j % 2][:], k_f[:], b_rest[:], ALU.mult).then_inc(kout_ok, 1)
                if tail:
                    waits = [(oss_ok, n * QB + QB * j)]
                    if not first or j >= 2:
                        waits.append((rmix_ok, n * QB + QB * (j - 1)))
                    waits_alone(pool, *waits)
                    inverse_root(o_rinv[:], o_var[:], o_ss[:], RK, orinv_ok, n * 2 + 2 * (j - 1))

            with pool.Fori(0, SEGS) as s:
                root_x(s, 0)
                root_x(s, 1)
                meet(pool, seg_phase(s, 0))
                tv = s * 10
                pool.tensor_tensor(ang, pos_f[:, bass.ds(s * NBLK, NBLK)].unsqueeze(2).to_broadcast([P, NBLK, H2]),
                                   freq[:].unsqueeze(1).to_broadcast([P, NBLK, H2]), ALU.mult).then_inc(trig_step, 1)
                waits_alone(pool, (trig_step, tv + 1))
                pool.tensor_scalar(turns, ang, float(1.0 / TWO_PI), ROUND, ALU.mult, ALU.add).then_inc(trig_step, 1)
                waits_alone(pool, (trig_step, tv + 2))
                pool.tensor_scalar(turns, turns, ROUND, None, ALU.subtract).then_inc(trig_step, 1)
                for m, part in enumerate((PI_A, PI_B, PI_C)):
                    waits_alone(pool, (trig_step, tv + (2 * m + 3)))
                    pool.tensor_scalar(cosv, turns, -part, None, ALU.mult).then_inc(trig_step, 1)
                    waits_alone(pool, (trig_step, tv + (2 * m + 4)))
                    pool.tensor_tensor(ang, ang, cosv, ALU.add).then_inc(trig_step, 1)
                waits_alone(pool, (trig_step, tv + 9))
                pool.tensor_scalar(ang, ang, PI_MAX, -PI_MAX, ALU.min, ALU.max).then_inc(trig_step, 1)
                waits_alone(pool, (trig_step, tv + 10))
                for i in range(NBLK):
                    att_iter(s, 0, i, True, i >= 1, True)
                with pool.Fori(1, GROUPS) as g:
                    for i in range(NBLK):
                        att_iter(s, g, i, True, True, False)
                att_iter(s, GROUPS - 1, NBLK, False, True, False)
                phase_over(pool, seg_phase(s, 1))
                for j in range(QUADS):
                    rec_iter(s, 0, j, True, j >= 1, True)
                with pool.Fori(1, RHEADS) as h:
                    for j in range(QUADS):
                        rec_iter(s, h, j, True, True, False)
                rec_iter(s, RHEADS - 1, QUADS, False, True, False)
                arrive(pool)


def constants():
    q, k = np.arange(P)[:, None], np.arange(P)[None, :]
    prev = np.where(k > q, 0.0, NEG)
    own = np.where(k <= q, 0.0, NEG)
    first = np.concatenate([np.full((P, P), NEG), own], 1)
    later = np.concatenate([prev, own], 1)
    masks = np.stack([first] + [later] * (SEGS - 1), 1).astype(np.float32)
    s, t = np.arange(P)[:, None], np.arange(P)[None, :]
    causal = ((s <= t) & (s // CH == t // CH)).astype(np.int32)
    inv = (np.float32(10000.0) ** (-np.arange(0, HD, 2, dtype=np.float32) / np.float32(HD))).astype(np.float32)
    sign = np.tile(inv, (P, 1))
    return np.eye(P, dtype=np.float32), masks, causal, sign


def kernel(x, c, positions, norm_w, w_ada, b_ada, w_in, q_norm_w, k_norm_w, sinks, rec_norm_w, lower_bounds, w_out):
    import concourse.bacc as bacc
    from concourse.bass_utils import run_bass_kernel_spmd

    def cols(a, n):
        return np.ascontiguousarray(np.asarray(a).reshape(n, P).T)

    def rows(a):
        return np.ascontiguousarray(np.broadcast_to(np.asarray(a).reshape(1, -1), (P, np.asarray(a).size)))

    ident, masks, causal, freq = constants()
    b = np.asarray(b_ada)[0]
    arrays = {
        "x": np.asarray(x)[0], "cT": cols(c, KT), "pos": cols(positions, SEQ // P), "norm_w": cols(norm_w, KT),
        "w_ada": np.asarray(w_ada)[0], "b_cols": cols(b[:2 * D], 2 * KT), "b_gate": rows(b[2 * D:]),
        "w_in": np.asarray(w_in)[0],
        "qk_w": np.ascontiguousarray(np.stack([rows(q_norm_w), rows(k_norm_w)], 1)),
        "sinks": rows(sinks), "rec_w": rows(rec_norm_w),
        "lbT": np.ascontiguousarray(np.asarray(lower_bounds).reshape(2, RHEADS, P).transpose(2, 0, 1)),
        "w_out": np.asarray(w_out)[0],
        "ident_d": ident, "masks_d": masks, "causal_d": causal, "freq_d": freq,
    }
    arrays = {k: np.ascontiguousarray(a) for k, a in arrays.items()}
    nc = bacc.Bacc("TRN2", target_bir_lowering=False, num_devices=1)
    args = {k: nc.dram_tensor(f"in_{k}", a.shape, mybir.dt.from_np(a.dtype), kind="ExternalInput").ap()
            for k, a in arrays.items()}
    out = nc.dram_tensor("out_rows", (SEQ, D), F32, kind="ExternalOutput").ap()
    mixed = nc.dram_tensor("mixed_rows", (SEQ, MIX), F32, kind="Internal").ap()
    hybrid_layer(nc, out=out, mixed=mixed, **args)
    r = run_bass_kernel_spmd(nc, [{f"in_{k}": a for k, a in arrays.items()}], core_ids=[0])
    return r.results[0]["out_rows"].reshape(1, SEQ, D)
```
